# Optimizing a Trainium2 kernel written in Bass

```python
import jax
import jax.numpy as jnp
from jax import lax
import numpy as np
import math

D_MODEL = 1024
BATCH = 1
SEQ = 512
DEPTH = 1

GDN_HEADS = 8
GDN_DK = 128
GDN_DV = 128
GDN_CONV = 4
CHUNK = 64
SC_WIDTH = D_MODEL
SC_CONV = 3
D_FF_RAW = (8 * D_MODEL + 2) // 3
D_FF = (D_FF_RAW + 255) // 256 * 256
EPS = 1e-6
N_MOD = 6

QK_W = GDN_HEADS * GDN_DK
V_W = GDN_HEADS * GDN_DV
QKV_W = 2 * QK_W + V_W
Q_OFF = 0
K_OFF = Q_OFF + QK_W
V_OFF = K_OFF + QK_W
Z_OFF = V_OFF + V_W
A_OFF = Z_OFF + V_W
BETA_OFF = A_OFF + GDN_HEADS
SCB_OFF = BETA_OFF + GDN_HEADS
SCC_OFF = SCB_OFF + SC_WIDTH
SCX_OFF = SCC_OFF + SC_WIDTH
GA_OFF = SCX_OFF + SC_WIDTH
GB_OFF = GA_OFF + D_MODEL
IN_COLS = GB_OFF + D_MODEL


def rms_norm(x, w):
    xf = x.astype(jnp.float32)
    y = xf * lax.rsqrt(jnp.mean(xf * xf, axis=-1, keepdims=True) + EPS)
    return (y * w.astype(jnp.float32)).astype(x.dtype)

def l2_normalize(x):
    xf = x.astype(jnp.float32)
    return (xf * lax.rsqrt(jnp.sum(xf * xf, axis=-1, keepdims=True) + EPS)).astype(x.dtype)

def modulate(h, shift, scale):
    return h * (1.0 + scale[:, None, :]) + shift[:, None, :]

def causal_depthwise_conv(x, w):
    width, ch = w.shape
    return lax.conv_general_dilated(
        x, w[:, None, :].astype(x.dtype), window_strides=(1,), padding=[(width - 1, 0)],
        dimension_numbers=("NWC", "WIO", "NWC"), feature_group_count=ch)

def gated_delta_rule_chunked(q, k, v, g, beta):
    f32 = jnp.float32
    out_dtype = v.dtype
    b, s, h, dk = q.shape
    dv = v.shape[-1]
    n = s // CHUNK

    def to_chunks(t):
        t = t.astype(f32).reshape((b, n, CHUNK, h) + t.shape[3:])
        return jnp.moveaxis(t, 3, 1)

    q, k, v, g, beta = map(to_chunks, (q, k, v, g, beta))
    q = q * (dk ** -0.5)
    g = jnp.cumsum(g, axis=-1)
    idx = jnp.arange(CHUNK)
    causal = idx[:, None] >= idx[None, :]
    strict = idx[:, None] > idx[None, :]
    decay = jnp.exp(jnp.where(causal, g[..., :, None] - g[..., None, :], -jnp.inf))

    k_beta = k * beta[..., None]
    v_beta = v * beta[..., None]
    lower = jnp.where(strict, jnp.einsum("bhncd,bhnsd->bhncs", k_beta, k) * decay, 0.0)
    eye = jnp.eye(CHUNK, dtype=f32)
    t_inv = lax.linalg.triangular_solve(eye + lower, jnp.broadcast_to(eye, lower.shape),
                                        left_side=True, lower=True, unit_diagonal=True)
    eg = jnp.exp(g)
    u = jnp.einsum("bhncs,bhnse->bhnce", t_inv, v_beta)
    w = jnp.einsum("bhncs,bhnsd->bhncd", t_inv, k_beta * eg[..., None])
    qk = jnp.where(causal, jnp.einsum("bhncd,bhnsd->bhncs", q, k) * decay, 0.0)
    q_g = q * eg[..., None]
    g_last = g[..., -1]
    k_dec = k * jnp.exp(g_last[..., None] - g)[..., None]

    def step(state, xs):
        q_c, qk_c, u_c, w_c, k_c, gl = xs
        v_new = u_c - jnp.einsum("bhcd,bhde->bhce", w_c, state)
        o = jnp.einsum("bhcd,bhde->bhce", q_c, state) + jnp.einsum("bhcs,bhse->bhce", qk_c, v_new)
        state = state * jnp.exp(gl)[..., None, None] + jnp.einsum("bhcd,bhce->bhde", k_c, v_new)
        return state, o

    xs = tuple(jnp.moveaxis(t, 2, 0) for t in (q_g, qk, u, w, k_dec, g_last))
    state0 = jnp.zeros((b, h, dk, dv), f32)
    _, o = lax.scan(step, state0, xs)
    o = jnp.transpose(o, (1, 0, 3, 2, 4)).reshape(b, s, h, dv)
    return o.astype(out_dtype)

def hybrid_mixer(h, w_in, gdn_conv_w, a_log, dt_bias, gdn_norm_w, w_gdn_proj, sc_conv_w, w_sc_out, w_o):
    b, s, _ = h.shape
    p = h @ w_in
    qkv = jax.nn.silu(causal_depthwise_conv(p[..., Q_OFF:Z_OFF], gdn_conv_w))
    q = l2_normalize(qkv[..., Q_OFF:K_OFF].reshape(b, s, GDN_HEADS, GDN_DK))
    k = l2_normalize(qkv[..., K_OFF:V_OFF].reshape(b, s, GDN_HEADS, GDN_DK))
    v = qkv[..., V_OFF:Z_OFF].reshape(b, s, GDN_HEADS, GDN_DV)
    z = p[..., Z_OFF:A_OFF].reshape(b, s, GDN_HEADS, GDN_DV)
    g = -jnp.exp(a_log) * jax.nn.softplus(p[..., A_OFF:BETA_OFF] + dt_bias)
    beta = jax.nn.sigmoid(p[..., BETA_OFF:SCB_OFF])
    o = gated_delta_rule_chunked(q, k, v, g, beta)
    o = rms_norm(o, gdn_norm_w) * jax.nn.silu(z)
    y_a = o.reshape(b, s, V_W) @ w_gdn_proj
    gb = p[..., SCB_OFF:SCC_OFF]
    gc = p[..., SCC_OFF:SCX_OFF]
    xin = p[..., SCX_OFF:GA_OFF]
    y_b = (gb * causal_depthwise_conv(gc * xin, sc_conv_w)) @ w_sc_out
    gate_a = jax.nn.sigmoid(p[..., GA_OFF:GB_OFF])
    gate_b = jax.nn.sigmoid(p[..., GB_OFF:IN_COLS])
    return (gate_a * y_a + gate_b * y_b) @ w_o

def swiglu(h, w_ffn_in, w_ffn_out):
    gu = h @ w_ffn_in
    return (jax.nn.silu(gu[..., :D_FF]) * gu[..., D_FF:]) @ w_ffn_out

def first_inputs(seed: int = 0) -> dict:
    key = jax.random.key(seed)
    ks = jax.random.split(key, 22)
    nrm = jax.random.normal
    D = D_MODEL
    x = nrm(ks[0], (BATCH, SEQ, D), jnp.float32)
    c = nrm(ks[1], (BATCH, D), jnp.float32)
    w_ada = nrm(ks[2], (DEPTH, D, N_MOD * D), jnp.float32) * (0.5 * D ** -0.5)
    b_ada = 0.02 * nrm(ks[3], (DEPTH, N_MOD * D), jnp.float32)
    norm1_w = 1.0 + 0.02 * nrm(ks[4], (DEPTH, D), jnp.float32)
    w_in = nrm(ks[5], (DEPTH, D, IN_COLS), jnp.float32) * D ** -0.5
    gdn_conv_w = nrm(ks[6], (DEPTH, GDN_CONV, QKV_W), jnp.float32) * GDN_CONV ** -0.5
    gdn_a_log = jnp.log(jax.random.uniform(ks[7], (DEPTH, GDN_HEADS), jnp.float32, 1.0, 16.0))
    dt = jnp.exp(jax.random.uniform(ks[8], (DEPTH, GDN_HEADS), jnp.float32,
                                    float(np.log(1e-3)), float(np.log(1e-1))))
    gdn_dt_bias = jnp.log(jnp.expm1(dt))
    gdn_norm_w = 1.0 + 0.02 * nrm(ks[9], (DEPTH, GDN_DV), jnp.float32)
    w_gdn_proj = nrm(ks[10], (DEPTH, V_W, D), jnp.float32) * V_W ** -0.5
    sc_conv_w = nrm(ks[11], (DEPTH, SC_CONV, SC_WIDTH), jnp.float32) * SC_CONV ** -0.5
    w_sc_out = nrm(ks[12], (DEPTH, SC_WIDTH, D), jnp.float32) * SC_WIDTH ** -0.5
    w_o = nrm(ks[13], (DEPTH, D, D), jnp.float32) * D ** -0.5
    norm2_w = 1.0 + 0.02 * nrm(ks[14], (DEPTH, D), jnp.float32)
    w_ffn_in = nrm(ks[15], (DEPTH, D, 2 * D_FF), jnp.float32) * D ** -0.5
    w_ffn_out = nrm(ks[16], (DEPTH, D_FF, D), jnp.float32) * D_FF ** -0.5
    w_ada_f = nrm(ks[17], (D, 2 * D), jnp.float32) * (0.5 * D ** -0.5)
    b_ada_f = 0.02 * nrm(ks[18], (2 * D,), jnp.float32)
    normf_w = 1.0 + 0.02 * nrm(ks[19], (D,), jnp.float32)
    return {"x": x, "c": c, "w_ada": w_ada, "b_ada": b_ada, "norm1_w": norm1_w, "w_in": w_in,
            "gdn_conv_w": gdn_conv_w, "gdn_a_log": gdn_a_log, "gdn_dt_bias": gdn_dt_bias,
            "gdn_norm_w": gdn_norm_w, "w_gdn_proj": w_gdn_proj, "sc_conv_w": sc_conv_w,
            "w_sc_out": w_sc_out, "w_o": w_o, "norm2_w": norm2_w, "w_ffn_in": w_ffn_in,
            "w_ffn_out": w_ffn_out, "w_ada_f": w_ada_f, "b_ada_f": b_ada_f, "normf_w": normf_w}

def first_block(x, c, w_ada, b_ada, norm1_w, w_in, gdn_conv_w, gdn_a_log, gdn_dt_bias, gdn_norm_w,
              w_gdn_proj, sc_conv_w, w_sc_out, w_o, norm2_w, w_ffn_in, w_ffn_out, w_ada_f, b_ada_f,
              normf_w):
    c_act = jax.nn.silu(c)
    for l in range(DEPTH):
        mod = c_act @ w_ada[l] + b_ada[l]
        sh1, sc1, g1, sh2, sc2, g2 = jnp.split(mod, N_MOD, axis=-1)
        h = modulate(rms_norm(x, norm1_w[l]), sh1, sc1)
        mix = hybrid_mixer(h, w_in[l], gdn_conv_w[l], gdn_a_log[l], gdn_dt_bias[l], gdn_norm_w[l],
                           w_gdn_proj[l], sc_conv_w[l], w_sc_out[l], w_o[l])
        x = x + g1[:, None, :] * mix
        h = modulate(rms_norm(x, norm2_w[l]), sh2, sc2)
        x = x + g2[:, None, :] * swiglu(h, w_ffn_in[l], w_ffn_out[l])
    shf, scf = jnp.split(c_act @ w_ada_f + b_ada_f, 2, axis=-1)
    return modulate(rms_norm(x, normf_w), shf, scf)


DEPTH_2 = 2

N_MIXERS = 4
NORM_EPS = 1e-6
ROPE_THETA = 10000.0
HEAD_DIM = 64
NEG_INF = -1e30

POOL_WINDOWS = (2, 4, 8, 16)
POOL_GROUP = D_MODEL // len(POOL_WINDOWS)

DIFF_HEADS = D_MODEL // (2 * HEAD_DIM)
DIFF_SUBLN_EPS = 1e-5
Q_BLOCK = 128

LRU_WIDTH = D_MODEL
LRU_BLOCKS = D_MODEL // HEAD_DIM
LRU_BLOCK_DIM = LRU_WIDTH // LRU_BLOCKS
LRU_CONV = 4
LRU_C = 8.0

DIL_GROUPS = ((128, 1), (512, 4), (2048, 16))
DIL_HEADS = D_MODEL // HEAD_DIM
DIL_WIDTH = DIL_HEADS * HEAD_DIM

D_FF_2 = 2816
FFN_CONV = 3


def _n_layers_of(mixer):
    return len(range(mixer, DEPTH_2, N_MIXERS))

def _rms_norm(x, gain, eps=NORM_EPS):
    xf = x.astype(jnp.float32)
    y = xf * lax.rsqrt(jnp.mean(xf * xf, axis=-1, keepdims=True) + eps)
    return (y * gain.astype(jnp.float32)).astype(x.dtype)

def _rope_tables(positions, head_dim):
    inv = ROPE_THETA ** (-jnp.arange(0, head_dim, 2, dtype=jnp.float32) / head_dim)
    ang = positions.astype(jnp.float32)[:, None] * inv[None, :]
    return jnp.cos(ang), jnp.sin(ang)

def _rope(x, cos, sin):
    shape = (cos.shape[0],) + (1,) * (x.ndim - 3) + (cos.shape[1],)
    c, s = cos.reshape(shape), sin.reshape(shape)
    xf = x.astype(jnp.float32)
    x1, x2 = jnp.split(xf, 2, axis=-1)
    return jnp.concatenate([x1 * c - x2 * s, x2 * c + x1 * s], axis=-1).astype(x.dtype)

def _pool_mixer(x, w, scale):
    b, s, d = x.shape
    xf = x.astype(jnp.float32)
    cs = jnp.concatenate([jnp.zeros((b, 1, d), jnp.float32), lax.cumsum(xf, axis=1)], axis=1)
    t = jnp.arange(s)
    parts = []
    for g, win in enumerate(POOL_WINDOWS):
        lo = jnp.clip(t - win // 2, 0, s)
        hi = jnp.clip(t + win - win // 2, 0, s)
        sl = slice(g * POOL_GROUP, (g + 1) * POOL_GROUP)
        csg = cs[:, :, sl]
        mean = (csg[:, hi] - csg[:, lo]) / (hi - lo).astype(jnp.float32)[:, None]
        parts.append(mean - xf[:, :, sl])
    pooled = jnp.stack(parts, axis=2).astype(x.dtype)
    y = jnp.einsum('bsgc,gce->bsge', pooled, w).reshape(b, s, d)
    return y * scale

def _diff_attention(x, w_qkv, lq1, lk1, lq2, lk2, subln, w_o, cos, sin, layer_idx):
    b, s, _ = x.shape
    h, dh = DIFF_HEADS, HEAD_DIM
    q, k, v = jnp.split(x @ w_qkv, 3, axis=-1)
    q = _rope(q.reshape(b, s, 2 * h, dh), cos, sin).reshape(b, s, h, 2, dh) * (dh ** -0.5)
    k = _rope(k.reshape(b, s, 2 * h, dh), cos, sin).reshape(b, s, h, 2, dh)
    v = v.reshape(b, s, h, 2 * dh)
    lam_init = 0.8 - 0.6 * math.exp(-0.3 * layer_idx)
    lam = (jnp.exp(jnp.sum(lq1.astype(jnp.float32) * lk1.astype(jnp.float32)))
           - jnp.exp(jnp.sum(lq2.astype(jnp.float32) * lk2.astype(jnp.float32))) + lam_init)
    nb = s // Q_BLOCK
    q_blocks = q.reshape(b, nb, Q_BLOCK, h, 2, dh).swapaxes(0, 1)

    def one_block(qb):
        sc = jnp.einsum('bqhce,bkhce->bhcqk', qb, k).astype(jnp.float32)
        p = jax.nn.softmax(sc, axis=-1)
        a = p[:, :, 0] - lam * p[:, :, 1]
        return jnp.einsum('bhqk,bkhe->bqhe', a.astype(v.dtype), v)

    o = lax.map(one_block, q_blocks).swapaxes(0, 1).reshape(b, s, h, 2 * dh)
    o = _rms_norm(o, subln, DIFF_SUBLN_EPS) * (1.0 - lam_init)
    return o.reshape(b, s, h * 2 * dh) @ w_o

def _causal_conv(x, w, bias):
    kw = w.shape[0]
    s = x.shape[1]
    xp = jnp.pad(x, ((0, 0), (kw - 1, 0), (0, 0)))
    y = bias
    for j in range(kw):
        y = y + w[j] * xp[:, j:j + s]
    return y

def _rg_lru_direction(u, conv_w, conv_b, w_a, b_a, w_x, b_x, lam):
    b, s, c = u.shape
    xc = _causal_conv(u, conv_w, conv_b)
    xb = xc.reshape(b, s, LRU_BLOCKS, LRU_BLOCK_DIM)
    r = jax.nn.sigmoid((jnp.einsum('bsni,nij->bsnj', xb, w_a).reshape(b, s, c) + b_a).astype(jnp.float32))
    i = jax.nn.sigmoid((jnp.einsum('bsni,nij->bsnj', xb, w_x).reshape(b, s, c) + b_x).astype(jnp.float32))
    log_a = LRU_C * r * jax.nn.log_sigmoid(lam.astype(jnp.float32))
    a = jnp.exp(log_a)
    inp = jnp.sqrt(-jnp.expm1(2.0 * log_a)) * (i * xc.astype(jnp.float32))

    def combine(left, right):
        a_l, b_l = left
        a_r, b_r = right
        return a_l * a_r, a_r * b_l + b_r

    _, h = lax.associative_scan(combine, (a, inp), axis=1)
    return h

def _rglru_mixer(x, w_in, conv_w, conv_b, w_a, b_a, w_x, b_x, lam, w_out):
    gate, u = jnp.split(x @ w_in, 2, axis=-1)
    h_fwd = _rg_lru_direction(u, conv_w[0], conv_b[0], w_a[0], b_a[0], w_x[0], b_x[0], lam[0])
    h_bwd = jnp.flip(_rg_lru_direction(jnp.flip(u, axis=1), conv_w[1], conv_b[1], w_a[1], b_a[1],
                                       w_x[1], b_x[1], lam[1]), axis=1)
    y = jax.nn.gelu(gate.astype(jnp.float32), approximate=True) * (h_fwd + h_bwd)
    return y.astype(x.dtype) @ w_out

def _dilated_chain_attention(q, k, v, dilation, half):
    b, s, h, dh = q.shape
    n = s // dilation
    blk = half
    nb = -(-n // blk)
    pad = nb * blk - n

    def chains(t):
        return t.reshape(b, n, dilation, h, dh).transpose(0, 2, 3, 1, 4)

    qc = jnp.pad(chains(q), ((0, 0), (0, 0), (0, 0), (0, pad), (0, 0))).reshape(b, dilation, h, nb, blk, dh)

    def windows(t):
        tp = jnp.pad(chains(t), ((0, 0), (0, 0), (0, 0), (blk, blk + pad), (0, 0)))
        tp = tp.reshape(b, dilation, h, nb + 2, blk, dh)
        return jnp.concatenate([tp[:, :, :, :-2], tp[:, :, :, 1:-1], tp[:, :, :, 2:]], axis=4)

    kw, vw = windows(k), windows(v)
    qpos = jnp.arange(nb * blk).reshape(nb, blk)
    kpos = jnp.arange(nb)[:, None] * blk + jnp.arange(-blk, 2 * blk)[None, :]
    rel = kpos[:, None, :] - qpos[:, :, None]
    valid = (jnp.abs(rel) <= half) & (kpos[:, None, :] >= 0) & (kpos[:, None, :] < n)
    sc = jnp.einsum('bdhnqe,bdhnke->bdhnqk', qc, kw).astype(jnp.float32)
    sc = jnp.where(valid, sc, NEG_INF)
    lse = jax.nn.logsumexp(sc, axis=-1)
    p = jnp.exp(sc - lse[..., None])
    o = jnp.einsum('bdhnqk,bdhnke->bdhnqe', p.astype(v.dtype), vw)

    def unchain(t):
        t = t.reshape((b, dilation, h, nb * blk) + t.shape[5:])[:, :, :, :n]
        t = jnp.moveaxis(t, 3, 1)
        return t.reshape((b, s, h) + t.shape[4:])

    return unchain(o), unchain(lse)

def _dilated_mixer(x, w_qkv, w_o, cos, sin):
    b, s, _ = x.shape
    n_groups = len(DIL_GROUPS)
    qkv = (x @ w_qkv).reshape(b, s, n_groups, 3, DIL_HEADS, HEAD_DIM)
    q = _rope(qkv[:, :, :, 0], cos, sin) * (HEAD_DIM ** -0.5)
    k = _rope(qkv[:, :, :, 1], cos, sin)
    v = qkv[:, :, :, 2]
    outs, lses = [], []
    for g, (window, dilation) in enumerate(DIL_GROUPS):
        o, l = _dilated_chain_attention(q[:, :, g], k[:, :, g], v[:, :, g], dilation, window // (2 * dilation))
        outs.append(o.astype(jnp.float32))
        lses.append(l)
    wts = jax.nn.softmax(jnp.stack(lses, axis=0), axis=0)
    o = jnp.sum(wts[..., None] * jnp.stack(outs, axis=0), axis=0)
    return o.astype(x.dtype).reshape(b, s, DIL_WIDTH) @ w_o

def _conv_ffn(x, w_up, conv_w, conv_b, w_down):
    s = x.shape[1]
    g, u = jnp.split(x @ w_up, 2, axis=-1)
    half = FFN_CONV // 2
    gp = jnp.pad(g, ((0, 0), (half, half), (0, 0)))
    gc = conv_b
    for j in range(FFN_CONV):
        gc = gc + conv_w[j] * gp[:, j:j + s]
    act = jax.nn.gelu(gc.astype(jnp.float32), approximate=False).astype(x.dtype)
    return (act * u) @ w_down

def second_inputs(seed: int = 0) -> dict:
    key = jax.random.key(seed)
    keys = iter(jax.random.split(key, 48))
    f32 = jnp.float32
    n_a, n_b, n_c, n_d = (_n_layers_of(m) for m in range(N_MIXERS))

    def dense(shape, fan_in):
        return jax.random.normal(next(keys), shape, f32) * fan_in ** -0.5

    def gain(shape):
        return 1.0 + 0.05 * jax.random.normal(next(keys), shape, f32)

    def small(shape, scale=0.02):
        return scale * jax.random.normal(next(keys), shape, f32)

    x = jax.random.normal(next(keys), (BATCH, SEQ, D_MODEL), f32)
    a_c = jax.random.uniform(next(keys), (n_c, 2, LRU_WIDTH), f32, 0.9, 0.999)
    base = a_c ** (1.0 / LRU_C)
    lru_lambda = jnp.log(base) - jnp.log1p(-base)
    return {
        "x": x,
        "positions": jnp.arange(SEQ, dtype=jnp.int32),
        "mix_norm": gain((DEPTH_2, D_MODEL)),
        "pool_w": dense((n_a, len(POOL_WINDOWS), POOL_GROUP, POOL_GROUP), POOL_GROUP),
        "pool_scale": gain((n_a, D_MODEL)),
        "diff_w_qkv": dense((n_b, D_MODEL, 3 * D_MODEL), D_MODEL),
        "diff_lam_q1": small((n_b, HEAD_DIM), 0.1),
        "diff_lam_k1": small((n_b, HEAD_DIM), 0.1),
        "diff_lam_q2": small((n_b, HEAD_DIM), 0.1),
        "diff_lam_k2": small((n_b, HEAD_DIM), 0.1),
        "diff_subln": gain((n_b, 2 * HEAD_DIM)),
        "diff_w_o": dense((n_b, D_MODEL, D_MODEL), D_MODEL),
        "lru_w_in": dense((n_c, D_MODEL, 2 * LRU_WIDTH), D_MODEL),
        "lru_conv_w": dense((n_c, 2, LRU_CONV, LRU_WIDTH), LRU_CONV),
        "lru_conv_b": small((n_c, 2, LRU_WIDTH)),
        "lru_w_a": dense((n_c, 2, LRU_BLOCKS, LRU_BLOCK_DIM, LRU_BLOCK_DIM), LRU_BLOCK_DIM),
        "lru_b_a": small((n_c, 2, LRU_WIDTH)),
        "lru_w_x": dense((n_c, 2, LRU_BLOCKS, LRU_BLOCK_DIM, LRU_BLOCK_DIM), LRU_BLOCK_DIM),
        "lru_b_x": small((n_c, 2, LRU_WIDTH)),
        "lru_lambda": lru_lambda,
        "lru_w_out": dense((n_c, LRU_WIDTH, D_MODEL), LRU_WIDTH),
        "dil_w_qkv": dense((n_d, D_MODEL, len(DIL_GROUPS) * 3 * DIL_WIDTH), D_MODEL),
        "dil_w_o": dense((n_d, DIL_WIDTH, D_MODEL), DIL_WIDTH),
        "ffn_norm": gain((DEPTH_2, D_MODEL)),
        "ffn_w_up": dense((DEPTH_2, D_MODEL, 2 * D_FF_2), D_MODEL),
        "ffn_conv_w": dense((DEPTH_2, FFN_CONV, D_FF_2), FFN_CONV),
        "ffn_conv_b": small((DEPTH_2, D_FF_2)),
        "ffn_w_down": dense((DEPTH_2, D_FF_2, D_MODEL), D_FF_2),
        "final_norm": gain((D_MODEL,)),
    }

def second_block(x, positions, mix_norm, pool_w, pool_scale, diff_w_qkv, diff_lam_q1, diff_lam_k1,
              diff_lam_q2, diff_lam_k2, diff_subln, diff_w_o, lru_w_in, lru_conv_w, lru_conv_b,
              lru_w_a, lru_b_a, lru_w_x, lru_b_x, lru_lambda, lru_w_out, dil_w_qkv, dil_w_o,
              ffn_norm, ffn_w_up, ffn_conv_w, ffn_conv_b, ffn_w_down, final_norm):
    cos, sin = _rope_tables(positions, HEAD_DIM)
    h = x
    for i in range(DEPTH_2):
        m, j = i % N_MIXERS, i // N_MIXERS
        hn = _rms_norm(h, mix_norm[i])
        if m == 0:
            y = _pool_mixer(hn, pool_w[j], pool_scale[j])
        elif m == 1:
            y = _diff_attention(hn, diff_w_qkv[j], diff_lam_q1[j], diff_lam_k1[j], diff_lam_q2[j],
                                diff_lam_k2[j], diff_subln[j], diff_w_o[j], cos, sin, i)
        elif m == 2:
            y = _rglru_mixer(hn, lru_w_in[j], lru_conv_w[j], lru_conv_b[j], lru_w_a[j], lru_b_a[j],
                             lru_w_x[j], lru_b_x[j], lru_lambda[j], lru_w_out[j])
        else:
            y = _dilated_mixer(hn, dil_w_qkv[j], dil_w_o[j], cos, sin)
        h = h + y
        h = h + _conv_ffn(_rms_norm(h, ffn_norm[i]), ffn_w_up[i], ffn_conv_w[i], ffn_conv_b[i], ffn_w_down[i])
    return _rms_norm(h, final_norm)


def setup_inputs(seed=0):
    out = dict(first_inputs(seed))
    for name, value in second_inputs(seed + 1).items():
        if name != "x":
            out[name + "_2"] = value
    return out


def reference(
    x, c, w_ada, b_ada, norm1_w, w_in, gdn_conv_w, gdn_a_log, gdn_dt_bias, gdn_norm_w,
    w_gdn_proj, sc_conv_w, w_sc_out, w_o, norm2_w, w_ffn_in, w_ffn_out, w_ada_f, b_ada_f,
    normf_w, positions_2, mix_norm_2, pool_w_2, pool_scale_2, diff_w_qkv_2, diff_lam_q1_2,
    diff_lam_k1_2, diff_lam_q2_2, diff_lam_k2_2, diff_subln_2, diff_w_o_2, lru_w_in_2,
    lru_conv_w_2, lru_conv_b_2, lru_w_a_2, lru_b_a_2, lru_w_x_2, lru_b_x_2, lru_lambda_2,
    lru_w_out_2, dil_w_qkv_2, dil_w_o_2, ffn_norm_2, ffn_w_up_2, ffn_conv_w_2, ffn_conv_b_2,
    ffn_w_down_2, final_norm_2,
):
    x = first_block(
        x, c, w_ada, b_ada, norm1_w, w_in, gdn_conv_w, gdn_a_log, gdn_dt_bias, gdn_norm_w,
        w_gdn_proj, sc_conv_w, w_sc_out, w_o, norm2_w, w_ffn_in, w_ffn_out, w_ada_f, b_ada_f,
        normf_w,
    )
    return second_block(
        x, positions_2, mix_norm_2, pool_w_2, pool_scale_2, diff_w_qkv_2, diff_lam_q1_2,
        diff_lam_k1_2, diff_lam_q2_2, diff_lam_k2_2, diff_subln_2, diff_w_o_2, lru_w_in_2,
        lru_conv_w_2, lru_conv_b_2, lru_w_a_2, lru_b_a_2, lru_w_x_2, lru_b_x_2, lru_lambda_2,
        lru_w_out_2, dil_w_qkv_2, dil_w_o_2, ffn_norm_2, ffn_w_up_2, ffn_conv_w_2, ffn_conv_b_2,
        ffn_w_down_2, final_norm_2,
    )


_drawn_inputs = setup_inputs


def setup_inputs(seed=0):
    import zlib

    import numpy as np

    out = dict(_drawn_inputs(seed))
    spreads = {}
    factors = {'norm1_w': 6.455,
     'gdn_norm_w': 64.0,
     'norm2_w': 64.0,
     'diff_lam_q1_2': 4.619,
     'diff_lam_k1_2': 3.298,
     'diff_lam_k2_2': 2.911,
     'ffn_conv_b_2': 4.737,
     'gdn_a_log': 3.138}
    for name, (base, spread) in spreads.items():
        noise = np.random.default_rng([zlib.crc32(name.encode()), seed]).standard_normal(out[name].shape)
        drawn = base * np.exp(spread * noise) if base else spread * noise
        out[name] = jnp.asarray(drawn.astype(out[name].dtype))
    for name, factor in factors.items():
        out[name] = (out[name] * factor).astype(out[name].dtype)
    return out
```

```python
from contextlib import ExitStack

import numpy as np

import concourse.bass as bass
from concourse import mybir

F32, F32R, I32 = mybir.dt.float32, mybir.dt.float32r, mybir.dt.int32
ALU = mybir.AluOpType
ACT = mybir.ActivationFunctionType
AX_X = mybir.AxisListType.X
MULT, ADD, SUB = ALU.mult, ALU.add, ALU.subtract

P = 128
T = 512
D = 1024
KD = D // P
NC = T // P
H = 8
FF = 2816
KF = FF // P
UPS = KF // 2
RING = 4
LEVELS = 6
EPS = 1e-6
SUBLN_EPS = 1e-5
LAM_INIT = 0.8 - 0.6 * float(np.exp(-0.3))

Q0, K0, V0, Z0 = 0, D, 2 * D, 3 * D
AB0 = 4 * D
SCB0 = AB0 + 2 * H
SCC0, SCX0 = SCB0 + D, SCB0 + 2 * D
GA0, GB0 = SCB0 + 3 * D, SCB0 + 4 * D

SH1, SC1, G1, SH2, SC2, G2, SHF, SCF = range(0, 64, 8)

V_BADA, V_BADAF, V_N1, V_N2, V_NF, V_C, V_MIX, V_PSC, V_FIN = 0, 48, 64, 72, 80, 88, 96, 112, 120
V_CONV, V_SCONV, V_GNW, V_SUB = 128, 224, 248, 249
V_FCW = (256, 384)
V_FCB, V_FFN = 322, 366
PACK_ROWS = (128, 122, 126, 66)

C_ID, C_ONE, C_UP, C_NEG, C_L1, C_COL = 0, P, 2 * P, 3 * P, 4 * P, 5 * P
C_FREQ, C_SIGN, C_MEAN = C_COL, C_COL + 1, C_COL + 2
TWO_PI = (6.28125, 0.0019350051879882812, 3.0199157663e-07)
MAGIC = 12582912.0

S_HALF, S_GNW, S_PI2, S_SUB, S_LAM = 0, 1, 2, 3, 4
S_ALOG, S_DT, S_NEGA = 5, 6, 7
S_MS, S_RSTD, S_KSQ, S_KSS, S_KN = 8, 12, 16, 20, 24
S_EG, S_ELAST, S_ELEFT, S_LEFT, S_OMS, S_ON = 28, 32, 36, 40, 44, 48
S_KB, S_KBEG, S_KDEC = 52, 56, 60
S_MAX, S_NEG, S_SUM, S_REC, S_L = 16, 20, 24, 28, 32


def constants():
    s, c = np.arange(P)[:, None], np.arange(P)[None, :]
    tile = np.zeros((P, C_COL + 8), np.float32)
    tile[:, C_ID:C_ID + P] = s == c
    tile[:, C_ONE:C_ONE + P] = 1.0
    tile[:, C_UP:C_UP + P] = c >= s
    tile[:, C_NEG:C_NEG + P] = -1.0 * (c > s)
    tile[:, C_L1:C_L1 + P] = (s % 2 == 0) & (c == s + 1)
    inv = (np.float32(10000.0) ** (-np.arange(0, 64, 2, dtype=np.float32) / np.float32(64))).astype(np.float32)
    tile[:, C_FREQ] = np.tile(inv, 4)
    tile[:, C_SIGN] = np.where(np.arange(P) % 64 < 32, -1.0, 1.0)
    tile[:, C_MEAN] = 1.0 / P
    masks = np.zeros((P, LEVELS, P), np.float32)
    for n in range(LEVELS):
        b = 2 << n
        masks[:, n, :] = (s // (2 * b) == c // (2 * b)) & (s % (2 * b) < b) & (c % (2 * b) >= b)
    t = np.arange(T)
    counts = [np.minimum(t + w // 2, T) - np.maximum(t - w // 2, 0) for w in (2, 4, 8, 16)]
    return tile, masks, (1.0 / np.array(counts)).astype(np.float32)


class Tile:

    def __init__(self, n0, step=0, i=0):
        self.n0, self.step, self.i = n0, step, i
        self.slot, self.raw = n0 % RING, n0 % 2
        self.before = n0 + step * i
        self.loads = n0 // 2 + (step // 2) * i

    def ahead(self):
        return Tile(self.n0 + RING, self.step, self.i)


class Stage:

    def __init__(self, tile0, tiles, base, banks, times):
        self.tile0, self.tiles, self.base, self.banks, self.times = tile0, tiles, base, banks, times

    def tile(self, t, i):
        return Tile(self.tile0 + t, self.tiles, i) if self.times > 1 else Tile(self.tile0 + t)

    def out(self, j, i):
        b = self.banks[j]
        loop = self.banks.count(b) * i if self.times > 1 else 0
        return b, self.base[b] + self.banks[:j].count(b) + loop


class Stream:
    def __init__(self):
        self.tiles, self.outs = 0, [0, 0]

    def stage(self, tiles, banks, times=1):
        s = Stage(self.tiles, tiles, tuple(self.outs), tuple(banks), times)
        self.tiles += tiles * times
        for b in (0, 1):
            self.outs[b] += s.banks.count(b) * times
        return s


PE_STEPS = ["kv_tokens", "g_rows", "kk_qk", "kb_rows", "x_pairs"]
DVE_STEPS = ["diag_g", "kss", "decay_arg", "g_left", "kb", "diag_kb", "kbeg_scale", "v_beta", "k_beg", "kdec_scale",
             "k_dec", "q_g", "decay", "qk", "kb_decay", "lower", "u_pairs", "u0"]
ACT_STEPS = ["k_squares", "exp_g", "exp_g_rows", "exp_last", "exp_left", "exp_decay", "q_squares", "x_pairs"]
POOL_STEPS = ["k_norm", "strict"] + [f"mask{_n}" for _n in range(LEVELS)] + ["ada", "o_norm"]
for _n in range(LEVELS):
    _x = [f"x{_n}"] if _n < LEVELS - 1 else []
    PE_STEPS += [f"y{_n}"] + _x + [f"u{_n}"]
    ACT_STEPS += [f"u{_n}"]
    DVE_STEPS += [f"y{_n}"] + _x
PE_STEPS += ["w"]
ACT_STEPS += ["w", "o_squares", "o_hi"]
for _n in range(NC):
    PE_STEPS += [f"v_new{_n}", f"o{_n}"]
    DVE_STEPS += [f"v_new{_n}"] + ([f"state{_n}"] if _n < NC - 1 else [])
PE_STEPS += ["o_sums", "o_norm_rows"]
DVE_STEPS += ["o_sum", "o_mean", "ada", "ada_f", "o_gate", "diag_o", "o_scale", "o_lo"]

HEAD_DUE = tuple(range(3, 32, 4))
LAST_DUE = tuple(range(7, 32, 8))

ATT_PE = [f"scores{_q}" for _q in range(NC)] + [f"turn{_q}" for _q in range(NC)] + ["pv", "sums", "rows", "v_next"]
ATT_ACT = [f"exp{_q}" for _q in range(NC)] + [f"turn{_q}" for _q in range(NC)] + ["o", "squares", "hi", "v_next"]
ATT_DVE = ["max0", "neg0"]
for _n in range(NC):
    ATT_DVE += [f"max{_n + 1}", f"neg{_n + 1}"] if _n + 1 < NC else []
    ATT_DVE += [f"recip{_n}", f"lam{_n}", f"second{_n}", f"a{_n}"]
ATT_DVE += ["mean", "diag", "scale", "lo"]


def step(steps, name, h):
    return len(steps) * h + (2 + steps.index(name))


def heads(steps, h):
    return len(steps) * h + 1


def block_kernel(nc, a, out):
    stream = Stream()
    AB = stream.stage(1, [0])
    QKVZ = stream.stage(4, [1, 0, 1, 0])
    HEAD = stream.stage(8, [0, 1] * 4, H - 1)
    LAST = stream.stage(4, [0, 1] * 2)
    GATE = stream.stage(12, [0, 1] * 6, 2)
    WO = stream.stage(4, [0, 1] * 2, 2)
    UP = [stream.stage(4, [0, 1] * 2, UPS)]
    DOWN = [stream.stage(12, [0, 1] * 2, 2)]
    POOLW = stream.stage(2, [0, 1] * 4)
    UP.append(stream.stage(4, [0, 1] * 2, UPS))
    DOWN.append(stream.stage(12, [0, 1] * 2, 2))
    ATT_Q = stream.stage(3, [0, 1, 0])
    ATT_0 = stream.stage(3, [0, 1, 0])
    ATT_H = stream.stage(4, [0, 1] * 4 + [0, 1, 0], H - 2)
    ATT_7 = stream.stage(1, [0, 1] * 4)
    ATT_WO = stream.stage(1, [0, 1] * 4)
    UP.append(stream.stage(4, [0, 1] * 2, UPS))
    DOWN.append(stream.stage(12, [0, 1] * 2, 2))
    N_TILES = stream.tiles

    N_MIX, N_FFN, N_OUT1, N_POOL, N_FFN0, N_ATT, N_FFN1, N_OUT2 = range(8)
    SPLIT_NORMS = (N_MIX, N_FFN, N_FFN0, N_ATT, N_FFN1)
    SCALED_NORMS = (N_MIX, N_FFN, N_OUT1, N_FFN0, N_ATT, N_FFN1, N_OUT2)

    def split_base(r):
        return KD * SPLIT_NORMS.index(r)

    def scaled_base(r):
        return KD * SCALED_NORMS.index(r)

    POOL_STEP = []
    for m in range(KD):
        POOL_STEP.append(POOL_STEP[-1] + 3 + (m // 2 + 1) if m else 5)

    ctx = ExitStack()
    with ctx:
        place = [(nc.sbuf_base + 63) // 64 * 64]

        def sb(name, shape, dt=F32, at=None):
            size = int(np.prod(shape[1:])) * 4
            off = place[0] if at is None else at
            if at is None:
                place[0] += size
            assert off + size <= nc.sbuf_usable_end, (name, off + size, nc.sbuf_usable_end)
            return nc.alloc_sbuf_tensor_at(name, list(shape), dt, offset=off)

        raw = sb("raw", [P, 2, KD, P])
        w_hi = sb("w_hi", [P, RING, KD, P], F32R)
        w_lo = sb("w_lo", [P, RING, KD, P], F32R)
        x = sb("x", [P, KD, T])
        h_hi = sb("h_hi", [P, KD, T], F32R)
        h_lo = sb("h_lo", [P, KD, T], F32R)
        cst = sb("cst", [P, C_COL + 8])
        masks = sb("masks", [P, LEVELS, P])
        vec = sb("vec", [P, 4 * P])
        mod = sb("mod", [P, 64])
        wsc = sb("wsc", [P, 3, KD])
        cact = sb("cact", [P, 2, KD])
        small = sb("small", [P, 64])
        state = sb("state", [P, P])
        g_tok = sb("g_tok", [P, NC, 16])
        b_tok = sb("b_tok", [P, NC, 16])
        bh_tok = sb("bh_tok", [P, NC, 16])
        work = place[0]
        sq_sum = sb("sq_sum", [P, T])
        sq_tmp = sb("sq_tmp", [P, T])
        tmp = sb("tmp", [P, 6, T])
        wide = place[0]
        end = nc.sbuf_usable_end // 64 * 64

        ident, ones = cst[:, C_ID:C_ID + P], cst[:, C_ONE:C_ONE + P]
        one_col = cst[:, C_ONE:C_ONE + 1]

        x_tok = sb("x_tok", [P, NC, D], at=wide)
        pack = sb("pack", [P, 4, P], at=wide + 16384)
        ada0 = sb("ada0", [P, KD, 2 * D], at=wide + 18432)
        ada0_sum = sb("ada0_sum", [P, 2 * D], at=wide + 18432 + 65536)
        ab = [sb(f"ab{n}", [P, T], at=wide + 2048 * n) for n in range(8)]
        og_hi = sb("og_hi", [P, H, T], F32R, at=end - 65536)
        og_lo = sb("og_lo", [P, H, T], F32R, at=end - 49152)
        sc_out = sb("sc_out", [P, KD, T], at=end - 32768)
        ga_t = sb("ga_t", [P, KD, T], at=end - 16384)
        names = ["q_s", "k_s", "v_s", "z_g", "th", "cc", "dec", "low_d", "low", "qk_t", "q_g", "u_t", "x_t",
                 "y_t", "k_beg", "k_dec", "v_b", "q_sq", "dia"]
        gd = {n: sb("gd_" + n, [P, T], at=work + 2048 * j) for j, n in enumerate(names)}
        gd["cx"] = gd["th"]
        low_part = (gd["low_d"], gd["dia"])
        ada_w = sb("ada_w", [P, 2, KD // 2, P], at=work + 2048 * len(names))
        ada_s = sb("ada_s", [P, 6, P], at=work + 2048 * len(names) + 4096)
        assert work + 2048 * len(names) + 4096 + 3072 <= end - 65536
        sc_hi = sb("sc_hi", [P, KD, T], F32R, at=work)
        sc_lo = sb("sc_lo", [P, KD, T], F32R, at=work + 16384)
        gb_t = sb("gb_t", [P, 4, T], at=work + 32768)
        yb = sb("yb", [P, T], at=work + 40960)
        act_hi = sb("act_hi", [P, KF, T], F32R, at=wide)
        act_lo = sb("act_lo", [P, KF, T], F32R, at=wide + 2048 * KF)
        inv_cnt = sb("inv_cnt", [P, 4, T], at=wide)
        win = [sb(f"win{n}", [P, T + 16], at=wide + 8192 + 2112 * n) for n in range(3)]
        pool_d = sb("pool_d", [P, 2, T], at=wide + 16384)
        p_hi = sb("p_hi", [P, KD, T], F32R, at=wide + 20480)
        p_lo = sb("p_lo", [P, KD, T], F32R, at=wide + 36864)
        names = ["q_r", "k_r", "cos", "sin", "swap", "rot", "v_f", "v_tok", "o_s", "o_n", "o_sq", "dia", "ang", "rnd"]
        at = {n: sb("at_" + n, [P, T], at=wide + 2048 * j) for j, n in enumerate(names)}
        prob = sb("prob", [P, 2, 2, T], at=wide + 2048 * 14)
        a_sb = sb("a_sb", [P, 2, T], at=wide + 2048 * 18)
        a_t = sb("a_t", [P, NC, T], at=wide + 2048 * 20)
        ao_hi = sb("ao_hi", [P, T], F32R, at=wide + 2048 * 24)
        ao_lo = sb("ao_lo", [P, T], F32R, at=wide + 2048 * 25)
        wo_s = sb("wo_s", [P, 4, T], at=wide + 2048 * 26)
        lam_in = sb("lam_in", [P, 4, 64], at=wide + 2048 * 30)
        pos_i = sb("pos_i", [P, T], I32, at=wide + 2048 * 31)
        pos_f = sb("pos_f", [P, T], at=wide + 2048 * 32)
        o_tok = sb("o_tok", [P, NC, D], at=wide)

        ps = ctx.enter_context(nc.psum_tensor("ps", [P, 8, T], F32))

        def bank(b):
            return ps[:, b, :]

        def chunks(v):
            return v.rearrange("p (n c) -> p n c", n=NC)

        def part(v, n):
            return v[:, P * n:P * n + P]

        def spread(col):
            return col.unsqueeze(2).to_broadcast([P, NC, P])

        def every(tile128):
            return tile128.unsqueeze(1).to_broadcast([P, NC, P])

        def col4(c):
            return small[:, c:c + NC]

        def dyn(buf, m):
            if isinstance(m, int):
                return buf[:, m]
            return buf[:, bass.ds(m, 1), :].rearrange("p o t -> p (o t)")

        def col(buf, c):
            return buf[:, c:c + 1] if isinstance(c, int) else buf[:, bass.ds(c, 1)]

        def head_cols(tok, c):
            if isinstance(c, int):
                return tok[:, :, c]
            return tok[:, :, bass.ds(c, 1)].rearrange("p n o -> p (n o)")

        def sem(name):
            return ctx.enter_context(nc.semaphore(name))

        w_landed = [sem("w_landed0"), sem("w_landed1")]
        hi_ready, lo_ready = sem("hi_ready"), sem("lo_ready")
        tile_done = sem("tile_done")
        out_used = [sem("out_used0"), sem("out_used1")]
        cst_in, pack_in, x_in, ab_in = sem("cst_in"), sem("pack_in"), sem("x_in"), sem("ab_in")
        ada_in = [sem(f"ada_in{n}") for n in range(4)]
        cnt_in, pos_in, lam_in_s, out_done = sem("cnt_in"), sem("pos_in"), sem("lam_in_s"), sem("out_done")
        pro_pe, pro_act, pro_dve, pro_pool = sem("pro_pe"), sem("pro_act"), sem("pro_dve"), sem("pro_pool")
        x_even, x_odd = sem("x_even"), sem("x_odd")
        ada0_own, ab_act, ab_dve, ab_pe = sem("ada0_own"), sem("ab_act"), sem("ab_dve"), sem("ab_pe")
        mod_ready = sem("mod_ready")
        sq_own, sq_done = sem("sq_own"), sem("sq_done")
        n_pe, n_dve, n_pool = sem("n_pe"), sem("n_dve"), sem("n_pool")
        n_t, n_ht, n_hi, h_ready = sem("n_t"), sem("n_ht"), sem("n_hi"), sem("h_ready")
        g_pe, g_dve, g_act, g_pool = sem("g_pe"), sem("g_dve"), sem("g_act"), sem("g_pool")
        cv_act, cv_dve, sc_dve = sem("cv_act"), sem("cv_dve"), sem("sc_dve")
        ada_land = [sem("ada_land0"), sem("ada_land1")]
        ada_own = sem("ada_own")
        sc_split, mixed, mix_hi, mix_lo = sem("sc_split"), sem("mixed"), sem("mix_hi"), sem("mix_lo")
        f_act, f_dve, f_hi, f_lo = sem("f_act"), sem("f_dve"), sem("f_hi"), sem("f_lo")
        pl_dve, pl_act, pl_hi, pl_lo = sem("pl_dve"), sem("pl_act"), sem("pl_hi"), sem("pl_lo")
        t_pe, t_dve, t_act, t_pool = sem("t_pe"), sem("t_dve"), sem("t_act"), sem("t_pool")
        rp_pe, rp_act, rp_dve, wo_add = sem("rp_pe"), sem("rp_act"), sem("rp_dve"), sem("wo_add")
        fin_pe, fin_act = sem("fin_pe"), sem("fin_act")
        wo_out, pl_out = sem("wo_out"), sem("pl_out")

        def rows(w):
            return w.rearrange("(k p) c -> p k c", p=P)

        w_in, w_ada, w_ada_f = rows(a["w_in"][0]), rows(a["w_ada"][0]), rows(a["w_ada_f"])
        w_gdn, w_sc, w_o = rows(a["w_gdn_proj"][0]), rows(a["w_sc_out"][0]), rows(a["w_o"][0])
        w_up = [rows(w) for w in (a["w_ffn_in"][0], a["ffn_w_up_2"][0], a["ffn_w_up_2"][1])]
        w_dn = [rows(w) for w in (a["w_ffn_out"][0], a["ffn_w_down_2"][0], a["ffn_w_down_2"][1])]
        pool_w = a["pool_w_2"][0].rearrange("g (k p) c -> p g k c", p=P)
        w_qkv, w_ao = rows(a["diff_w_qkv_2"][0]), a["diff_w_o_2"][0]
        out_t = out[0].rearrange("(n p) d -> p n d", p=P)

        ROPE_SETUP = 12

        def roped(n):
            return ROPE_SETUP + 2 * n

        block = ctx.enter_context(nc.Block())

        @block.sync
        def _(sp):
            def load(tile, src, blocks=KD):
                if tile.n0 >= 2:
                    sp.wait_ge(lo_ready, tile.before - 1)
                sp.dma_start(raw[:, tile.raw, 0:blocks, 0:src.shape[-1]], src).then_inc(w_landed[tile.raw], 16)

            def cols(w, start, k0=0, k=KD):
                return w[:, k0:k0 + k, bass.ds(start, P)]

            sp.dma_start(x_tok[:], a["x"][0].rearrange("(n p) d -> p n d", p=P)).then_inc(x_in, 16)
            for n in range(4):
                sp.dma_start(ada0[:, :, T * n:T * n + T], w_ada[:, :, T * n:T * n + T]).then_inc(ada_in[n], 16)
            sp.wait_ge(pro_dve, 1)
            load(AB.tile(0, 0), w_in[:, :, AB0:AB0 + 2 * H])
            for t, c in enumerate((Q0, K0, V0, Z0)):
                load(QKVZ.tile(t, 0), cols(w_in, c))

            def short_conv(stage, i, m):
                for t, c in enumerate((SCC0, SCX0, SCB0, GA0)):
                    load(stage.tile(t, i), cols(w_in, m * P + c))

            with sp.Fori(0, H - 1) as i:
                short_conv(HEAD, i, i)
                for t, c in enumerate((Q0, K0, V0, Z0)):
                    load(HEAD.tile(4 + t, i), cols(w_in, i * P + (c + P)))
            short_conv(LAST, 0, H - 1)
            with sp.Fori(0, 2) as i:
                for m in range(4):
                    load(GATE.tile(m, i), cols(w_in, i * (4 * P) + (GB0 + m * P)))
                for m in range(4):
                    load(GATE.tile(4 + 2 * m, i), cols(w_sc, (i + 1) * (4 * P) + (m - 4) * P))
                    load(GATE.tile(5 + 2 * m, i), cols(w_gdn, (i + 1) * (4 * P) + (m - 4) * P))
            with sp.Fori(0, 2) as i:
                for m in range(4):
                    load(WO.tile(m, i), cols(w_o, i * (4 * P) + m * P))

            def feed_forward(f):
                with sp.Fori(0, UPS) as i:
                    for j in range(2):
                        load(UP[f].tile(2 * j, i), cols(w_up[f], i * (2 * P) + j * P))
                        load(UP[f].tile(2 * j + 1, i), cols(w_up[f], i * (2 * P) + (FF + j * P)))
                with sp.Fori(0, 2) as i:
                    for m in range(4):
                        for c in range(3):
                            k = min(KD, KF - KD * c)
                            load(DOWN[f].tile(3 * m + c, i), cols(w_dn[f], i * (4 * P) + m * P, KD * c, k), k)

            feed_forward(0)
            for t in range(2):
                tile = POOLW.tile(t, 0)
                sp.wait_ge(lo_ready, tile.before - 1)
                dst = raw[:, tile.raw].rearrange("p (g k e) c -> p (g k) (e c)", g=2, k=2)
                sp.dma_start(dst, pool_w[:, 2 * t:2 * t + 2].rearrange("p g k c -> p (g k) c"))\
                  .then_inc(w_landed[tile.raw], 16)
            sp.wait_ge(tile_done, POOLW.tile0)
            sp.dma_start(inv_cnt[:], a["const_counts"].rearrange("(o g) t -> o g t", o=1).to_broadcast([P, 4, T]))\
              .then_inc(cnt_in, 16)
            feed_forward(1)
            for t, which in enumerate((1, 2, 0)):
                load(ATT_Q.tile(t, 0), cols(w_qkv, which * D))
            sp.wait_ge(tile_done, ATT_Q.tile0)
            sp.dma_start(pos_i[0:1, :], a["positions_2"].rearrange("(o t) -> o t", o=1)).then_inc(pos_in, 16)
            for n, name in enumerate(("diff_lam_q1_2", "diff_lam_k1_2", "diff_lam_q2_2", "diff_lam_k2_2")):
                sp.dma_start(lam_in[0:1, n, :], a[name]).then_inc(lam_in_s, 16)

            def wo_rows(stage, i, h):
                tile = stage.tile(0, i)
                sp.wait_ge(lo_ready, tile.before - 1)
                sp.dma_start(raw[:, tile.raw], w_ao[bass.ds(h * P, P), :].rearrange("p (m c) -> p m c", c=P))\
                  .then_inc(w_landed[tile.raw], 16)

            for t, which in enumerate((1, 2, 0)):
                load(ATT_0.tile(t, 0), cols(w_qkv, P + which * D))
            with sp.Fori(0, H - 2) as i:
                wo_rows(ATT_H, i, i)
                for t, which in enumerate((1, 2, 0)):
                    load(ATT_H.tile(1 + t, i), cols(w_qkv, i * P + (which * D + 2 * P)))
            wo_rows(ATT_7, 0, H - 2)
            wo_rows(ATT_WO, 0, H - 1)
            feed_forward(2)
            for m in range(KD):
                sp.wait_ge(fin_act, m + 1)
                sp.dma_start(out_t[:, :, m * P:m * P + P], o_tok[:, :, m * P:m * P + P]).then_inc(out_done, 16)
            sp.wait_ge(out_done, 16 * KD)

        @block.gpsimd
        def _(pool):
            minus_half = small[:, S_HALF:S_HALF + 1].to_broadcast([P, NC])
            done = {"own": 0, "sum": 0}

            def clear_sum():
                nc.gpsimd.memset(sq_sum[:], 0.0).then_inc(sq_own, 1)
                done["own"] += 1
                pool.wait_ge(sq_own, done["own"])

            def add_square(xm, own, summed):
                if not (isinstance(summed, int) and summed == 0):
                    pool.wait_ge(sq_done, summed)
                nc.gpsimd.tensor_tensor(sq_tmp[:], xm, xm, MULT).then_inc(sq_own, 1)
                pool.wait_ge(sq_own, own + 1)
                nc.gpsimd.tensor_tensor(sq_sum[:], sq_sum[:], sq_tmp[:], ADD).then_inc(sq_done, 1)

            def sum_in_loop(stage):
                clear_sum()
                with pool.Fori(0, 2) as i:
                    for m in range(4):
                        b, before = stage.out(m, i)
                        pool.wait_ge(out_used[b], before + 1)
                        add_square(dyn(x, 4 * i + m), 4 * i + (done["own"] + m), 4 * i + (done["sum"] + m))
                done["own"] += KD
                done["sum"] += KD

            def sum_flat(ready):
                clear_sum()
                for m in range(KD):
                    ready(m)
                    add_square(x[:, m], done["own"], done["sum"])
                    done["own"] += 1
                    done["sum"] += 1

            def factor(r):
                pool.wait_ge(n_dve, 2 * r + 1)
                nc.gpsimd.tensor_tensor(col4(S_RSTD), col4(S_MS), minus_half, ALU.pow).then_inc(n_pool, 1)

            pool.wait_ge(pro_dve, 2)
            nc.gpsimd.memset(small[:, S_HALF:S_HALF + 1], -0.5).then_inc(pro_pool, 1)
            pool.wait_ge(pro_pool, 1)
            sum_flat(lambda m: pool.wait_ge(x_odd if m % 2 else x_even, m // 2 + 1))
            factor(N_MIX)

            def head(h):
                own = [42 * h + 1]

                def ada_load(j, half):
                    ks = slice(4 * half, 4 * half + 4)
                    src = w_ada[:, ks, bass.ds(h * (4 * P) + (2 * D + j * P), P)] if j < 4 else \
                        w_ada_f[:, ks, bass.ds(h * (2 * P) + (j - 4) * P, P)]
                    nc.gpsimd.dma_start(ada_w[:, half], src).then_inc(ada_land[half], 16)

                def add(dst, a, b, op=ADD):
                    nc.gpsimd.tensor_tensor(dst, a, b, op).then_inc(ada_own, 1)
                    own[0] += 1
                    pool.wait_ge(ada_own, own[0])

                pool.wait_ge(ada_own, own[0])
                ada_load(0, 0)
                ada_load(0, 1)
                pool.wait_ge(g_dve, step(DVE_STEPS, "kss", h))
                nc.gpsimd.tensor_tensor(col4(S_KN), col4(S_KSS), minus_half, ALU.pow).then_inc(g_pool, 1)
                pool.wait_ge(g_dve, step(DVE_STEPS, "decay", h))
                nc.gpsimd.tensor_tensor(chunks(gd["low_d"][:]), chunks(gd["dec"][:]), every(cst[:, C_NEG:C_NEG + P]),
                                        MULT).then_inc(g_pool, 1)
                pool.wait_ge(g_dve, step(DVE_STEPS, "lower", h))
                for n in range(LEVELS):
                    if n >= 2:
                        pool.wait_ge(g_pe, step(PE_STEPS, f"y{n - 2}", h))
                    nc.gpsimd.tensor_tensor(chunks(low_part[n % 2][:]), chunks(gd["low"][:]), every(masks[:, n]), MULT)\
                      .then_inc(g_pool, 1)
                pool.wait_ge(g_pe, heads(PE_STEPS, h))
                for j in range(6):
                    for half in range(2):
                        w = ada_w[:, half]
                        pool.wait_ge(ada_land[half], 96 * h + 16 * (j + 1))
                        add(w, w, cact[:, 1, 4 * half:4 * half + 4].unsqueeze(2).to_broadcast([P, 4, P]), MULT)
                        add(w[:, 0:2], w[:, 0:2], w[:, 2:4])
                        add(w[:, 0] if half else ada_s[:, j], w[:, 0], w[:, 1])
                        if half:
                            add(ada_s[:, j], ada_s[:, j], w[:, 0])
                        if j < 5:
                            ada_load(j + 1, half)
                pool.sem_inc(g_pool, 1)
                pool.wait_ge(g_dve, step(DVE_STEPS, "o_mean", h))
                nc.gpsimd.tensor_tensor(col4(S_ON), col4(S_OMS), minus_half, ALU.pow).then_inc(g_pool, 1)

            pool.wait_ge(ab_dve, 29)
            pool.sem_inc(g_pool, 1)
            pool.sem_inc(ada_own, 1)
            with pool.Fori(0, H - 1) as h:
                head(h)
            head(H - 1)
            pool.wait_ge(mixed, KD)
            pool.wait_ge(mix_lo, KD)
            sum_in_loop(WO)
            factor(N_FFN)
            sum_in_loop(DOWN[0])
            factor(N_OUT1)
            sum_flat(lambda m: pool.wait_ge(n_ht, scaled_base(N_OUT1) + m + 1))
            factor(N_POOL)
            sum_flat(lambda m: pool.wait_ge(out_used[POOLW.out(m, 0)[0]], POOLW.out(m, 0)[1] + 1))
            factor(N_FFN0)
            sum_in_loop(DOWN[1])
            factor(N_ATT)

            def att_head(h):
                pool.wait_ge(t_dve, step(ATT_DVE, "mean", h))
                nc.gpsimd.tensor_tensor(col4(S_ON), col4(S_OMS), minus_half, ALU.pow).then_inc(t_pool, 1)

            def add_projection(stage, i, h):
                for m in range(KD):
                    b, before = stage.out(m, i)
                    pool.wait_ge(out_used[b], before + 1)
                    nc.gpsimd.tensor_tensor(x[:, m], x[:, m], wo_s[:, m % 4], ADD).then_inc(wo_add, 1)

            pool.sem_inc(wo_add, 4)
            att_head(0)
            with pool.Fori(0, H - 2) as i:
                add_projection(ATT_H, i, i)
                att_head(i + 1)
            add_projection(ATT_7, 0, H - 2)
            att_head(H - 1)
            add_projection(ATT_WO, 0, H - 1)
            sum_flat(lambda m: pool.wait_ge(wo_add, 8 * H + 4))
            factor(N_FFN1)
            sum_in_loop(DOWN[2])
            factor(N_OUT2)

        @block.scalar
        def _(act):
            def split(tile):
                if isinstance(tile.before, int) and tile.before >= N_TILES:
                    return
                act.wait_ge(w_landed[tile.raw], 16 * tile.loads + 16)
                if tile.n0 >= RING:
                    act.wait_ge(tile_done, tile.before - 3)
                nc.scalar.activation(w_hi[:, tile.slot], raw[:, tile.raw], ACT.Copy).then_inc(hi_ready, 1)

            def next_tile(stage, t, i):
                tile = stage.tile(t, i)
                split(tile.ahead())
                act.wait_ge(tile_done, tile.before + 1)
                return stage.out(t, i)

            def normed(r, scale, shift=None):
                base = scaled_base(r)
                for m in range(KD):
                    act.wait_ge(n_t, base + m + 1)
                    dst = x[:, m] if r == N_OUT1 else tmp[:, 2 + m % 2]
                    if m >= 2 and r in SPLIT_NORMS:
                        act.wait_ge(h_ready, split_base(r) + m - 1)
                    if m >= 2 and r == N_OUT2:
                        act.wait_ge(fin_pe, m - 1)
                    if shift is None:
                        nc.scalar.activation(dst, tmp[:, m % 2], ACT.Copy, scale=scale(m)).then_inc(n_ht, 1)
                    else:
                        nc.scalar.activation(dst, tmp[:, m % 2], ACT.Identity, bias=shift(m), scale=scale(m))\
                          .then_inc(n_ht, 1)
                    if r in SPLIT_NORMS:
                        act.wait_ge(n_ht, base + m + 1)
                        nc.scalar.activation(h_hi[:, m], dst, ACT.Copy).then_inc(n_hi, 1)
                    if r == N_OUT2 and m:
                        output(m - 1)
                if r == N_OUT2:
                    output(KD - 1)

            def output(m):
                act.wait_ge(fin_pe, m + 1)
                nc.scalar.activation(o_tok[:, :, P * m:P * m + P], chunks(bank(4 + m % 2)), ACT.Copy).then_inc(fin_act, 1)

            act.dma_start(cst[:], a["const_tile"]).then_inc(cst_in, 16)
            act.dma_start(masks[:], a["const_masks"]).then_inc(cst_in, 16)

            def by_tile(v):
                return v.rearrange("(r p) -> r p", p=P)

            def by_row_tile(v):
                return v.rearrange("j (r p) -> (j r) p", p=P)

            for first, src in ((V_BADA, by_tile(a["b_ada"][0])), (V_BADAF, by_tile(a["b_ada_f"])),
                               (V_N1, by_tile(a["norm1_w"][0])), (V_N2, by_tile(a["norm2_w"][0])),
                               (V_NF, by_tile(a["normf_w"])), (V_C, by_tile(a["c"][0])),
                               (V_MIX, by_row_tile(a["mix_norm_2"])), (V_PSC, by_tile(a["pool_scale_2"][0])),
                               (V_FIN, by_tile(a["final_norm_2"])), (V_CONV, by_row_tile(a["gdn_conv_w"][0])),
                               (V_SCONV, by_row_tile(a["sc_conv_w"][0])), (V_GNW, a["gdn_norm_w"]),
                               (V_SUB, a["diff_subln_2"]), (V_FCW[0], by_row_tile(a["ffn_conv_w_2"][0])),
                               (V_FCB, by_row_tile(a["ffn_conv_b_2"])), (V_FFN, by_row_tile(a["ffn_norm_2"])),
                               (V_FCW[1], by_row_tile(a["ffn_conv_w_2"][1]))):
                act.dma_start(pack[first % P:first % P + src.shape[0], first // P, :], src).then_inc(pack_in, 16)
            act.wait_ge(pro_dve, 2)
            for c, name in ((S_ALOG, "gdn_a_log"), (S_DT, "gdn_dt_bias")):
                act.dma_start(small[0:H, c:c + 1], a[name][0].rearrange("(p o) -> p o", o=1)).then_inc(ab_in, 16)
            for m in range(1, KD, 2):
                act.wait_ge(pro_pe, m + 1)
                nc.scalar.activation(x[:, m], bank(m), ACT.Copy).then_inc(x_odd, 1)
            act.wait_ge(pro_dve, 3)
            nc.scalar.activation(cact[:, 0], vec[:, V_C:V_C + KD], ACT.Tanh, scale=0.5).then_inc(pro_act, 1)
            split(Tile(0))
            split(Tile(1))
            act.wait_ge(mod_ready, 1)
            normed(N_MIX, lambda m: col(wsc[:, 0], m), lambda m: col(mod, SH1 + m))
            split(Tile(2))
            split(Tile(3))

            split(AB.tile(0, 0).ahead())
            act.wait_ge(out_used[0], 1)
            nc.scalar.activation(ab[1][0:16], ab[0][0:16], ACT.Abs).then_inc(ab_act, 1)
            act.wait_ge(ab_act, 1)
            nc.scalar.activation(ab[1][0:16], ab[1][0:16], ACT.Exp, scale=-1.0).then_inc(ab_act, 1)
            act.wait_ge(ab_in, 32)
            nc.scalar.activation(small[0:H, S_NEGA:S_NEGA + 1], small[0:H, S_ALOG:S_ALOG + 1], ACT.Exp).then_inc(ab_act, 1)

            def conv_tile(stage, t, i, n, hh):
                b, before = next_tile(stage, t, i)
                buf = gd[("q_s", "k_s", "v_s")[n]]
                nc.scalar.activation(buf[:], bank(b), ACT.Copy, scale=col(vec, hh + (V_CONV + 72 + 8 * n))).then_inc(cv_act, 1)
                act.wait_ge(out_used[b], before + 1)
                if not (isinstance(hh, int) and hh == 0 and n == 0):
                    act.wait_ge(cv_dve, 10 * hh + 3 * n)
                nc.scalar.activation(gd["th"][:], buf[:], ACT.Tanh, scale=0.5).then_inc(cv_act, 1)

            def z_tile(stage, t, i, hh):
                b, before = next_tile(stage, t, i)
                nc.scalar.activation(gd["z_g"][:], bank(b), ACT.Copy, scale=small[:, S_GNW:S_GNW + 1]).then_inc(cv_act, 1)
                act.wait_ge(cv_dve, 10 * hh + 9)
                nc.scalar.activation(gd["th"][:], bank(b), ACT.Tanh, scale=0.5).then_inc(out_used[b], 1)

            act.wait_ge(ab_dve, 29)
            act.sem_inc(g_act, 1)
            for n in range(3):
                conv_tile(QKVZ, n, 0, n, 0)
            z_tile(QKVZ, 3, 0, 0)

            def head(stage, i, h, due):
                served = [0]

                def serve(point):
                    while served[0] < len(due) and due[served[0]] <= point:
                        t = served[0]
                        served[0] += 1
                        if t == 0:
                            b, before = next_tile(stage, t, i)
                            nc.scalar.activation(gd["cc"][:], bank(b), ACT.Copy).then_inc(out_used[b], 1)
                        elif t == 3:
                            b, before = next_tile(stage, t, i)
                            nc.scalar.activation(dyn(ga_t, h), bank(b), ACT.Tanh, scale=0.5).then_inc(out_used[b], 1)
                        elif t < 4:
                            split(stage.tile(t, i).ahead())
                        elif t < 7:
                            if t == 4:
                                act.wait_ge(g_pe, step(PE_STEPS, "kk_qk", h))
                                act.wait_ge(g_dve, step(DVE_STEPS, "q_g", h))
                            conv_tile(stage, t, i, t - 4, h + 1)
                        else:
                            act.wait_ge(g_dve, step(DVE_STEPS, "o_gate", h))
                            z_tile(stage, t, i, h + 1)

                def after_pe(name):
                    act.wait_ge(g_pe, step(PE_STEPS, name, h))

                def after_dve(name):
                    act.wait_ge(g_dve, step(DVE_STEPS, name, h))

                after_pe("kv_tokens")
                for n in range(NC):
                    k_sq = nc.scalar.activation(part(gd["y_t"], n), part(bank(2), n), ACT.Square,
                                                accum_out=small[:, S_KSQ + n:S_KSQ + n + 1])
                k_sq.then_inc(g_act, 1)
                nc.scalar.activation(col4(S_EG), head_cols(g_tok, h), ACT.Exp).then_inc(g_act, 1)
                after_dve("g_left")
                nc.scalar.activation(gd["y_t"][:], bank(4), ACT.Exp).then_inc(g_act, 1)
                nc.scalar.activation(col4(S_ELAST), chunks(bank(4))[:, :, P - 1], ACT.Exp).then_inc(g_act, 1)
                nc.scalar.activation(col4(S_ELEFT), col4(S_LEFT), ACT.Exp).then_inc(g_act, 1)
                nc.scalar.activation(gd["dec"][:], gd["dec"][:], ACT.Exp).then_inc(g_act, 1)
                nc.scalar.activation(gd["q_sq"][:], gd["q_s"][:], ACT.Square, scale=P * 1e-3).then_inc(g_act, 1)
                serve(3)
                after_pe("x_pairs")
                nc.scalar.activation(gd["x_t"][:], bank(6), ACT.Copy).then_inc(g_act, 1)
                for n in range(LEVELS):
                    after_pe(f"u{n}")
                    nc.scalar.activation(gd["u_t"][:], bank(6), ACT.Copy).then_inc(g_act, 1)
                    if n < LEVELS - 1:
                        serve(3 * n + 8)
                after_pe("w")
                nc.scalar.activation(gd["x_t"][:], bank(7), ACT.Copy).then_inc(g_act, 1)
                serve(28)
                after_pe(f"o{NC - 1}")
                nc.scalar.activation(gd["dec"][:], bank(3), ACT.Square).then_inc(g_act, 1)
                after_dve("o_scale")
                nc.scalar.activation(dyn(og_hi, h), gd["low_d"][:], ACT.Copy).then_inc(g_act, 1)
                serve(len(PE_STEPS))

            with act.Fori(0, H - 1) as h:
                head(HEAD, h, h, HEAD_DUE)
            head(LAST, 0, H - 1, LAST_DUE)

            act.wait_ge(out_used[LAST.out(2, 0)[0]], LAST.out(2, 0)[1] + 1)
            act.wait_ge(g_dve, heads(DVE_STEPS, H))
            nc.scalar.activation(sc_hi[:], sc_out[:], ACT.Copy).then_inc(sc_split, 1)
            with act.Fori(0, 2) as i:
                for t in range(4):
                    b, before = next_tile(GATE, t, i)
                    nc.scalar.activation(gb_t[:, t], bank(b), ACT.Tanh, scale=0.5).then_inc(out_used[b], 1)
                for t in range(4, 12):
                    split(GATE.tile(t, i).ahead())
            act.wait_ge(tile_done, GATE.tile0 + 16)
            for m in range(KD):
                act.wait_ge(mixed, m + 1)
                nc.scalar.activation(h_hi[:, m], ga_t[:, m], ACT.Copy).then_inc(mix_hi, 1)
            with act.Fori(0, 2) as i:
                for t in range(4):
                    split(WO.tile(t, i).ahead())

            def feed_forward(f):
                base = 0 if f == 0 else 2 * UPS + 4 * UPS * (f - 1)
                with act.Fori(0, UPS) as i:
                    for j in range(2):
                        b, before = next_tile(UP[f], 2 * j, i)
                        if f == 0:
                            nc.scalar.activation(tmp[:, j], bank(b), ACT.Tanh, scale=0.5).then_inc(f_act, 1)
                        else:
                            nc.scalar.activation(tmp[:, 2 + j], bank(b), ACT.Identity,
                                                 bias=col(vec, 2 * i + (V_FCB + KF * (f - 1) + j)),
                                                 scale=col(vec, 2 * i + (V_FCW[f - 1] + KF + j))).then_inc(f_act, 1)
                            act.wait_ge(out_used[b], before + 1)
                            nc.scalar.activation(tmp[:, j], tmp[:, 2 + j], ACT.Gelu).then_inc(f_act, 1)
                        split(UP[f].tile(2 * j + 1, i).ahead())
                        b, before = UP[f].out(2 * j + 1, i)
                        act.wait_ge(out_used[b], before + 1)
                        nc.scalar.activation(dyn(act_hi, 2 * i + j), tmp[:, 4 + j], ACT.Copy).then_inc(f_hi, 1)
                if f == 2:
                    for n in range(24):
                        split(DOWN[f].tile(n % 12, n // 12).ahead())
                else:
                    with act.Fori(0, 2) as i:
                        for t in range(12):
                            split(DOWN[f].tile(t, i).ahead())

            act.wait_ge(mod_ready, 2)
            normed(N_FFN, lambda m: col(wsc[:, 1], m), lambda m: col(mod, SH2 + m))
            feed_forward(0)
            normed(N_OUT1, lambda m: col(wsc[:, 2], m), lambda m: col(mod, SHF + m))

            for m in range(KD):
                act.wait_ge(pl_dve, POOL_STEP[m])
                if m >= 2:
                    act.wait_ge(pl_lo, m - 1)
                nc.scalar.activation(tmp[:, 2 + m % 2], pool_d[:, m % 2], ACT.Copy, scale=col(vec, V_MIX + m))\
                  .then_inc(pl_act, 1)
                act.wait_ge(pl_act, m + 1)
                nc.scalar.activation(p_hi[:, m], tmp[:, 2 + m % 2], ACT.Copy).then_inc(pl_hi, 1)
            for t in range(2):
                split(POOLW.tile(t, 0).ahead())
            normed(N_FFN0, lambda m: col(vec, V_FFN + m))
            feed_forward(1)

            normed(N_ATT, lambda m: col(vec, V_MIX + KD + m))
            act.wait_ge(rp_dve, 8)
            nc.scalar.activation(at["sin"][:], at["ang"][:], ACT.Sin).then_inc(rp_act, 1)
            nc.scalar.activation(at["rnd"][:], at["ang"][:], ACT.Abs).then_inc(rp_act, 1)
            act.wait_ge(rp_act, 2)
            nc.scalar.activation(at["cos"][:], at["rnd"][:], ACT.Sin, bias=small[:, S_PI2:S_PI2 + 1], scale=-1.0)\
              .then_inc(rp_act, 1)
            act.wait_ge(rp_dve, 11)
            nc.scalar.activation(small[0:1, S_NEG:S_NEG + 2], small[0:1, S_MAX:S_MAX + 2], ACT.Exp).then_inc(rp_act, 1)

            def rope_tile(stage, t, j, i, n):
                tile = stage.tile(t, i)
                split(tile.ahead())
                act.wait_ge(tile_done, tile.before + 1)
                b, before = stage.out(j, i)
                act.wait_ge(rp_dve, roped(n))
                for q in range(4):
                    swapped = nc.scalar.activation(at["swap"][32 * q:32 * q + 32], ps[32 * (q ^ 1):32 * (q ^ 1) + 32, b, :],
                                                   ACT.Copy)
                swapped.then_inc(rp_act, 1)

            def v_tile(stage, t, j, i):
                tile = stage.tile(t, i)
                split(tile.ahead())
                act.wait_ge(tile_done, tile.before + 1)
                b, before = stage.out(j, i)
                nc.scalar.activation(at["v_f"][:], bank(b), ACT.Copy).then_inc(out_used[b], 1)

            def projection(stage, i, h, m):
                b, before = stage.out(m, i)
                tile = stage.tile(0, i)
                if m < KD - 1:
                    act.wait_ge(wo_out, (KD - 1) * h + m + 1)
                else:
                    split(tile.ahead())
                    act.wait_ge(tile_done, tile.before + 1)
                act.wait_ge(wo_add, KD * h + m + 1)
                nc.scalar.activation(wo_s[:, m % 4], bank(b), ACT.Copy).then_inc(out_used[b], 1)

            def att_head(stage, i, h, wo, nxt):
                t0, j0 = (1, KD) if wo else (0, 0)
                for q in range(NC):
                    act.wait_ge(t_dve, step(ATT_DVE, f"neg{q}", h))
                    if q >= 2:
                        act.wait_ge(t_dve, step(ATT_DVE, f"a{q - 2}", h))
                    for c in range(2):
                        s = 2 * (q % 2) + c
                        e = nc.scalar.activation(prob[:, q % 2, c], bank(2 + s), ACT.Exp, bias=small[:, S_NEG + s:S_NEG + s + 1],
                                                 scale=0.125, accum_out=small[:, S_SUM + s:S_SUM + s + 1])
                    e.then_inc(t_act, 1)
                    if wo:
                        projection(stage, i, h - 1, 2 * q)
                        projection(stage, i, h - 1, 2 * q + 1)
                for q in range(NC):
                    act.wait_ge(t_pe, step(ATT_PE, f"turn{q}", h))
                    nc.scalar.activation(a_t[:, :, P * q:P * q + P], chunks(bank(6)), ACT.Copy).then_inc(t_act, 1)
                if nxt:
                    rope_tile(stage, t0, j0, i, 2 * h + 2)
                act.wait_ge(t_pe, step(ATT_PE, "pv", h))
                nc.scalar.activation(at["o_s"][:], bank(7), ACT.Copy, scale=small[:, S_SUB:S_SUB + 1]).then_inc(t_act, 1)
                nc.scalar.activation(at["o_sq"][:], bank(7), ACT.Square).then_inc(t_act, 1)
                if nxt:
                    v_tile(stage, t0 + 1, j0 + 1, i)
                act.wait_ge(t_dve, step(ATT_DVE, "scale", h))
                nc.scalar.activation(ao_hi[:], at["o_n"][:], ACT.Copy).then_inc(t_act, 1)
                if nxt:
                    rope_tile(stage, t0 + 2, j0 + 2, i, 2 * h + 3)
                    act.wait_ge(t_pe, step(ATT_PE, "v_next", h))
                    nc.scalar.activation(at["v_tok"][:], bank(6), ACT.Copy).then_inc(t_act, 1)

            rope_tile(ATT_Q, 0, 0, 0, 0)
            v_tile(ATT_Q, 1, 1, 0)
            rope_tile(ATT_Q, 2, 2, 0, 1)
            act.wait_ge(t_pe, 1)
            nc.scalar.activation(at["v_tok"][:], bank(6), ACT.Copy).then_inc(t_act, 1)
            att_head(ATT_0, 0, 0, False, True)
            with act.Fori(0, H - 2) as i:
                att_head(ATT_H, i, i + 1, True, True)
            att_head(ATT_7, 0, H - 1, True, False)
            for m in range(KD):
                projection(ATT_WO, 0, H - 1, m)
            normed(N_FFN1, lambda m: col(vec, V_FFN + KD + m))
            feed_forward(2)
            normed(N_OUT2, lambda m: col(vec, V_FIN + m))

        @block.vector
        def _(dve):
            def split(tile):
                if isinstance(tile.before, int) and tile.before >= N_TILES:
                    return
                dve.wait_ge(hi_ready, tile.before + 1)
                nc.vector.tensor_tensor(w_lo[:, tile.slot], raw[:, tile.raw], w_hi[:, tile.slot].bitcast(F32), SUB)\
                  .then_inc(lo_ready, 1)

            def next_tile(stage, t, i):
                tile = stage.tile(t, i)
                split(tile.ahead())
                dve.wait_ge(tile_done, tile.before + 1)
                return stage.out(t, i)

            def token_factor(r):
                dve.wait_ge(n_pe, 2 * r + 1)
                nc.vector.tensor_scalar(col4(S_MS), bank(2)[:, 0:NC], 1.0 / D, EPS, MULT, ADD).then_inc(n_dve, 1)
                dve.wait_ge(n_pool, r + 1)
                nc.vector.tensor_tensor(chunks(tmp[:, 4]), every(ident), spread(col4(S_RSTD)), MULT).then_inc(n_dve, 1)
                dve.wait_ge(n_pe, 2 * r + 2)

            def lo_part(r, m):
                dve.wait_ge(n_hi, split_base(r) + m + 1)
                nc.vector.tensor_tensor(h_lo[:, m], tmp[:, 2 + m % 2], h_hi[:, m].bitcast(F32), SUB).then_inc(h_ready, 1)

            def normed(r):
                token_factor(r)
                for m in range(KD):
                    if m >= 2:
                        dve.wait_ge(n_ht, scaled_base(r) + m - 1)
                    nc.vector.tensor_tensor(tmp[:, m % 2], x[:, m], bank(3), MULT).then_inc(n_t, 1)
                    if r in SPLIT_NORMS and m:
                        lo_part(r, m - 1)
                if r in SPLIT_NORMS:
                    lo_part(r, KD - 1)

            nc.vector.memset(raw[:], 0.0).then_inc(pro_dve, 1)
            nc.vector.memset(small[:], 0.0).then_inc(pro_dve, 1)
            for m in range(0, KD, 2):
                dve.wait_ge(pro_pe, m + 1)
                nc.vector.tensor_copy(x[:, m], bank(m)).then_inc(x_even, 1)
            dve.wait_ge(pro_pe, 9)
            for n, rows_in in enumerate(PACK_ROWS):
                copied = nc.vector.tensor_copy(vec[:, P * n:P * n + rows_in], bank(0)[:, P * n:P * n + rows_in])
            copied.then_inc(pro_dve, 1)
            dve.wait_ge(pro_dve, 3)
            dve.wait_ge(pro_pool, 1)
            nc.vector.tensor_scalar(small[:, S_GNW:S_GNW + 1], vec[:, V_GNW:V_GNW + 1], 0.5, None, MULT)
            nc.vector.tensor_scalar(small[:, S_SUB:S_SUB + 1], vec[:, V_SUB:V_SUB + 1], 1.0 - LAM_INIT, None, MULT)
            nc.vector.memset(small[:, S_PI2:S_PI2 + 1], float(np.pi / 2))
            dve.wait_ge(pro_act, 1)
            nc.vector.scalar_tensor_tensor(cact[:, 1], cact[:, 0], 1.0, vec[:, V_C:V_C + KD], ADD, MULT).then_inc(pro_dve, 1)
            dve.wait_ge(pro_dve, 4)
            nc.vector.tensor_scalar(cact[:, 1], cact[:, 1], 0.5, None, MULT).then_inc(pro_dve, 1)
            dve.wait_ge(pro_dve, 5)
            for n in range(4):
                dve.wait_ge(ada_in[n], 16)
                total = ada0_sum[:, T * n:T * n + T]
                for k in range(KD):
                    src = ada0[:, k, T * n:T * n + T]
                    if k == 0:
                        nc.vector.tensor_scalar(total, src, cact[:, 1, k:k + 1], None, MULT).then_inc(ada0_own, 1)
                    else:
                        dve.wait_ge(ada0_own, KD * n + k)
                        nc.vector.scalar_tensor_tensor(total, src, cact[:, 1, k:k + 1], total, MULT, ADD).then_inc(ada0_own, 1)
            dve.wait_ge(pro_pe, 10)
            nc.vector.tensor_tensor(mod[:, 0:16], bank(1)[:, 0:16], vec[:, V_BADA:V_BADA + 16], ADD).then_inc(pro_dve, 1)
            dve.wait_ge(pro_dve, 6)
            nc.vector.scalar_tensor_tensor(wsc[:, 0], mod[:, SC1:SC1 + KD], 1.0, vec[:, V_N1:V_N1 + KD], ADD, MULT)\
              .then_inc(mod_ready, 1)
            split(Tile(0))
            split(Tile(1))
            normed(N_MIX)
            split(Tile(2))
            split(Tile(3))

            dve.wait_ge(ab_in, 32)
            b, before = next_tile(AB, 0, 0)
            v, e, s2, s3, s4, s5, s6, s7 = [buf[0:16] for buf in ab]
            nc.vector.tensor_scalar(v, bank(b)[0:16], small[0:16, S_DT:S_DT + 1], None, ADD).then_inc(out_used[b], 1)
            dve.wait_ge(ab_act, 2)
            links = [0]

            def link(ins):
                ins.then_inc(ab_dve, 1)
                links[0] += 1
                dve.wait_ge(ab_dve, links[0])

            link(nc.vector.tensor_scalar(s2, e, 2.0, None, ADD))
            link(nc.vector.reciprocal(s3, s2))
            link(nc.vector.tensor_tensor(s3, s3, e, MULT))
            link(nc.vector.tensor_tensor(s4, s3, s3, MULT))
            link(nc.vector.tensor_scalar(s5, s4, 1.0 / 15, None, MULT))
            for c in (13, 11, 9, 7, 5, 3):
                link(nc.vector.scalar_tensor_tensor(s5, s5, 1.0 / c, s4, ADD, MULT))
            link(nc.vector.scalar_tensor_tensor(s5, s5, 1.0, s3, ADD, MULT))
            dve.wait_ge(out_used[b], 1)
            link(nc.vector.tensor_scalar(s2, v, 0.0, None, ALU.max))
            link(nc.vector.scalar_tensor_tensor(s5, s5, 2.0, s2, MULT, ADD))
            dve.wait_ge(ab_act, 3)
            link(nc.vector.tensor_scalar(small[0:H, S_NEGA:S_NEGA + 1], small[0:H, S_NEGA:S_NEGA + 1], -1.0, None, MULT))
            link(nc.vector.tensor_scalar(s5, s5, small[0:16, S_NEGA:S_NEGA + 1], None, MULT))
            link(nc.vector.memset(s6, 1.0))
            link(nc.vector.memset(chunks(s6)[:, :, 0:1], 0.0))
            link(nc.vector.tensor_tensor_scan(s7, s6, s5, 0.0, MULT, ADD))
            link(nc.vector.tensor_scalar(s2, e, 1.0, None, ADD))
            link(nc.vector.reciprocal(s4, s2))
            link(nc.vector.tensor_scalar(s3, v, 0.0, None, ALU.is_ge))
            link(nc.vector.tensor_scalar(s2, e, -1.0, 1.0, MULT, ADD))
            link(nc.vector.tensor_tensor(s3, s3, s2, MULT))
            link(nc.vector.tensor_tensor(s3, s3, e, ADD))
            link(nc.vector.tensor_tensor(s3, s3, s4, MULT))
            dve.wait_ge(ab_pe, 1)
            link(nc.vector.tensor_copy(g_tok[:], bank(2)[:, 0:16 * NC].rearrange("p (n c) -> p n c", n=NC)))
            dve.wait_ge(ab_pe, 2)
            beta = bank(3)[:, 0:16 * NC].rearrange("p (n c) -> p n c", n=NC)
            link(nc.vector.tensor_copy(b_tok[:], beta))
            link(nc.vector.tensor_scalar(bh_tok[:], beta, 0.5, None, MULT))
            dve.sem_inc(g_dve, 1)

            def conv_tile(stage, t, i, n, hh):
                b, before = next_tile(stage, t, i)
                buf = gd[("q_s", "k_s", "v_s")[n]]
                dve.wait_ge(cv_act, 7 * hh + 2 * n + 1)
                for d in (1, 2, 3):
                    if d > 1:
                        dve.wait_ge(cv_dve, 10 * hh + 3 * n + d - 1)
                    nc.vector.scalar_tensor_tensor(buf[:, d:T], bank(b)[:, 0:T - d],
                                                   col(vec, hh + (V_CONV + 24 * (3 - d) + 8 * n)), buf[:, d:T], MULT, ADD)\
                      .then_inc(*((cv_dve, 1) if d < 3 else (out_used[b], 1)))
                dve.wait_ge(cv_act, 7 * hh + 2 * n + 2)
                nc.vector.scalar_tensor_tensor(buf[:], gd["th"][:], 1.0, buf[:], ADD, MULT).then_inc(cv_dve, 1)

            def z_tile(stage, t, i, hh):
                b, before = next_tile(stage, t, i)
                dve.wait_ge(cv_act, 7 * hh + 7)
                dve.wait_ge(out_used[b], before + 1)
                nc.vector.scalar_tensor_tensor(gd["z_g"][:], gd["th"][:], 1.0, gd["z_g"][:], ADD, MULT).then_inc(cv_dve, 1)

            for n in range(3):
                conv_tile(QKVZ, n, 0, n, 0)
            z_tile(QKVZ, 3, 0, 0)

            def head(stage, i, h, due):
                served = [0]

                def serve(point):
                    while served[0] < len(due) and due[served[0]] <= point:
                        t = served[0]
                        served[0] += 1
                        if t == 1:
                            b0, before0 = stage.out(0, i)
                            b, before = next_tile(stage, t, i)
                            dve.wait_ge(out_used[b0], before0 + 1)
                            nc.vector.tensor_tensor(gd["cx"][:], gd["cc"][:], bank(b), MULT).then_inc(out_used[b], 1)
                            dve.wait_ge(out_used[b], before + 1)
                            nc.vector.tensor_scalar(gd["cc"][:], gd["cx"][:], col(vec, h + (V_SCONV + 16)), None, MULT)\
                              .then_inc(sc_dve, 1)
                            for d in (1, 2):
                                dve.wait_ge(sc_dve, 3 * h + d)
                                nc.vector.scalar_tensor_tensor(gd["cc"][:, d:T], gd["cx"][:, 0:T - d],
                                                               col(vec, h + (V_SCONV + 8 * (2 - d))), gd["cc"][:, d:T],
                                                               MULT, ADD).then_inc(sc_dve, 1)
                        elif t == 2:
                            b, before = next_tile(stage, t, i)
                            dve.wait_ge(sc_dve, 3 * h + 3)
                            nc.vector.tensor_tensor(dyn(sc_out, h), gd["cc"][:], bank(b), MULT).then_inc(out_used[b], 1)
                        elif t < 4:
                            split(stage.tile(t, i).ahead())
                        elif t < 7:
                            conv_tile(stage, t, i, t - 4, h + 1)
                        else:
                            z_tile(stage, t, i, h + 1)

                def after_pe(name):
                    dve.wait_ge(g_pe, step(PE_STEPS, name, h))

                def after_act(name):
                    dve.wait_ge(g_act, step(ACT_STEPS, name, h))

                def after_pool(name):
                    dve.wait_ge(g_pool, step(POOL_STEPS, name, h))

                def own(name):
                    dve.wait_ge(g_dve, step(DVE_STEPS, name, h))

                g_col = head_cols(g_tok, h)
                nc.vector.tensor_tensor(chunks(gd["dia"][:]), every(ident), spread(g_col), MULT).then_inc(g_dve, 1)
                after_act("k_squares")
                nc.vector.tensor_scalar(col4(S_KSS), col4(S_KSQ), 4 * EPS, None, ADD).then_inc(g_dve, 1)
                after_pe("g_rows")
                for n in range(NC):
                    arg = nc.vector.tensor_scalar(part(gd["dec"], n), part(bank(4), n), col(g_tok[:, n], h), 0.0, SUB, ALU.min)
                arg.then_inc(g_dve, 1)
                nc.vector.tensor_tensor(col4(S_LEFT), chunks(bank(4))[:, :, P - 1], g_col, SUB).then_inc(g_dve, 1)
                after_pool("k_norm")
                nc.vector.tensor_tensor(col4(S_KB), col4(S_KN), head_cols(b_tok, h + H), MULT).then_inc(g_dve, 1)
                own("kb")
                nc.vector.tensor_tensor(chunks(gd["dia"][:]), every(ident), spread(col4(S_KB)), MULT).then_inc(g_dve, 1)
                after_act("exp_g")
                nc.vector.scalar_tensor_tensor(col4(S_KBEG), col4(S_KB), -1.0, col4(S_EG), MULT, MULT).then_inc(g_dve, 1)
                after_pe("kv_tokens")
                nc.vector.tensor_tensor(chunks(gd["v_b"][:]), chunks(bank(3)), spread(head_cols(bh_tok, h + H)), MULT)\
                  .then_inc(g_dve, 1)
                own("kbeg_scale")
                nc.vector.tensor_tensor(chunks(gd["k_beg"][:]), chunks(bank(2)), spread(col4(S_KBEG)), MULT).then_inc(g_dve, 1)
                after_act("exp_left")
                nc.vector.tensor_tensor(col4(S_KDEC), col4(S_KN), col4(S_ELEFT), MULT).then_inc(g_dve, 1)
                own("kdec_scale")
                nc.vector.tensor_tensor(chunks(gd["k_dec"][:]), chunks(bank(2)), spread(col4(S_KDEC)), MULT).then_inc(g_dve, 1)
                after_act("exp_g_rows")
                nc.vector.tensor_tensor(gd["q_g"][:], gd["q_s"][:], gd["y_t"][:], MULT).then_inc(g_dve, 1)
                after_act("exp_decay")
                nc.vector.tensor_tensor(chunks(gd["dec"][:]), chunks(gd["dec"][:]), every(cst[:, C_UP:C_UP + P]), MULT)\
                  .then_inc(g_dve, 1)
                after_pe("kk_qk")
                own("decay")
                for n in range(NC):
                    qk = nc.vector.scalar_tensor_tensor(part(gd["qk_t"], n), part(bank(6), n), small[:, S_KN + n:S_KN + n + 1],
                                                        part(gd["dec"], n), MULT, MULT)
                qk.then_inc(g_dve, 1)
                after_pool("strict")
                after_pe("kb_rows")
                nc.vector.tensor_tensor(gd["low_d"][:], gd["low_d"][:], bank(7), MULT).then_inc(g_dve, 1)
                own("kb_decay")
                for n in range(NC):
                    low = nc.vector.scalar_tensor_tensor(part(gd["low"], n), part(bank(5), n), small[:, S_KN + n:S_KN + n + 1],
                                                         part(gd["low_d"], n), MULT, MULT)
                low.then_inc(g_dve, 1)
                own("lower")
                nc.vector.tensor_tensor(chunks(gd["u_t"][:]), chunks(gd["low"][:]), every(cst[:, C_L1:C_L1 + P]), MULT)\
                  .then_inc(g_dve, 1)
                own("u_pairs")
                nc.vector.tensor_tensor(chunks(gd["u_t"][:]), chunks(gd["u_t"][:]), every(ident), ADD).then_inc(g_dve, 1)
                serve(5)
                for n in range(LEVELS):
                    after_pe(f"y{n}")
                    nc.vector.tensor_tensor(chunks(gd["y_t"][:]), chunks(bank(4)), every(ident), ADD).then_inc(g_dve, 1)
                    if n < LEVELS - 1:
                        after_pe(f"x{n}")
                        nc.vector.tensor_copy(gd["x_t"][:], bank(5)).then_inc(g_dve, 1)
                        serve(3 * n + 8)
                serve(23)
                for n in range(NC):
                    after_pe(f"v_new{n}")
                    nc.vector.tensor_copy(part(gd["y_t"], n), part(bank(2), n)).then_inc(g_dve, 1)
                    if n < NC - 1:
                        after_pe(f"o{n}")
                        if n == 0:
                            nc.vector.tensor_copy(state[:], part(bank(4), 0)).then_inc(g_dve, 1)
                        else:
                            nc.vector.scalar_tensor_tensor(state[:], state[:], small[:, S_ELAST + n:S_ELAST + n + 1],
                                                           part(bank(4), 0), MULT, ADD).then_inc(g_dve, 1)
                    if n == 1:
                        serve(28)
                after_act("o_squares")
                nc.vector.tensor_tensor(gd["dec"][:], gd["dec"][:], gd["q_sq"][:], ADD).then_inc(g_dve, 1)
                after_pe("o_sums")
                nc.vector.tensor_scalar(col4(S_OMS), bank(5)[:, 0:NC], P * EPS * 4 * EPS, None, ADD).then_inc(g_dve, 1)
                nc.vector.tensor_tensor(mod[:, bass.ds(4 * h + 16, 4)], bank(5)[:, 8:12],
                                        vec[:, bass.ds(4 * h + (V_BADA + 16), 4)], ADD).then_inc(g_dve, 1)
                nc.vector.tensor_tensor(mod[:, bass.ds(2 * h + 48, 2)], bank(5)[:, 12:14],
                                        vec[:, bass.ds(2 * h + V_BADAF, 2)], ADD).then_inc(g_dve, 1)
                dve.wait_ge(cv_dve, 10 * h + 10)
                nc.vector.tensor_tensor(gd["low"][:], bank(3), gd["z_g"][:], MULT).then_inc(g_dve, 1)
                after_pool("o_norm")
                nc.vector.tensor_tensor(chunks(gd["dia"][:]), every(ident), spread(col4(S_ON)), MULT).then_inc(g_dve, 1)
                after_pe("o_norm_rows")
                own("o_gate")
                nc.vector.tensor_tensor(gd["low_d"][:], gd["low"][:], bank(6), MULT).then_inc(g_dve, 1)
                after_act("o_hi")
                nc.vector.tensor_tensor(dyn(og_lo, h), gd["low_d"][:], dyn(og_hi, h).bitcast(F32), SUB).then_inc(g_dve, 1)
                serve(len(PE_STEPS))

            with dve.Fori(0, H - 1) as h:
                head(HEAD, h, h, HEAD_DUE)
            head(LAST, 0, H - 1, LAST_DUE)

            dve.wait_ge(g_dve, heads(DVE_STEPS, H))
            nc.vector.scalar_tensor_tensor(wsc[:, 1], mod[:, SC2:SC2 + KD], 1.0, vec[:, V_N2:V_N2 + KD], ADD, MULT)
            nc.vector.scalar_tensor_tensor(wsc[:, 2], mod[:, SCF:SCF + KD], 1.0, vec[:, V_NF:V_NF + KD], ADD, MULT)
            nc.vector.tensor_scalar(mod[:, G1:G1 + KD], mod[:, G1:G1 + KD], 0.5, None, MULT).then_inc(mod_ready, 1)
            dve.wait_ge(sc_split, 1)
            nc.vector.tensor_tensor(sc_lo[:], sc_out[:], sc_hi[:].bitcast(F32), SUB).then_inc(sc_split, 1)
            with dve.Fori(0, 2) as i:
                for t in range(4):
                    split(GATE.tile(t, i).ahead())
                for m in range(4):
                    bg, before_g = GATE.out(m, i)
                    b, before = next_tile(GATE, 4 + 2 * m, i)
                    dve.wait_ge(out_used[bg], before_g + 1)
                    nc.vector.scalar_tensor_tensor(yb[:], gb_t[:, m], 1.0, bank(b), ADD, MULT).then_inc(out_used[b], 1)
                    b2, before2 = next_tile(GATE, 5 + 2 * m, i)
                    ga = dyn(ga_t, 4 * i + m)
                    nc.vector.scalar_tensor_tensor(ga, ga, 1.0, bank(b2), ADD, MULT).then_inc(out_used[b2], 1)
                    dve.wait_ge(out_used[b], before + 1)
                    dve.wait_ge(out_used[b2], before2 + 1)
                    nc.vector.tensor_tensor(ga, ga, yb[:], ADD).then_inc(mixed, 1)
                    dve.wait_ge(mixed, 4 * i + m + 1)
            for m in range(KD):
                dve.wait_ge(mix_hi, m + 1)
                nc.vector.tensor_tensor(h_lo[:, m], ga_t[:, m], h_hi[:, m].bitcast(F32), SUB).then_inc(mix_lo, 1)
            dve.wait_ge(mod_ready, 2)
            with dve.Fori(0, 2) as i:
                for t in range(4):
                    b, before = next_tile(WO, t, i)
                    xm = dyn(x, 4 * i + t)
                    nc.vector.scalar_tensor_tensor(xm, bank(b), col(mod, 4 * i + (G1 + t)), xm, MULT, ADD)\
                      .then_inc(out_used[b], 1)

            def feed_forward(f):
                base = 0 if f == 0 else 2 * UPS + 4 * UPS * (f - 1)
                own = 2 * UPS * (f - 1)
                with dve.Fori(0, UPS) as i:
                    for j in range(2):
                        g, u, gu = tmp[:, 2 + j], 2 * j + 1, tmp[:, 4 + j]
                        b, before = next_tile(UP[f], 2 * j, i)
                        if f == 0:
                            dve.wait_ge(f_act, 2 * i + j + 1)
                            nc.vector.scalar_tensor_tensor(g, tmp[:, j], 1.0, bank(b), ADD, MULT).then_inc(out_used[b], 1)
                        else:
                            dve.wait_ge(f_act, 4 * i + (base + 2 * j + 1))
                            nc.vector.scalar_tensor_tensor(g[:, 1:T], bank(b)[:, 0:T - 1], col(vec, 2 * i + (V_FCW[f - 1] + j)),
                                                           g[:, 1:T], MULT, ADD).then_inc(f_dve, 1)
                            dve.wait_ge(f_dve, 2 * i + (own + j + 1))
                            nc.vector.scalar_tensor_tensor(g[:, 0:T - 1], bank(b)[:, 1:T],
                                                           col(vec, 2 * i + (V_FCW[f - 1] + 2 * KF + j)),
                                                           g[:, 0:T - 1], MULT, ADD).then_inc(out_used[b], 1)
                        bu, before_u = next_tile(UP[f], u, i)
                        if f == 0:
                            dve.wait_ge(out_used[b], before + 1)
                            nc.vector.scalar_tensor_tensor(gu, g, 0.5, bank(bu), MULT, MULT).then_inc(out_used[bu], 1)
                        else:
                            dve.wait_ge(f_act, 4 * i + (base + 2 * j + 2))
                            nc.vector.tensor_tensor(gu, tmp[:, j], bank(bu), MULT).then_inc(out_used[bu], 1)
                        dve.wait_ge(f_hi, 2 * i + (KF * f + j + 1))
                        nc.vector.tensor_tensor(dyn(act_lo, 2 * i + j), gu, dyn(act_hi, 2 * i + j).bitcast(F32), SUB)\
                          .then_inc(f_lo, 1)

                def down(i):
                    for m in range(4):
                        for c in range(3):
                            split(DOWN[f].tile(3 * m + c, i).ahead())
                        dve.wait_ge(tile_done, DOWN[f].tile(3 * m + 2, i).before + 1)
                        b, before = DOWN[f].out(m, i)
                        xm = dyn(x, 4 * i + m)
                        if f == 0:
                            nc.vector.scalar_tensor_tensor(xm, bank(b), col(mod, 4 * i + (G2 + m)), xm, MULT, ADD)\
                              .then_inc(out_used[b], 1)
                        else:
                            nc.vector.tensor_tensor(xm, xm, bank(b), ADD).then_inc(out_used[b], 1)

                if f == 2:
                    down(0)
                    down(1)
                else:
                    with dve.Fori(0, 2) as i:
                        down(i)

            normed(N_FFN)
            feed_forward(0)
            normed(N_OUT1)

            nc.vector.memset(win[0][:], 0.0).then_inc(pl_dve, 1)
            token_factor(N_POOL)
            dve.wait_ge(cnt_in, 16)
            count = 1

            def pool_lo(m):
                dve.wait_ge(pl_hi, m + 1)
                nc.vector.tensor_tensor(p_lo[:, m], tmp[:, 2 + m % 2], p_hi[:, m].bitcast(F32), SUB).then_inc(pl_lo, 1)

            for m in range(KD):
                group = m // 2
                centre = win[0][:, 8:8 + T]
                dve.wait_ge(pl_dve, count)
                dve.wait_ge(n_ht, scaled_base(N_OUT1) + m + 1)
                nc.vector.tensor_tensor(centre, x[:, m], bank(3), MULT).then_inc(pl_dve, 1)
                count += 1
                src = win[0]
                for n in range(group + 1):
                    back, ahead, edge = (1, 0, 1) if n == 0 else (1 << (n - 1), 1 << (n - 1), 1 << n)
                    dst = win[1 + n % 2]
                    lo, hi = edge, T + 16 - edge
                    dve.wait_ge(pl_dve, count)
                    nc.vector.tensor_tensor(dst[:, lo:hi], src[:, lo - back:hi - back], src[:, lo + ahead:hi + ahead], ADD)\
                      .then_inc(pl_dve, 1)
                    count += 1
                    src = dst
                if m >= 2:
                    dve.wait_ge(pl_act, m - 1)
                dve.wait_ge(pl_dve, count)
                nc.vector.tensor_tensor(pool_d[:, m % 2], src[:, 8:8 + T], inv_cnt[:, group], MULT).then_inc(pl_dve, 1)
                dve.wait_ge(pl_dve, count + 1)
                nc.vector.tensor_tensor(pool_d[:, m % 2], pool_d[:, m % 2], centre, SUB).then_inc(pl_dve, 1)
                count += 2
                assert count == POOL_STEP[m]
                if m:
                    pool_lo(m - 1)
            pool_lo(KD - 1)
            for t in range(2):
                for j in range(4):
                    m = 4 * t + j
                    b, before = POOLW.out(m, 0)
                    if j < 3:
                        dve.wait_ge(pl_out, 3 * t + j + 1)
                    else:
                        dve.wait_ge(tile_done, POOLW.tile(t, 0).before + 1)
                    nc.vector.scalar_tensor_tensor(x[:, m], bank(b), vec[:, V_PSC + m:V_PSC + m + 1], x[:, m], MULT, ADD)\
                      .then_inc(out_used[b], 1)
                split(POOLW.tile(t, 0).ahead())
            normed(N_FFN0)
            feed_forward(1)

            dve.wait_ge(pos_in, 16)
            nc.vector.tensor_copy(pos_f[0:1], pos_i[0:1]).then_inc(rp_dve, 1)
            normed(N_ATT)
            ang, rnd = at["ang"][:], at["rnd"][:]
            dve.wait_ge(rp_pe, 1)
            nc.vector.tensor_scalar(ang, bank(4), cst[:, C_FREQ:C_FREQ + 1], None, MULT).then_inc(rp_dve, 1)
            dve.wait_ge(rp_dve, 2)
            nc.vector.tensor_scalar(rnd, ang, float(1 / (2 * np.pi)), MAGIC, MULT, ADD).then_inc(rp_dve, 1)
            dve.wait_ge(rp_dve, 3)
            nc.vector.tensor_scalar(rnd, rnd, -MAGIC, None, ADD).then_inc(rp_dve, 1)
            for n in range(3):
                dve.wait_ge(rp_dve, 4 + n)
                nc.vector.scalar_tensor_tensor(ang, rnd, -TWO_PI[n], ang, MULT, ADD).then_inc(rp_dve, 1)
            dve.wait_ge(rp_dve, 7)
            nc.vector.tensor_scalar(ang, ang, 3.1415925, -3.1415925, ALU.min, ALU.max).then_inc(rp_dve, 1)
            dve.wait_ge(rp_act, 1)
            nc.vector.tensor_scalar(at["sin"][:], at["sin"][:], cst[:, C_SIGN:C_SIGN + 1], None, MULT).then_inc(rp_dve, 1)
            dve.wait_ge(lam_in_s, 64)
            pairs = lam_in[0:1].rearrange("o (c e) d -> o c e d", e=2)
            nc.vector.tensor_tensor(pairs[:, :, 0], pairs[:, :, 0], pairs[:, :, 1], MULT).then_inc(rp_dve, 1)
            dve.wait_ge(rp_dve, 10)
            nc.vector.tensor_reduce(small[0:1, S_MAX:S_MAX + 2], pairs[:, :, 0], AX_X, ADD).then_inc(rp_dve, 1)
            dve.wait_ge(rp_act, 4)
            nc.vector.scalar_tensor_tensor(small[0:1, S_SUM:S_SUM + 1], small[0:1, S_NEG:S_NEG + 1], LAM_INIT,
                                           small[0:1, S_NEG + 1:S_NEG + 2], ADD, SUB).then_inc(rp_dve, 1)

            def rope_tile(stage, t, j, i, n, name):
                split(stage.tile(t, i).ahead())
                b, before = stage.out(j, i)
                dve.wait_ge(rp_act, n + 5)
                nc.vector.tensor_tensor(at["rot"][:], bank(b), at["cos"][:], MULT).then_inc(out_used[b], 1)
                nc.vector.tensor_tensor(at["swap"][:], at["swap"][:], at["sin"][:], MULT).then_inc(rp_dve, 1)
                dve.wait_ge(out_used[b], before + 1)
                dve.wait_ge(rp_dve, roped(n) + 1)
                nc.vector.tensor_tensor(at[name][:], at["rot"][:], at["swap"][:], ADD).then_inc(rp_dve, 1)

            rope_tile(ATT_Q, 0, 0, 0, 0, "k_r")
            split(ATT_Q.tile(1, 0).ahead())
            rope_tile(ATT_Q, 2, 2, 0, 1, "q_r")
            dve.wait_ge(rp_pe, 2)
            nc.vector.tensor_copy(small[:, S_LAM:S_LAM + 1], bank(7)[:, 0:1]).then_inc(t_dve, 1)

            def att_head(stage, i, h, wo, nxt):
                t0, j0 = (1, KD) if wo else (0, 0)

                def own(name):
                    dve.wait_ge(t_dve, step(ATT_DVE, name, h))

                def maxima(q):
                    s = 2 * (q % 2)
                    dve.wait_ge(t_pe, step(ATT_PE, f"scores{q}", h))
                    nc.vector.tensor_reduce(small[:, S_MAX + s:S_MAX + s + 2], ps[:, 2 + s:4 + s, :], AX_X, ALU.max)\
                      .then_inc(t_dve, 1)
                    own(f"max{q}")
                    nc.vector.tensor_scalar(small[:, S_NEG + s:S_NEG + s + 2], small[:, S_MAX + s:S_MAX + s + 2], -0.125, None,
                                            MULT).then_inc(t_dve, 1)

                maxima(0)
                for q in range(NC):
                    if q + 1 < NC:
                        maxima(q + 1)
                    s, pr = 2 * (q % 2), prob[:, q % 2]
                    dve.wait_ge(t_act, step(ATT_ACT, f"exp{q}", h))
                    nc.vector.reciprocal(small[:, S_REC + s:S_REC + s + 2], small[:, S_SUM + s:S_SUM + s + 2]).then_inc(t_dve, 1)
                    own(f"recip{q}")
                    nc.vector.tensor_tensor(small[:, S_L + s:S_L + s + 1], small[:, S_REC + s + 1:S_REC + s + 2],
                                            small[:, S_LAM:S_LAM + 1], MULT).then_inc(t_dve, 1)
                    own(f"lam{q}")
                    nc.vector.tensor_scalar(pr[:, 1], pr[:, 1], small[:, S_L + s:S_L + s + 1], None, MULT).then_inc(t_dve, 1)
                    own(f"second{q}")
                    if q >= 2:
                        dve.wait_ge(t_pe, step(ATT_PE, f"turn{q - 2}", h))
                    nc.vector.scalar_tensor_tensor(a_sb[:, q % 2], pr[:, 0], small[:, S_REC + s:S_REC + s + 1], pr[:, 1], MULT, SUB)\
                      .then_inc(t_dve, 1)
                if wo:
                    split(stage.tile(0, i).ahead())
                if nxt:
                    rope_tile(stage, t0, j0, i, 2 * h + 2, "k_r")
                dve.wait_ge(t_pe, step(ATT_PE, "sums", h))
                nc.vector.tensor_scalar(col4(S_OMS), bank(7)[:, 0:NC], SUBLN_EPS, None, ADD).then_inc(t_dve, 1)
                dve.wait_ge(t_pool, h + 1)
                nc.vector.tensor_tensor(chunks(at["dia"][:]), every(ident), spread(col4(S_ON)), MULT).then_inc(t_dve, 1)
                dve.wait_ge(t_pe, step(ATT_PE, "rows", h))
                nc.vector.tensor_tensor(at["o_n"][:], at["o_s"][:], bank(6), MULT).then_inc(t_dve, 1)
                dve.wait_ge(t_act, step(ATT_ACT, "hi", h))
                nc.vector.tensor_tensor(ao_lo[:], at["o_n"][:], ao_hi[:].bitcast(F32), SUB).then_inc(t_dve, 1)
                if nxt:
                    split(stage.tile(t0 + 1, i).ahead())
                    rope_tile(stage, t0 + 2, j0 + 2, i, 2 * h + 3, "q_r")

            att_head(ATT_0, 0, 0, False, True)
            with dve.Fori(0, H - 2) as i:
                att_head(ATT_H, i, i + 1, True, True)
            att_head(ATT_7, 0, H - 1, True, False)
            split(ATT_WO.tile(0, 0).ahead())
            normed(N_FFN1)
            feed_forward(2)
            normed(N_OUT2)

        @block.tensor
        def _(pe):
            def open_out(out):
                b, before = out
                if not (isinstance(before, int) and before == 0):
                    pe.wait_ge(out_used[b], before)
                return b

            def term(dst, tile, k, hi, lo, first, last):
                nc.tensor.matmul(dst, w_hi[:, tile.slot, k], hi, start=first, stop=False)
                nc.tensor.matmul(dst, w_hi[:, tile.slot, k], lo, start=False, stop=False)
                return nc.tensor.matmul(dst, w_lo[:, tile.slot, k], hi, start=False, stop=last)

            def quarter(stage, t, j, i, q):
                tile = stage.tile(t, i)
                if q == 0:
                    pe.wait_ge(lo_ready, tile.before + 1)
                    open_out(stage.out(j, i))
                for k in (2 * q, 2 * q + 1):
                    last = term(bank(stage.banks[j]), tile, k, h_hi[:, k], h_lo[:, k], k == 0, k == KD - 1)
                if q == 3:
                    last.then_inc(tile_done, 1)

            def product(stage, t, i, hi, lo, ready=None):
                tile = stage.tile(t, i)
                pe.wait_ge(lo_ready, tile.before + 1)
                b = open_out(stage.out(t, i))
                for k in range(KD):
                    if ready:
                        pe.wait_ge(ready[0], ready[1] + k + 1)
                    last = term(bank(b), tile, k, hi[:, k], lo[:, k], k == 0, k == KD - 1)
                last.then_inc(tile_done, 1)

            def turn(dst, src, n_rows=P):
                return nc.tensor.transpose(dst, src, ident[0:n_rows, 0:n_rows])

            def norm(r):
                pe.wait_ge(sq_done, KD * (r + 1))
                for n in range(NC):
                    s = nc.tensor.matmul(bank(2)[:, n:n + 1], part(sq_sum, n), one_col, start=True, stop=True)
                s.then_inc(n_pe, 1)
                pe.wait_ge(n_dve, 2 * r + 2)
                nc.tensor.matmul(bank(3), ones, tmp[:, 4], start=True, stop=True).then_inc(n_pe, 1)

            pe.wait_ge(x_in, 16)
            pe.wait_ge(cst_in, 32)
            for m in range(KD):
                for n in range(NC):
                    t = turn(part(bank(m), n), x_tok[:, n, P * m:P * m + P])
                t.then_inc(pro_pe, 1)
            pe.wait_ge(pack_in, 16 * 17)
            pe.wait_ge(x_even, 1)
            for n, rows_in in enumerate(PACK_ROWS):
                t = turn(bank(0)[:, P * n:P * n + rows_in], pack[0:rows_in, n, :], rows_in)
            t.then_inc(pro_pe, 1)
            pe.wait_ge(ada0_own, 4 * KD)
            pe.wait_ge(x_odd, 1)
            for j in range(16):
                s = nc.tensor.matmul(bank(1)[:, j:j + 1], ada0_sum[:, P * j:P * j + P], one_col, start=True, stop=True)
            s.then_inc(pro_pe, 1)
            norm(N_MIX)
            product(AB, 0, 0, h_hi, h_lo, (h_ready, split_base(N_MIX)))
            pe.wait_ge(mod_ready, 1)
            for t in range(2):
                product(QKVZ, t, 0, h_hi, h_lo)
            for n_bank, (buf, count) in enumerate(((ab[7], 19), (ab[3], 26))):
                pe.wait_ge(ab_dve, count)
                for n in range(NC):
                    t = turn(bank(2 + n_bank)[:, 16 * n:16 * n + 16], part(buf[0:16], n), 16)
                t.then_inc(ab_pe, 1)
            pe.sem_inc(g_pe, 1)
            for t in range(2, 4):
                product(QKVZ, t, 0, h_hi, h_lo)

            def head(stage, i, h, every_steps, due_steps):
                q_s, k_s, v_s, x_t, y_t, u_t = [gd[n] for n in ("q_s", "k_s", "v_s", "x_t", "y_t", "u_t")]
                at_step = [0]

                def fill():
                    at_step[0] += 1
                    n, rest = divmod(at_step[0], every_steps)
                    if rest == 0 and n <= 4 * stage.tiles:
                        quarter(stage, (n - 1) // 4, (n - 1) // 4, i, (n - 1) % 4)

                def after_dve(name):
                    pe.wait_ge(g_dve, step(DVE_STEPS, name, h))

                def after_act(name):
                    pe.wait_ge(g_act, step(ACT_STEPS, name, h))

                def by_chunk(b, lhs, rhs, turned=False):
                    for n in range(NC):
                        if turned:
                            ins = turn(part(bank(b), n), part(lhs, n))
                        else:
                            ins = nc.tensor.matmul(part(bank(b), n), part(lhs, n), part(rhs, n), start=True, stop=True)
                    return ins

                fill()
                pe.wait_ge(cv_dve, 10 * h + 9)
                pe.wait_ge(g_dve, heads(DVE_STEPS, h))
                by_chunk(2, k_s, None, True)
                by_chunk(3, v_s, None, True).then_inc(g_pe, 1)
                fill()
                after_dve("diag_g")
                nc.tensor.matmul(bank(4), ones, gd["dia"][:], start=True, stop=True).then_inc(g_pe, 1)
                fill()
                by_chunk(5, k_s, k_s)
                by_chunk(6, k_s, q_s).then_inc(g_pe, 1)
                fill()
                after_dve("diag_kb")
                nc.tensor.matmul(bank(7), ones, gd["dia"][:], start=True, stop=True).then_inc(g_pe, 1)
                fill()
                after_dve("u0")
                by_chunk(6, u_t, None, True).then_inc(g_pe, 1)
                for n in range(LEVELS):
                    fill()
                    pe.wait_ge(g_pool, step(POOL_STEPS, f"mask{n}", h))
                    if n:
                        after_dve(f"x{n - 1}")
                    else:
                        after_act("x_pairs")
                    by_chunk(4, low_part[n % 2], x_t).then_inc(g_pe, 1)
                    fill()
                    after_dve(f"y{n}")
                    if n:
                        after_act(f"u{n - 1}")
                    if n < LEVELS - 1:
                        by_chunk(5, u_t, y_t).then_inc(g_pe, 1)
                        fill()
                    by_chunk(6, y_t, u_t).then_inc(g_pe, 1)
                fill()
                after_act(f"u{LEVELS - 1}")
                by_chunk(7, gd["k_beg"], u_t).then_inc(g_pe, 1)
                for n in range(NC):
                    fill()
                    v_new = nc.tensor.matmul(part(bank(2), n), part(u_t, n), part(gd["v_b"], n), start=True, stop=n == 0)
                    if n:
                        after_act("w")
                        after_dve(f"state{n - 1}")
                        v_new = nc.tensor.matmul(part(bank(2), n), part(x_t, n), state[:], start=False, stop=True)
                    v_new.then_inc(g_pe, 1)
                    fill()
                    after_dve(f"v_new{n}")
                    if n:
                        nc.tensor.matmul(part(bank(3), n), state[:], part(gd["q_g"], n), start=True, stop=False)
                    o = nc.tensor.matmul(part(bank(3), n), part(y_t, n), part(gd["qk_t"], n), start=n == 0, stop=True)
                    if n < NC - 1:
                        o = nc.tensor.matmul(part(bank(4), 0), part(gd["k_dec"], n), part(y_t, n), start=True, stop=True)
                    o.then_inc(g_pe, 1)
                fill()
                after_dve("o_sum")
                for n in range(NC):
                    nc.tensor.matmul(bank(5)[:, n:n + 1], part(gd["dec"], n), cst[:, C_MEAN:C_MEAN + 1], start=True, stop=True)
                pe.wait_ge(g_pool, step(POOL_STEPS, "ada", h))
                for j in range(6):
                    s = nc.tensor.matmul(bank(5)[:, 8 + j:9 + j], ada_s[:, j], one_col, start=True, stop=True)
                s.then_inc(g_pe, 1)
                fill()
                after_dve("diag_o")
                nc.tensor.matmul(bank(6), ones, gd["dia"][:], start=True, stop=True).then_inc(g_pe, 1)

            with pe.Fori(0, H - 1) as h:
                head(HEAD, h, h, 1, HEAD_DUE)
            head(LAST, 0, H - 1, 2, LAST_DUE)

            with pe.Fori(0, 2) as i:
                for t in range(4):
                    product(GATE, t, i, h_hi, h_lo)
                for m in range(4):
                    if m == 0:
                        pe.wait_ge(sc_split, 2)
                    product(GATE, 4 + 2 * m, i, sc_hi, sc_lo)
                    if m == 0:
                        pe.wait_ge(g_dve, heads(DVE_STEPS, H))
                    product(GATE, 5 + 2 * m, i, og_hi, og_lo)
            with pe.Fori(0, 2) as i:
                for t in range(4):
                    product(WO, t, i, h_hi, h_lo, (mix_lo, 0) if t == 0 else None)

            def feed_forward(f, r):
                with pe.Fori(0, UPS) as i:
                    for t in range(4):
                        product(UP[f], t, i, h_hi, h_lo, (h_ready, split_base(r)) if t == 0 else None)
                with pe.Fori(0, 2) as i:
                    for m in range(4):
                        b = open_out(DOWN[f].out(m, i))
                        for c in range(3):
                            tile = DOWN[f].tile(3 * m + c, i)
                            pe.wait_ge(lo_ready, tile.before + 1)
                            pe.wait_ge(f_lo, KF * f + min(KD * (c + 1), KF))
                            for k in range(min(KD, KF - KD * c)):
                                n = KD * c + k
                                last = term(bank(b), tile, k, act_hi[:, n], act_lo[:, n], n == 0, n == KF - 1)
                            last.then_inc(tile_done, 1)

            norm(N_FFN)
            feed_forward(0, N_FFN)
            norm(N_OUT1)

            norm(N_POOL)
            for t in range(2):
                tile = POOLW.tile(t, 0)
                pe.wait_ge(lo_ready, tile.before + 1)
                for j in range(4):
                    group, half = divmod(4 * t + j, 2)
                    b = open_out(POOLW.out(4 * t + j, 0))
                    pe.wait_ge(pl_lo, 2 * group + 2)
                    for k in range(2):
                        n = 2 * group + k
                        last = term(bank(b), tile, 4 * (group % 2) + 2 * k + half, p_hi[:, n], p_lo[:, n], k == 0, k == 1)
                    last.then_inc(tile_done if j == 3 else pl_out, 1)
            norm(N_FFN0)
            feed_forward(1, N_FFN0)

            pe.wait_ge(rp_dve, 1)
            nc.tensor.matmul(bank(4), ones[0:1, :], pos_f[0:1, :], start=True, stop=True).then_inc(rp_pe, 1)
            norm(N_ATT)
            product(ATT_Q, 0, 0, h_hi, h_lo, (h_ready, split_base(N_ATT)))
            product(ATT_Q, 1, 0, h_hi, h_lo)
            product(ATT_Q, 2, 0, h_hi, h_lo)
            pe.wait_ge(rp_dve, ROPE_SETUP)
            nc.tensor.matmul(bank(7)[:, 0:1], ones[0:1, :], small[0:1, S_SUM:S_SUM + 1], start=True, stop=True).then_inc(rp_pe, 1)

            def v_tokens(out):
                pe.wait_ge(out_used[out[0]], out[1] + 1)
                for n in range(NC):
                    t = turn(part(bank(6), n), part(at["v_f"], n))
                t.then_inc(t_pe, 1)

            v_tokens(ATT_Q.out(1, 0))

            def projection(stage, i, h, ms):
                tile = stage.tile(0, i)
                if ms[0] == 0:
                    pe.wait_ge(lo_ready, tile.before + 1)
                    pe.wait_ge(t_dve, step(ATT_DVE, "lo", h))
                for m in ms:
                    b = open_out(stage.out(m, i))
                    last = term(bank(b), tile, m, ao_hi[:], ao_lo[:], True, True)
                    last.then_inc(wo_out if m < KD - 1 else tile_done, 1)

            def att_head(stage, i, h, wo, nxt):
                t0, j0 = (1, KD) if wo else (0, 0)

                def fill(t, q):
                    if nxt:
                        quarter(stage, t0 + t, j0 + t, i, q)

                pe.wait_ge(rp_dve, roped(2 * h + 2))
                for q in range(NC):
                    if q >= 2:
                        pe.wait_ge(t_act, step(ATT_ACT, f"exp{q - 2}", h))
                    for c in range(2):
                        s = nc.tensor.matmul(bank(2 + 2 * (q % 2) + c), at["q_r"][64 * c:64 * c + 64, P * q:P * q + P],
                                             at["k_r"][64 * c:64 * c + 64, :], start=True, stop=True)
                    s.then_inc(t_pe, 1)
                    if wo:
                        projection(stage, i, h - 1, (2 * q, 2 * q + 1))
                for q in range(NC):
                    pe.wait_ge(t_dve, step(ATT_DVE, f"a{q}", h))
                    pe.wait_ge(t_act, step(ATT_ACT, f"turn{q - 1}", h) if q else heads(ATT_ACT, h))
                    for n in range(NC):
                        t = turn(part(bank(6), n), part(a_sb[:, q % 2], n))
                    t.then_inc(t_pe, 1)
                    fill(0, q)
                fill(1, 0)
                pe.wait_ge(t_act, step(ATT_ACT, f"turn{NC - 1}", h))
                for n in range(NC):
                    o = nc.tensor.matmul(bank(7), part(at["v_tok"], n), a_t[:, n], start=n == 0, stop=n == NC - 1)
                o.then_inc(t_pe, 1)
                fill(1, 1)
                fill(1, 2)
                pe.wait_ge(t_act, step(ATT_ACT, "squares", h))
                for n in range(NC):
                    s = nc.tensor.matmul(bank(7)[:, n:n + 1], part(at["o_sq"], n), cst[:, C_MEAN:C_MEAN + 1], start=True, stop=True)
                s.then_inc(t_pe, 1)
                fill(1, 3)
                pe.wait_ge(t_dve, step(ATT_DVE, "diag", h))
                nc.tensor.matmul(bank(6), ones, at["dia"][:], start=True, stop=True).then_inc(t_pe, 1)
                for q in range(4):
                    fill(2, q)
                if nxt:
                    pe.wait_ge(t_dve, step(ATT_DVE, "scale", h))
                    v_tokens(stage.out(j0 + 1, i))

            att_head(ATT_0, 0, 0, False, True)
            with pe.Fori(0, H - 2) as i:
                att_head(ATT_H, i, i + 1, True, True)
            att_head(ATT_7, 0, H - 1, True, False)
            for q in range(4):
                projection(ATT_WO, 0, H - 1, (2 * q, 2 * q + 1))
            norm(N_FFN1)
            feed_forward(2, N_FFN1)

            norm(N_OUT2)
            for m in range(KD):
                pe.wait_ge(n_ht, scaled_base(N_OUT2) + m + 1)
                if m >= 2:
                    pe.wait_ge(fin_act, m - 1)
                for n in range(NC):
                    t = turn(part(bank(4 + m % 2), n), part(tmp[:, 2 + m % 2], n))
                t.then_inc(fin_pe, 1)


def kernel(**inputs):
    import numpy as _np
    import concourse.bacc as _bacc
    from concourse import mybir as _mybir
    from concourse.bass_utils import run_bass_kernel_spmd as _run

    nc = _bacc.Bacc("TRN2", target_bir_lowering=False, num_devices=1)
    arrays = {name: _np.ascontiguousarray(v) for name, v in inputs.items() if _np.size(v)}
    tile, masks, counts = constants()
    arrays.update(const_tile=tile, const_masks=masks, const_counts=counts)
    aps = {name: nc.dram_tensor(name, v.shape, _mybir.dt.from_np(v.dtype), kind="ExternalInput").ap()
           for name, v in arrays.items()}
    out = nc.dram_tensor("out", (1, T, D), F32, kind="ExternalOutput").ap()
    block_kernel(nc, aps, out)
    r = _run(nc, [arrays], core_ids=[0])
    return r.results[0]["out"]
```

```python
from contextlib import ExitStack

import numpy as np

import concourse.bass as bass
from concourse import mybir

F32, F32R, I32 = mybir.dt.float32, mybir.dt.float32r, mybir.dt.int32
ALU = mybir.AluOpType
ACT = mybir.ActivationFunctionType
AX_X = mybir.AxisListType.X
MULT, ADD, SUB = ALU.mult, ALU.add, ALU.subtract

P = 128
T = 512
D = 1024
KD = D // P
NC = T // P
H = 8
FF = 2816
KF = FF // P
UPS = KF // 2
RING = 4
LEVELS = 6
EPS = 1e-6
SUBLN_EPS = 1e-5
LAM_INIT = 0.8 - 0.6 * float(np.exp(-0.3))

Q0, K0, V0, Z0 = 0, D, 2 * D, 3 * D
AB0 = 4 * D
SCB0 = AB0 + 2 * H
SCC0, SCX0 = SCB0 + D, SCB0 + 2 * D
GA0, GB0 = SCB0 + 3 * D, SCB0 + 4 * D

SH1, SC1, G1, SH2, SC2, G2, SHF, SCF = range(0, 64, 8)

V_BADA, V_BADAF, V_N1, V_N2, V_NF, V_C, V_MIX, V_PSC, V_FIN = 0, 48, 64, 72, 80, 88, 96, 112, 120
V_CONV, V_SCONV, V_GNW, V_SUB = 128, 224, 248, 249
V_FCW = (256, 384)
V_FCB, V_FFN = 322, 366
PACK_ROWS = (128, 122, 126, 66)

C_ID, C_ONE, C_LOW, C_L1, C_UP, C_COL = 0, P, 2 * P, 3 * P, 4 * P, 5 * P
C_FREQ, C_SIGN, C_MEAN, C_ZERO = C_COL, C_COL + 1, C_COL + 2, C_COL + 4
TWO_PI = (6.28125, 0.0019350051879882812, 3.0199157663e-07)
FORBIDDEN = -1e4
MAGIC = 12582912.0

S_HALF, S_GNW, S_PI2, S_SUB, S_LAM = 0, 1, 2, 3, 4
S_DT = 5
S_MS, S_RSTD, S_KSQ, S_KSS, S_KN = 8, 12, 16, 20, 24
S_EG, S_ELAST, S_ELEFT, S_LEFT, S_OMS, S_ON = 28, 32, 36, 40, 44, 48
S_KB, S_KBEG, S_KDEC, S_G = 52, 56, 60, 64
S_MAX, S_NEG, S_SUM, S_REC, S_L = 16, 20, 24, 28, 32


def constants():
    s, c = np.arange(P)[:, None], np.arange(P)[None, :]
    tile = np.zeros((P, C_COL + 8), np.float32)
    tile[:, C_ID:C_ID + P] = s == c
    tile[:, C_ONE:C_ONE + P] = 1.0
    tile[:, C_UP:C_UP + P] = c >= s
    tile[:, C_LOW:C_LOW + P] = np.where(c >= s, 0.0, FORBIDDEN)
    tile[:, C_L1:C_L1 + P] = (s % 2 == 0) & (c == s + 1)
    inv = (np.float32(10000.0) ** (-np.arange(0, 64, 2, dtype=np.float32) / np.float32(64))).astype(np.float32)
    tile[:, C_FREQ] = np.tile(inv, 4)
    tile[:, C_SIGN] = np.where(np.arange(P) % 64 < 32, -1.0, 1.0)
    tile[:, C_MEAN] = 1.0 / P
    masks = np.zeros((P, LEVELS, P), np.float32)
    for n in range(LEVELS):
        b = 2 << n
        masks[:, n, :] = (s // (2 * b) == c // (2 * b)) & (s % (2 * b) < b) & (c % (2 * b) >= b)
    t = np.arange(T)
    counts = [np.minimum(t + w // 2, T) - np.maximum(t - w // 2, 0) for w in (2, 4, 8, 16)]
    return tile, masks, (1.0 / np.array(counts)).astype(np.float32)


class Tile:

    def __init__(self, n0, step=0, i=0):
        self.n0, self.step, self.i = n0, step, i
        self.slot, self.raw = n0 % RING, n0 % 2
        self.before = n0 + step * i
        self.loads = n0 // 2 + (step // 2) * i

    def ahead(self):
        return Tile(self.n0 + RING, self.step, self.i)


class Stage:

    def __init__(self, tile0, tiles, base, banks, times):
        self.tile0, self.tiles, self.base, self.banks, self.times = tile0, tiles, base, banks, times

    def tile(self, t, i):
        return Tile(self.tile0 + t, self.tiles, i) if self.times > 1 else Tile(self.tile0 + t)

    def out(self, j, i):
        b = self.banks[j]
        loop = self.banks.count(b) * i if self.times > 1 else 0
        return b, self.base[b] + self.banks[:j].count(b) + loop

    def after_first(self):
        base = [n + self.banks.count(b) for b, n in enumerate(self.base)]
        return Stage(self.tile0 + self.tiles, self.tiles, base, self.banks, self.times - 1)


class Stream:
    def __init__(self):
        self.tiles, self.outs = 0, [0, 0]

    def stage(self, tiles, banks, times=1):
        s = Stage(self.tiles, tiles, tuple(self.outs), tuple(banks), times)
        self.tiles += tiles * times
        for b in (0, 1):
            self.outs[b] += s.banks.count(b) * times
        return s


PE_STEPS = ["kv_tokens", "g_rows", "kk_qk", "kb_rows", "x_pairs"]
DVE_STEPS = ["g_col", "kss", "decay_arg", "g_left", "kb", "kb_decay", "lower", "u_pairs", "u0", "q_g", "qk"]
ACT_STEPS = ["k_squares", "exp_decay", "exp_g", "exp_g_rows", "exp_last", "exp_left", "q_squares", "x_pairs"]
POOL_STEPS = ["k_norm"] + [f"mask{_n}" for _n in range(LEVELS)] + ["ada", "o_norm"]
for _n in range(LEVELS):
    _x = [f"x{_n}"] if _n < LEVELS - 1 else []
    PE_STEPS += [f"y{_n}"] + _x + [f"u{_n}"]
    ACT_STEPS += [f"u{_n}"]
    DVE_STEPS += [f"y{_n}"] + (["kbeg_scale", "v_beta", "k_beg"] if _n == 0 else []) + _x
    DVE_STEPS += ["kdec_scale", "k_dec"] if _n == 0 else []
PE_STEPS += ["w"]
ACT_STEPS += ["w", "o_squares", "o_hi"]
for _n in range(NC):
    PE_STEPS += [f"v_new{_n}", f"o{_n}"]
    DVE_STEPS += [f"v_new{_n}"] + ([f"state{_n}"] if _n < NC - 1 else [])
PE_STEPS += ["o_sums", "o_norm_rows"]
DVE_STEPS += ["o_sum", "o_mean", "ada", "ada_f", "o_gate", "o_scale", "o_lo"]

HEAD_FILL = {name: 1 for name in PE_STEPS if name != "w" and name not in [f"u{_n}" for _n in range(LEVELS - 1)]}
HEAD_FILL.update(kb_rows=2, x_pairs=3, o_sums=2, o_norm_rows=2)
LAST_FILL = {name: 1 for name in ["kv_tokens", "g_rows", "kk_qk", "kb_rows"] + [f"y{_n}" for _n in range(LEVELS)]}
LAST_FILL.update(x_pairs=2, o_sums=2, o_norm_rows=2)
assert sum(HEAD_FILL.values()) == 32 and sum(LAST_FILL.values()) == 16

ATT_PE = [f"scores{_q}" for _q in range(NC)] + [f"turn{_q}" for _q in range(NC)] + ["pv", "sums", "rows", "v_next"]
ATT_ACT = [f"exp{_q}" for _q in range(NC)] + [f"turn{_q}" for _q in range(NC)] + ["o", "squares", "hi", "v_next"]
ATT_DVE = ["max0", "neg0"]
for _n in range(NC):
    ATT_DVE += [f"max{_n + 1}", f"neg{_n + 1}"] if _n + 1 < NC else []
    ATT_DVE += [f"recip{_n}", f"lam{_n}", f"second{_n}", f"a{_n}"] + ([f"turn_lo{_n - 2}"] if _n >= 2 else [])
ATT_DVE += ["turn_lo2", "turn_lo3", "mean", "scale", "lo", "v_next_lo"]



def step(steps, name, h):
    return len(steps) * h + (2 + steps.index(name))


def heads(steps, h):
    return len(steps) * h + 1


def block_kernel(nc, a, out):
    stream = Stream()
    AB = stream.stage(1, [0])
    QKVZ = stream.stage(4, [1, 0, 1, 0])
    HEAD = stream.stage(8, [0, 1] * 4, H - 1)
    LAST = stream.stage(4, [0, 1] * 2)
    GATE = stream.stage(12, [0, 1] * 6, 2)
    WO = stream.stage(4, [0, 1] * 2, 2)
    UP = [stream.stage(4, [0, 1] * 2, UPS)]
    DOWN = [stream.stage(12, [0, 1] * 2, 2)]
    POOLW = stream.stage(2, [0, 1] * 4)
    UP.append(stream.stage(4, [0, 1] * 2, UPS))
    DOWN.append(stream.stage(12, [0, 1] * 2, 2))
    ATT_Q = stream.stage(3, [0, 1, 0])
    ATT_0 = stream.stage(3, [0, 1, 0])
    ATT_H = stream.stage(4, [0, 1] * 4 + [0, 1, 0], H - 2)
    ATT_7 = stream.stage(1, [0, 1] * 4)
    ATT_WO = stream.stage(1, [0, 1] * 4)
    UP.append(stream.stage(4, [0, 1] * 2, UPS))
    DOWN.append(stream.stage(12, [0, 1] * 2, 2))
    N_TILES = stream.tiles

    N_MIX, N_FFN, N_OUT1, N_POOL, N_FFN0, N_ATT, N_FFN1, N_OUT2 = range(8)
    SPLIT_NORMS = (N_MIX, N_FFN, N_FFN0, N_ATT, N_FFN1)
    POOL_SUMS = (N_MIX, N_FFN, N_OUT1, N_ATT, N_OUT2)
    PSUM_SUMS = (N_POOL, N_FFN0, N_FFN1)
    SCALED_NORMS = (N_MIX, N_FFN, N_OUT1, N_FFN0, N_ATT, N_FFN1, N_OUT2)

    def split_base(r):
        return KD * SPLIT_NORMS.index(r)

    def scaled_base(r):
        return KD * SCALED_NORMS.index(r)

    AB_LINKS = 26

    POOL_STEP = []
    for m in range(KD):
        POOL_STEP.append(POOL_STEP[-1] + 3 + (m // 2 + 1) if m else 5)

    ctx = ExitStack()
    with ctx:
        place = [(nc.sbuf_base + 63) // 64 * 64]

        def sb(name, shape, dt=F32, at=None):
            size = int(np.prod(shape[1:])) * 4
            off = place[0] if at is None else at
            if at is None:
                place[0] += size
            assert off + size <= nc.sbuf_usable_end, (name, off + size, nc.sbuf_usable_end)
            return nc.alloc_sbuf_tensor_at(name, list(shape), dt, offset=off)

        raw = sb("raw", [P, 2, KD, P])
        w_hi = sb("w_hi", [P, RING, KD, P], F32R)
        w_lo = sb("w_lo", [P, RING, KD, P], F32R)
        x = sb("x", [P, KD, T])
        h_hi = sb("h_hi", [P, KD, T], F32R)
        h_lo = sb("h_lo", [P, KD, T], F32R)
        cst = sb("cst", [P, C_COL + 8])
        masks = sb("masks", [P, LEVELS, P])
        vec = sb("vec", [P, 4 * P])
        mod = sb("mod", [P, 64])
        wsc = sb("wsc", [P, 3, KD])
        cact = sb("cact", [P, 2, KD])
        small = sb("small", [P, 72])
        alog = sb("alog", [P, H])
        state = sb("state", [P, P])
        g_tok = sb("g_tok", [P, NC, 16])
        b_tok = sb("b_tok", [P, NC, 16])
        bh_tok = sb("bh_tok", [P, NC, 16])
        work = place[0]
        sq_sum = sb("sq_sum", [P, T])
        sq_tmp = sb("sq_tmp", [P, T])
        tmp = sb("tmp", [P, 6, T])
        wide = place[0]
        end = nc.sbuf_usable_end // 64 * 64

        ident, ones = cst[:, C_ID:C_ID + P], cst[:, C_ONE:C_ONE + P]
        one_col = cst[:, C_ONE:C_ONE + 1]

        x_tok = sb("x_tok", [P, NC, D], at=wide)
        pack = sb("pack", [P, 4, P], at=wide + 16384)
        ada0 = sb("ada0", [P, KD, 2 * D], at=wide + 18432)
        ada0_sum = sb("ada0_sum", [P, 2 * D], at=wide + 18432 + 65536)
        ab_f = sb("ab_f", [P, T], at=wide)
        ab = [sb(f"ab{n}", [P, NC, 2 * H], at=wide + 2048 + 256 * n) for n in range(7)]
        og_hi = sb("og_hi", [P, H, T], F32R, at=end - 65536)
        og_lo = sb("og_lo", [P, H, T], F32R, at=end - 49152)
        sc_out = sb("sc_out", [P, KD, T], at=end - 32768)
        ga_t = sb("ga_t", [P, KD, T], at=end - 16384)
        names = ["q_s", "k_s", "v_s", "z_g", "th", "cc", "dec", "low_d", "low", "qk_t", "q_g", "u_t", "x_t",
                 "y_t", "k_beg", "k_dec", "v_b", "q_sq", "dia"]
        gd = {n: sb("gd_" + n, [P, T], at=work + 2048 * j) for j, n in enumerate(names)}
        gd["cx"] = gd["th"]
        low_part = (gd["low_d"], gd["dia"])
        ada_w = sb("ada_w", [P, 2, KD // 2, P], at=work + 2048 * len(names))
        ada_s = sb("ada_s", [P, 6, P], at=work + 2048 * len(names) + 4096)
        assert work + 2048 * len(names) + 4096 + 3072 <= end - 65536
        sc_hi = sb("sc_hi", [P, KD, T], F32R, at=work)
        sc_lo = sb("sc_lo", [P, KD, T], F32R, at=work + 16384)
        gb_t = sb("gb_t", [P, 4, T], at=work + 32768)
        yb = sb("yb", [P, T], at=work + 40960)
        act_hi = sb("act_hi", [P, KF, T], F32R, at=wide)
        act_lo = sb("act_lo", [P, KF, T], F32R, at=wide + 2048 * KF)
        inv_cnt = sb("inv_cnt", [P, 4, T], at=wide)
        win = [sb(f"win{n}", [P, T + 16], at=wide + 8192 + 2112 * n) for n in range(3)]
        pool_d = sb("pool_d", [P, 2, T], at=wide + 16384)
        p_hi = sb("p_hi", [P, KD, T], F32R, at=wide + 20480)
        p_lo = sb("p_lo", [P, KD, T], F32R, at=wide + 36864)
        names = ["cos", "sin", "swap", "rot", "v_f", "o_s", "o_n", "o_sq", "dia", "ang", "rnd"]
        at = {n: sb("at_" + n, [P, T], at=wide + 2048 * j) for j, n in enumerate(names)}
        split_names = ["q_hi", "q_lo", "k_hi", "k_lo", "v_hi", "v_lo", "ao_hi", "ao_lo"]
        at.update({n: sb("at_" + n, [P, T], F32R, at=wide + 2048 * (11 + j)) for j, n in enumerate(split_names)})
        prob = sb("prob", [P, 2, 2, T], at=wide + 2048 * 19)
        a_sb = sb("a_sb", [P, 2, T], at=wide + 2048 * 23)
        at_hi = sb("a_t_hi", [P, NC, T], F32R, at=wide + 2048 * 25)
        at_lo = sb("a_t_lo", [P, NC, T], F32R, at=wide + 2048 * 29)
        wo_s = sb("wo_s", [P, 4, T], at=wide + 2048 * 33)
        lam_in = sb("lam_in", [P, 4, 64], at=wide + 2048 * 37)
        pos_i = sb("pos_i", [P, T], I32, at=wide + 2048 * 38)
        pos_f = sb("pos_f", [P, T], at=wide + 2048 * 39)
        o_tok = sb("o_tok", [P, NC, D], at=wide)

        ps = ctx.enter_context(nc.psum_tensor("ps", [P, 8, T], F32))

        def bank(b):
            return ps[:, b, :]

        def chunks(v):
            return v.rearrange("p (n c) -> p n c", n=NC)

        def part(v, n):
            return v[:, P * n:P * n + P]

        def spread(col):
            return col.unsqueeze(2).to_broadcast([P, NC, P])

        def every(tile128):
            return tile128.unsqueeze(1).to_broadcast([P, NC, P])

        def col4(c):
            return small[:, c:c + NC]

        def dyn(buf, m):
            if isinstance(m, int):
                return buf[:, m]
            return buf[:, bass.ds(m, 1), :].rearrange("p o t -> p (o t)")

        def col(buf, c):
            return buf[:, c:c + 1] if isinstance(c, int) else buf[:, bass.ds(c, 1)]

        def head_cols(tok, c):
            if isinstance(c, int):
                return tok[:, :, c]
            return tok[:, :, bass.ds(c, 1)].rearrange("p n o -> p (n o)")

        def sem(name):
            return ctx.enter_context(nc.semaphore(name))

        w_landed = [sem("w_landed0"), sem("w_landed1")]
        hi_ready, lo_ready = sem("hi_ready"), sem("lo_ready")
        tile_done = sem("tile_done")
        out_used = [sem("out_used0"), sem("out_used1")]
        cst_in, pack_in, x_in, ab_in = sem("cst_in"), sem("pack_in"), sem("x_in"), sem("ab_in")
        ada_in = [sem(f"ada_in{n}") for n in range(4)]
        cnt_in, pos_in, lam_in_s, out_done = sem("cnt_in"), sem("pos_in"), sem("lam_in_s"), sem("out_done")
        pro_pe, pro_act, pro_dve, pro_pool = sem("pro_pe"), sem("pro_act"), sem("pro_dve"), sem("pro_pool")
        x_even, x_odd = sem("x_even"), sem("x_odd")
        ada0_own, ab_act, ab_dve, ab_pe = sem("ada0_own"), sem("ab_act"), sem("ab_dve"), sem("ab_pe")
        mod_ready = sem("mod_ready")
        sq_own, sq_done = sem("sq_own"), sem("sq_done")
        fsq_act, fsq_pe = sem("fsq_act"), sem("fsq_pe")
        n_pe, n_dve, n_pool = sem("n_pe"), sem("n_dve"), sem("n_pool")
        n_t, n_ht, n_hi, h_ready = sem("n_t"), sem("n_ht"), sem("n_hi"), sem("h_ready")
        g_pe, g_dve, g_act, g_pool = sem("g_pe"), sem("g_dve"), sem("g_act"), sem("g_pool")
        cv_act, cv_dve, sc_dve = sem("cv_act"), sem("cv_dve"), sem("sc_dve")
        ada_land = [sem("ada_land0"), sem("ada_land1")]
        ada_own = sem("ada_own")
        sc_split, mixed, mix_hi, mix_lo = sem("sc_split"), sem("mixed"), sem("mix_hi"), sem("mix_lo")
        f_act, f_dve, f_hi, f_lo = sem("f_act"), sem("f_dve"), sem("f_hi"), sem("f_lo")
        pl_dve, pl_act, pl_hi, pl_lo = sem("pl_dve"), sem("pl_act"), sem("pl_hi"), sem("pl_lo")
        t_pe, t_dve, t_act, t_pool = sem("t_pe"), sem("t_dve"), sem("t_act"), sem("t_pool")
        rp_pe, rp_act, rp_dve, wo_add = sem("rp_pe"), sem("rp_act"), sem("rp_dve"), sem("wo_add")
        fin_pe, fin_act = sem("fin_pe"), sem("fin_act")
        wo_out, pl_out = sem("wo_out"), sem("pl_out")

        def rows(w):
            return w.rearrange("(k p) c -> p k c", p=P)

        w_in, w_ada, w_ada_f = rows(a["w_in"][0]), rows(a["w_ada"][0]), rows(a["w_ada_f"])
        w_gdn, w_sc, w_o = rows(a["w_gdn_proj"][0]), rows(a["w_sc_out"][0]), rows(a["w_o"][0])
        w_up = [rows(w) for w in (a["w_ffn_in"][0], a["ffn_w_up_2"][0], a["ffn_w_up_2"][1])]
        w_dn = [rows(w) for w in (a["w_ffn_out"][0], a["ffn_w_down_2"][0], a["ffn_w_down_2"][1])]
        pool_w = a["pool_w_2"][0].rearrange("g (k p) c -> p g k c", p=P)
        w_qkv, w_ao = rows(a["diff_w_qkv_2"][0]), a["diff_w_o_2"][0]
        out_t = out[0].rearrange("(n p) d -> p n d", p=P)

        ROPE_SETUP = 12

        def roped(n):
            return ROPE_SETUP + 3 * n

        block = ctx.enter_context(nc.Block())

        @block.sync
        def _(sp):
            def load(tile, src, blocks=KD):
                if tile.n0 >= 2:
                    sp.wait_ge(lo_ready, tile.before - 1)
                sp.dma_start(raw[:, tile.raw, 0:blocks, 0:src.shape[-1]], src).then_inc(w_landed[tile.raw], 16)

            def cols(w, start, k0=0, k=KD):
                return w[:, k0:k0 + k, bass.ds(start, P)]

            sp.dma_start(x_tok[:], a["x"][0].rearrange("(n p) d -> p n d", p=P)).then_inc(x_in, 16)
            sp.wait_ge(pack_in, 16 * 17)
            for n in range(4):
                sp.dma_start(ada0[:, :, T * n:T * n + T], w_ada[:, :, T * n:T * n + T]).then_inc(ada_in[n], 16)
            sp.wait_ge(pro_dve, 1)
            load(AB.tile(0, 0), w_in[:, :, AB0:AB0 + 2 * H])
            for t, c in enumerate((Q0, K0, V0, Z0)):
                load(QKVZ.tile(t, 0), cols(w_in, c))

            with sp.Fori(0, H - 1) as i:
                for t, c in enumerate((SCC0, Q0 + P, K0 + P, V0 + P, SCX0, SCB0, GA0, Z0 + P)):
                    load(HEAD.tile(t, i), cols(w_in, i * P + c))
            for t, c in enumerate((SCC0, SCX0, SCB0, GA0)):
                load(LAST.tile(t, 0), cols(w_in, (H - 1) * P + c))
            with sp.Fori(0, 2) as i:
                for m in range(4):
                    load(GATE.tile(m, i), cols(w_in, i * (4 * P) + (GB0 + m * P)))
                for m in range(4):
                    load(GATE.tile(4 + 2 * m, i), cols(w_sc, (i + 1) * (4 * P) + (m - 4) * P))
                    load(GATE.tile(5 + 2 * m, i), cols(w_gdn, (i + 1) * (4 * P) + (m - 4) * P))
            with sp.Fori(0, 2) as i:
                for m in range(4):
                    load(WO.tile(m, i), cols(w_o, i * (4 * P) + m * P))

            def feed_forward(f):
                with sp.Fori(0, UPS) as i:
                    for j in range(2):
                        load(UP[f].tile(2 * j, i), cols(w_up[f], i * (2 * P) + j * P))
                        load(UP[f].tile(2 * j + 1, i), cols(w_up[f], i * (2 * P) + (FF + j * P)))
                with sp.Fori(0, 2) as i:
                    for m in range(4):
                        for c in range(3):
                            k = min(KD, KF - KD * c)
                            load(DOWN[f].tile(3 * m + c, i), cols(w_dn[f], i * (4 * P) + m * P, KD * c, k), k)

            feed_forward(0)
            for t in range(2):
                tile = POOLW.tile(t, 0)
                sp.wait_ge(lo_ready, tile.before - 1)
                dst = raw[:, tile.raw].rearrange("p (g k e) c -> p (g k) (e c)", g=2, k=2)
                sp.dma_start(dst, pool_w[:, 2 * t:2 * t + 2].rearrange("p g k c -> p (g k) c"))\
                  .then_inc(w_landed[tile.raw], 16)
            sp.wait_ge(tile_done, POOLW.tile0)
            sp.dma_start(inv_cnt[:], a["const_counts"].rearrange("(o g) t -> o g t", o=1).to_broadcast([P, 4, T]))\
              .then_inc(cnt_in, 16)
            feed_forward(1)
            for t, which in enumerate((1, 0, 2)):
                load(ATT_Q.tile(t, 0), cols(w_qkv, which * D))
            sp.wait_ge(tile_done, ATT_Q.tile0)
            sp.dma_start(pos_i[0:1, :], a["positions_2"].rearrange("(o t) -> o t", o=1)).then_inc(pos_in, 16)
            for n, name in enumerate(("diff_lam_q1_2", "diff_lam_k1_2", "diff_lam_q2_2", "diff_lam_k2_2")):
                sp.dma_start(lam_in[0:1, n, :], a[name]).then_inc(lam_in_s, 16)

            def wo_rows(stage, i, h):
                tile = stage.tile(0, i)
                sp.wait_ge(lo_ready, tile.before - 1)
                sp.dma_start(raw[:, tile.raw], w_ao[bass.ds(h * P, P), :].rearrange("p (m c) -> p m c", c=P))\
                  .then_inc(w_landed[tile.raw], 16)

            for t, which in enumerate((1, 0, 2)):
                load(ATT_0.tile(t, 0), cols(w_qkv, P + which * D))
            with sp.Fori(0, H - 2) as i:
                wo_rows(ATT_H, i, i)
                for t, which in enumerate((1, 0, 2)):
                    load(ATT_H.tile(1 + t, i), cols(w_qkv, i * P + (which * D + 2 * P)))
            wo_rows(ATT_7, 0, H - 2)
            wo_rows(ATT_WO, 0, H - 1)
            feed_forward(2)
            for m in range(KD):
                sp.wait_ge(fin_act, m + 1)
                sp.dma_start(out_t[:, :, m * P:m * P + P], o_tok[:, :, m * P:m * P + P]).then_inc(out_done, 16)
            sp.wait_ge(out_done, 16 * KD)

        @block.gpsimd
        def _(pool):
            minus_half = small[:, S_HALF:S_HALF + 1].to_broadcast([P, NC])
            done = {"own": 0, "sum": 0}

            def clear_sum():
                nc.gpsimd.memset(sq_sum[:], 0.0).then_inc(sq_own, 1)
                done["own"] += 1
                pool.wait_ge(sq_own, done["own"])

            def add_square(xm, own, summed):
                if not (isinstance(summed, int) and summed == 0):
                    pool.wait_ge(sq_done, summed)
                nc.gpsimd.tensor_tensor(sq_tmp[:], xm, xm, MULT).then_inc(sq_own, 1)
                pool.wait_ge(sq_own, own + 1)
                nc.gpsimd.tensor_tensor(sq_sum[:], sq_sum[:], sq_tmp[:], ADD).then_inc(sq_done, 1)

            def sum_in_loop(stage):
                clear_sum()
                with pool.Fori(0, 2) as i:
                    for m in range(4):
                        b, before = stage.out(m, i)
                        pool.wait_ge(out_used[b], before + 1)
                        add_square(dyn(x, 4 * i + m), 4 * i + (done["own"] + m), 4 * i + (done["sum"] + m))
                done["own"] += KD
                done["sum"] += KD

            def sum_flat(ready):
                clear_sum()
                for m in range(KD):
                    ready(m)
                    add_square(x[:, m], done["own"], done["sum"])
                    done["own"] += 1
                    done["sum"] += 1

            def factor(r):
                pool.wait_ge(n_dve, r + 1)
                nc.gpsimd.tensor_tensor(col4(S_RSTD), col4(S_MS), minus_half, ALU.pow).then_inc(n_pool, 1)

            pool.wait_ge(pro_dve, 2)
            nc.gpsimd.memset(small[:, S_HALF:S_HALF + 1], -0.5).then_inc(pro_pool, 1)
            pool.wait_ge(pro_pool, 1)
            sum_flat(lambda m: pool.wait_ge(x_odd if m % 2 else x_even, m // 2 + 1))
            factor(N_MIX)

            def head(h):
                own = [42 * h + 1]

                def ada_load(j, half):
                    ks = slice(4 * half, 4 * half + 4)
                    src = w_ada[:, ks, bass.ds(h * (4 * P) + (2 * D + j * P), P)] if j < 4 else \
                        w_ada_f[:, ks, bass.ds(h * (2 * P) + (j - 4) * P, P)]
                    nc.gpsimd.dma_start(ada_w[:, half], src).then_inc(ada_land[half], 16)

                def add(dst, a, b, op=ADD):
                    nc.gpsimd.tensor_tensor(dst, a, b, op).then_inc(ada_own, 1)
                    own[0] += 1
                    pool.wait_ge(ada_own, own[0])

                pool.wait_ge(ada_own, own[0])
                ada_load(0, 0)
                ada_load(0, 1)
                pool.wait_ge(g_dve, step(DVE_STEPS, "kss", h))
                nc.gpsimd.tensor_tensor(col4(S_KN), col4(S_KSS), minus_half, ALU.pow).then_inc(g_pool, 1)
                def modulation(j, half):
                    w = ada_w[:, half]
                    pool.wait_ge(ada_land[half], 96 * h + 16 * (j + 1))
                    add(w, w, cact[:, 1, 4 * half:4 * half + 4].unsqueeze(2).to_broadcast([P, 4, P]), MULT)
                    add(w[:, 0:2], w[:, 0:2], w[:, 2:4])
                    add(w[:, 0] if half else ada_s[:, j], w[:, 0], w[:, 1])
                    if half:
                        add(ada_s[:, j], ada_s[:, j], w[:, 0])
                    if j < 5:
                        ada_load(j + 1, half)

                pool.wait_ge(g_pe, heads(PE_STEPS, h))
                pool.wait_ge(g_dve, step(DVE_STEPS, "lower", h))
                for n in range(LEVELS):
                    if n >= 2:
                        pool.wait_ge(g_pe, step(PE_STEPS, f"y{n - 2}", h))
                    nc.gpsimd.tensor_tensor(chunks(low_part[n % 2][:]), chunks(gd["low"][:]), every(masks[:, n]), MULT)\
                      .then_inc(g_pool, 1)
                    if n >= 1:
                        modulation((n - 1) // 2, (n - 1) % 2)
                for n in range(LEVELS - 1, 12):
                    modulation(n // 2, n % 2)
                pool.sem_inc(g_pool, 1)
                pool.wait_ge(g_dve, step(DVE_STEPS, "o_mean", h))
                nc.gpsimd.tensor_tensor(col4(S_ON), col4(S_OMS), minus_half, ALU.pow).then_inc(g_pool, 1)

            pool.wait_ge(ab_dve, AB_LINKS)
            pool.sem_inc(g_pool, 1)
            pool.sem_inc(ada_own, 1)
            with pool.Fori(0, H - 1) as h:
                head(h)
            head(H - 1)
            pool.wait_ge(mixed, KD)
            pool.wait_ge(mix_lo, KD)
            sum_in_loop(WO)
            factor(N_FFN)
            sum_in_loop(DOWN[0])
            factor(N_OUT1)
            factor(N_POOL)
            factor(N_FFN0)
            sum_in_loop(DOWN[1])
            factor(N_ATT)

            def att_head(h):
                pool.wait_ge(t_dve, step(ATT_DVE, "mean", h))
                nc.gpsimd.tensor_tensor(col4(S_ON), col4(S_OMS), minus_half, ALU.pow).then_inc(t_pool, 1)

            def add_projection(stage, i, h):
                for m in range(KD):
                    b, before = stage.out(m, i)
                    pool.wait_ge(out_used[b], before + 1)
                    nc.gpsimd.tensor_tensor(x[:, m], x[:, m], wo_s[:, m % 4], ADD).then_inc(wo_add, 1)

            pool.sem_inc(wo_add, 4)
            att_head(0)
            with pool.Fori(0, H - 2) as i:
                add_projection(ATT_H, i, i)
                att_head(i + 1)
            add_projection(ATT_7, 0, H - 2)
            att_head(H - 1)
            factor(N_FFN1)
            sum_in_loop(DOWN[2])
            factor(N_OUT2)

        @block.scalar
        def _(act):
            def split(tile):
                if isinstance(tile.before, int) and tile.before >= N_TILES:
                    return
                act.wait_ge(w_landed[tile.raw], 16 * tile.loads + 16)
                if tile.n0 >= RING:
                    act.wait_ge(tile_done, tile.before - 3)
                nc.scalar.activation(w_hi[:, tile.slot], raw[:, tile.raw], ACT.Copy).then_inc(hi_ready, 1)

            def next_tile(stage, t, i):
                tile = stage.tile(t, i)
                split(tile.ahead())
                act.wait_ge(tile_done, tile.before + 1)
                return stage.out(t, i)

            def normed(r, scale, shift=None):
                base = scaled_base(r)
                for m in range(KD):
                    act.wait_ge(n_t, base + m + 1)
                    dst = x[:, m] if r == N_OUT1 else tmp[:, 2 + m % 2]
                    if m >= 2 and r in SPLIT_NORMS:
                        act.wait_ge(h_ready, split_base(r) + m - 1)
                    if m >= 2 and r == N_OUT2:
                        act.wait_ge(fin_pe, m - 1)
                    if shift is None:
                        nc.scalar.activation(dst, tmp[:, m % 2], ACT.Copy, scale=scale(m)).then_inc(n_ht, 1)
                    else:
                        nc.scalar.activation(dst, tmp[:, m % 2], ACT.Identity, bias=shift(m), scale=scale(m))\
                          .then_inc(n_ht, 1)
                    if r in SPLIT_NORMS:
                        act.wait_ge(n_ht, base + m + 1)
                        nc.scalar.activation(h_hi[:, m], dst, ACT.Copy).then_inc(n_hi, 1)
                    if r == N_OUT2 and m:
                        output(m - 1)
                    if r == N_OUT1 and m:
                        act.wait_ge(n_ht, base + m)
                        square(N_POOL, m - 1)
                if r == N_OUT2:
                    output(KD - 1)
                if r == N_OUT1:
                    act.wait_ge(n_ht, base + KD)
                    square(N_POOL, KD - 1)

            def square(r, m):
                base = (KD - 1) * PSUM_SUMS.index(r)
                if m >= 4:
                    act.wait_ge(fsq_pe, base + m - 3)
                nc.scalar.activation(tmp[:, 2 + m % 4], x[:, m], ACT.Square).then_inc(fsq_act, 1)

            def output(m):
                act.wait_ge(fin_pe, m + 1)
                nc.scalar.activation(o_tok[:, :, P * m:P * m + P], chunks(bank(4 + m % 2)), ACT.Copy).then_inc(fin_act, 1)

            act.dma_start(cst[:], a["const_tile"]).then_inc(cst_in, 16)
            act.dma_start(masks[:], a["const_masks"]).then_inc(cst_in, 16)

            def by_tile(v):
                return v.rearrange("(r p) -> r p", p=P)

            def by_row_tile(v):
                return v.rearrange("j (r p) -> (j r) p", p=P)

            for first, src in ((V_BADA, by_tile(a["b_ada"][0])), (V_BADAF, by_tile(a["b_ada_f"])),
                               (V_N1, by_tile(a["norm1_w"][0])), (V_N2, by_tile(a["norm2_w"][0])),
                               (V_NF, by_tile(a["normf_w"])), (V_C, by_tile(a["c"][0])),
                               (V_MIX, by_row_tile(a["mix_norm_2"])), (V_PSC, by_tile(a["pool_scale_2"][0])),
                               (V_FIN, by_tile(a["final_norm_2"])), (V_CONV, by_row_tile(a["gdn_conv_w"][0])),
                               (V_SCONV, by_row_tile(a["sc_conv_w"][0])), (V_GNW, a["gdn_norm_w"]),
                               (V_SUB, a["diff_subln_2"]), (V_FCW[0], by_row_tile(a["ffn_conv_w_2"][0])),
                               (V_FCB, by_row_tile(a["ffn_conv_b_2"])), (V_FFN, by_row_tile(a["ffn_norm_2"])),
                               (V_FCW[1], by_row_tile(a["ffn_conv_w_2"][1]))):
                act.dma_start(pack[first % P:first % P + src.shape[0], first // P, :], src).then_inc(pack_in, 16)
            act.wait_ge(pro_dve, 2)
            act.dma_start(small[0:H, S_DT:S_DT + 1], a["gdn_dt_bias"][0].rearrange("(p o) -> p o", o=1)).then_inc(ab_in, 16)
            act.dma_start(alog[:], a["gdn_a_log"].to_broadcast([P, H])).then_inc(ab_in, 16)
            for m in range(1, KD, 2):
                act.wait_ge(pro_pe, m + 1)
                nc.scalar.activation(x[:, m], bank(m), ACT.Copy).then_inc(x_odd, 1)
            act.wait_ge(pro_dve, 3)
            nc.scalar.activation(cact[:, 0], vec[:, V_C:V_C + KD], ACT.Tanh, scale=0.5).then_inc(pro_act, 1)
            split(Tile(0))
            split(Tile(1))
            act.wait_ge(mod_ready, 1)
            normed(N_MIX, lambda m: col(wsc[:, 0], m), lambda m: col(mod, SH1 + m))
            split(Tile(2))
            split(Tile(3))

            split(AB.tile(0, 0).ahead())
            act.wait_ge(ab_dve, 1)
            nc.scalar.activation(ab[1][:], ab[0][:], ACT.Abs).then_inc(ab_act, 1)
            act.wait_ge(ab_act, 1)
            nc.scalar.activation(ab[1][:], ab[1][:], ACT.Exp, scale=-1.0).then_inc(ab_act, 1)
            act.wait_ge(ab_in, 32)
            nc.scalar.activation(alog[:], alog[:], ACT.Exp).then_inc(ab_act, 1)

            def conv_tap(stage, t, i, n, hh):
                b, before = stage.out(t, i)
                act.wait_ge(tile_done, stage.tile(t, i).before + 1)
                nc.scalar.activation(conv_bufs[n][:], bank(b), ACT.Copy, scale=col(vec, hh + (V_CONV + 72 + 8 * n)))\
                  .then_inc(cv_act, 1)

            def conv_tanh(stage, t, i, n, hh):
                b, before = stage.out(t, i)
                act.wait_ge(out_used[b], before + 1)
                if not (isinstance(hh, int) and hh == 0 and n == 0):
                    act.wait_ge(cv_dve, 10 * hh + 3 * n)
                nc.scalar.activation(gd["th"][:], conv_bufs[n][:], ACT.Tanh, scale=0.5).then_inc(cv_act, 1)

            def z_tile(stage, t, i, hh):
                b, before = stage.out(t, i)
                act.wait_ge(tile_done, stage.tile(t, i).before + 1)
                nc.scalar.activation(gd["z_g"][:], bank(b), ACT.Copy, scale=small[:, S_GNW:S_GNW + 1]).then_inc(cv_act, 1)
                act.wait_ge(cv_dve, 10 * hh + 9)
                nc.scalar.activation(gd["th"][:], bank(b), ACT.Tanh, scale=0.5).then_inc(out_used[b], 1)

            conv_bufs = [gd[n] for n in ("q_s", "k_s", "v_s")]
            act.wait_ge(ab_dve, AB_LINKS)
            act.sem_inc(g_act, 1)
            for n in range(3):
                split(QKVZ.tile(n, 0).ahead())
                conv_tap(QKVZ, n, 0, n, 0)
                conv_tanh(QKVZ, n, 0, n, 0)
            split(QKVZ.tile(3, 0).ahead())
            z_tile(QKVZ, 3, 0, 0)

            def head(stage, i, h):
                more = stage is HEAD

                def ahead(t):
                    split(stage.tile(t, i).ahead())

                def after_pe(name):
                    act.wait_ge(g_pe, step(PE_STEPS, name, h))

                def after_dve(name):
                    act.wait_ge(g_dve, step(DVE_STEPS, name, h))

                after_pe("kv_tokens")
                for n in range(NC):
                    k_sq = nc.scalar.activation(part(gd["y_t"], n), part(bank(2), n), ACT.Square,
                                                accum_out=small[:, S_KSQ + n:S_KSQ + n + 1])
                k_sq.then_inc(g_act, 1)
                after_dve("decay_arg")
                nc.scalar.activation(gd["dec"][:], gd["dec"][:], ACT.Exp).then_inc(g_act, 1)
                nc.scalar.activation(col4(S_EG), head_cols(g_tok, h), ACT.Exp).then_inc(g_act, 1)
                after_dve("g_left")
                nc.scalar.activation(gd["y_t"][:], bank(4), ACT.Exp).then_inc(g_act, 1)
                nc.scalar.activation(col4(S_ELAST), chunks(bank(4))[:, :, P - 1], ACT.Exp).then_inc(g_act, 1)
                nc.scalar.activation(col4(S_ELEFT), col4(S_LEFT), ACT.Exp).then_inc(g_act, 1)
                nc.scalar.activation(gd["q_sq"][:], gd["q_s"][:], ACT.Square, scale=P * 1e-3).then_inc(g_act, 1)
                ahead(0)
                b, before = stage.out(0, i)
                act.wait_ge(tile_done, stage.tile(0, i).before + 1)
                nc.scalar.activation(gd["cc"][:], bank(b), ACT.Copy).then_inc(out_used[b], 1)
                after_pe("x_pairs")
                nc.scalar.activation(gd["x_t"][:], bank(4), ACT.Copy).then_inc(g_act, 1)
                for n in range(LEVELS):
                    after_pe(f"u{n}")
                    nc.scalar.activation(gd["u_t"][:], bank(6), ACT.Copy).then_inc(g_act, 1)
                    if more and n == 0:
                        after_pe("kk_qk")
                        after_dve("q_g")
                        conv_tap(stage, 1, i, 0, h + 1)
                        ahead(1)
                    if more and n == 1:
                        conv_tanh(stage, 1, i, 0, h + 1)
                        conv_tap(stage, 2, i, 1, h + 1)
                        ahead(2)
                    if more and n == 2:
                        conv_tanh(stage, 2, i, 1, h + 1)
                    if more and n == 3:
                        conv_tap(stage, 3, i, 2, h + 1)
                        ahead(3)
                    if more and n == 4:
                        conv_tanh(stage, 3, i, 2, h + 1)
                        ahead(4)
                    if not more and n == 1:
                        ahead(1)
                after_pe("w")
                nc.scalar.activation(gd["x_t"][:], bank(7), ACT.Copy).then_inc(g_act, 1)
                ahead(5 if more else 2)
                after_pe(f"o{NC - 1}")
                nc.scalar.activation(gd["dec"][:], bank(3), ACT.Square).then_inc(g_act, 1)
                if more:
                    ahead(6)
                    b, before = stage.out(6, i)
                    act.wait_ge(tile_done, stage.tile(6, i).before + 1)
                    nc.scalar.activation(dyn(ga_t, h), bank(b), ACT.Tanh, scale=0.5).then_inc(out_used[b], 1)
                after_dve("o_scale")
                nc.scalar.activation(dyn(og_hi, h), gd["low_d"][:], ACT.Copy).then_inc(g_act, 1)
                if more:
                    ahead(7)
                    after_dve("o_gate")
                    act.wait_ge(sc_dve, 3 * h + 3)
                    z_tile(stage, 7, i, h + 1)
                else:
                    b, before = next_tile(stage, 3, i)
                    nc.scalar.activation(dyn(ga_t, h), bank(b), ACT.Tanh, scale=0.5).then_inc(out_used[b], 1)

            with act.Fori(0, H - 1) as h:
                head(HEAD, h, h)
            head(LAST, 0, H - 1)

            act.wait_ge(out_used[LAST.out(2, 0)[0]], LAST.out(2, 0)[1] + 1)
            act.wait_ge(g_dve, heads(DVE_STEPS, H))
            nc.scalar.activation(sc_hi[:], sc_out[:], ACT.Copy).then_inc(sc_split, 1)
            with act.Fori(0, 2) as i:
                for t in range(4):
                    b, before = next_tile(GATE, t, i)
                    nc.scalar.activation(gb_t[:, t], bank(b), ACT.Tanh, scale=0.5).then_inc(out_used[b], 1)
                for t in range(4, 12):
                    split(GATE.tile(t, i).ahead())
            act.wait_ge(tile_done, GATE.tile0 + 16)
            for m in range(KD):
                act.wait_ge(mixed, m + 1)
                nc.scalar.activation(h_hi[:, m], ga_t[:, m], ACT.Copy).then_inc(mix_hi, 1)
            with act.Fori(0, 2) as i:
                for t in range(4):
                    split(WO.tile(t, i).ahead())

            def feed_forward(f):
                base = 0 if f == 0 else 2 * UPS + 4 * UPS * (f - 1)
                with act.Fori(0, UPS) as i:
                    for j in range(2):
                        b, before = next_tile(UP[f], 2 * j, i)
                        if f == 0:
                            nc.scalar.activation(tmp[:, j], bank(b), ACT.Tanh, scale=0.5).then_inc(f_act, 1)
                        else:
                            nc.scalar.activation(tmp[:, 2 + j], bank(b), ACT.Identity,
                                                 bias=col(vec, 2 * i + (V_FCB + KF * (f - 1) + j)),
                                                 scale=col(vec, 2 * i + (V_FCW[f - 1] + KF + j))).then_inc(f_act, 1)
                            act.wait_ge(out_used[b], before + 1)
                            nc.scalar.activation(tmp[:, j], tmp[:, 2 + j], ACT.Gelu).then_inc(f_act, 1)
                        split(UP[f].tile(2 * j + 1, i).ahead())
                        b, before = UP[f].out(2 * j + 1, i)
                        act.wait_ge(out_used[b], before + 1)
                        nc.scalar.activation(dyn(act_hi, 2 * i + j), tmp[:, 4 + j], ACT.Copy).then_inc(f_hi, 1)
                if f == 2:
                    for n in range(24):
                        split(DOWN[f].tile(n % 12, n // 12).ahead())
                else:
                    with act.Fori(0, 2) as i:
                        for t in range(12):
                            split(DOWN[f].tile(t, i).ahead())

            act.wait_ge(mod_ready, 2)
            normed(N_FFN, lambda m: col(wsc[:, 1], m), lambda m: col(mod, SH2 + m))
            feed_forward(0)
            normed(N_OUT1, lambda m: col(wsc[:, 2], m), lambda m: col(mod, SHF + m))

            for m in range(KD):
                act.wait_ge(pl_dve, POOL_STEP[m])
                if m >= 2:
                    act.wait_ge(pl_lo, m - 1)
                nc.scalar.activation(tmp[:, 2 + m % 2], pool_d[:, m % 2], ACT.Copy, scale=col(vec, V_MIX + m))\
                  .then_inc(pl_act, 1)
                act.wait_ge(pl_act, m + 1)
                nc.scalar.activation(p_hi[:, m], tmp[:, 2 + m % 2], ACT.Copy).then_inc(pl_hi, 1)
            for m in range(KD):
                b, before = POOLW.out(m, 0)
                act.wait_ge(out_used[b], before + 1)
                square(N_FFN0, m)
                if m % 4 == 3:
                    split(POOLW.tile(m // 4, 0).ahead())
            normed(N_FFN0, lambda m: col(vec, V_FFN + m))
            feed_forward(1)

            normed(N_ATT, lambda m: col(vec, V_MIX + KD + m))
            act.wait_ge(rp_dve, 8)
            nc.scalar.activation(at["sin"][:], at["ang"][:], ACT.Sin).then_inc(rp_act, 1)
            nc.scalar.activation(at["rnd"][:], at["ang"][:], ACT.Abs).then_inc(rp_act, 1)
            act.wait_ge(rp_act, 2)
            nc.scalar.activation(at["cos"][:], at["rnd"][:], ACT.Sin, bias=small[:, S_PI2:S_PI2 + 1], scale=-1.0)\
              .then_inc(rp_act, 1)
            act.wait_ge(rp_dve, 11)
            nc.scalar.activation(small[0:1, S_NEG:S_NEG + 2], small[0:1, S_MAX:S_MAX + 2], ACT.Exp).then_inc(rp_act, 1)

            def rope_tile(stage, t, j, i, n, name):
                tile = stage.tile(t, i)
                split(tile.ahead())
                act.wait_ge(tile_done, tile.before + 1)
                b, before = stage.out(j, i)
                act.wait_ge(rp_dve, roped(n))
                for q in range(4):
                    swapped = nc.scalar.activation(at["swap"][32 * q:32 * q + 32], ps[32 * (q ^ 1):32 * (q ^ 1) + 32, b, :],
                                                   ACT.Copy)
                swapped.then_inc(rp_act, 1)
                act.wait_ge(rp_dve, roped(n) + 2)
                nc.scalar.activation(at[name][:], at["rot"][:], ACT.Copy).then_inc(rp_act, 1)

            def v_tile(stage, t, j, i):
                tile = stage.tile(t, i)
                split(tile.ahead())
                act.wait_ge(tile_done, tile.before + 1)
                b, before = stage.out(j, i)
                nc.scalar.activation(at["v_f"][:], bank(b), ACT.Copy).then_inc(out_used[b], 1)

            def projection(stage, i, h, m):
                b, before = stage.out(m, i)
                tile = stage.tile(0, i)
                if m < KD - 1:
                    act.wait_ge(wo_out, (KD - 1) * h + m + 1)
                else:
                    split(tile.ahead())
                    act.wait_ge(tile_done, tile.before + 1)
                act.wait_ge(wo_add, KD * h + m + 1)
                nc.scalar.activation(wo_s[:, m % 4], bank(b), ACT.Copy).then_inc(out_used[b], 1)

            def att_head(stage, i, h, wo, nxt):
                t0, j0 = (1, KD) if wo else (0, 0)
                for q in range(NC):
                    act.wait_ge(t_dve, step(ATT_DVE, f"neg{q}", h))
                    if q >= 2:
                        act.wait_ge(t_dve, step(ATT_DVE, f"a{q - 2}", h))
                    for c in range(2):
                        s = 2 * (q % 2) + c
                        e = nc.scalar.activation(prob[:, q % 2, c], bank(2 + s), ACT.Exp, bias=small[:, S_NEG + s:S_NEG + s + 1],
                                                 scale=0.125, accum_out=small[:, S_SUM + s:S_SUM + s + 1])
                    e.then_inc(t_act, 1)
                    if wo:
                        projection(stage, i, h - 1, 2 * q)
                        projection(stage, i, h - 1, 2 * q + 1)
                for q in range(NC):
                    act.wait_ge(t_pe, step(ATT_PE, f"turn{q}", h))
                    nc.scalar.activation(at_hi[:, :, P * q:P * q + P], chunks(bank(6 + q % 2)), ACT.Copy).then_inc(t_act, 1)
                if nxt:
                    rope_tile(stage, t0, j0, i, 2 * h + 2, "k_hi")
                act.wait_ge(t_pe, step(ATT_PE, "pv", h))
                nc.scalar.activation(at["o_s"][:], bank(7), ACT.Copy, scale=small[:, S_SUB:S_SUB + 1]).then_inc(t_act, 1)
                nc.scalar.activation(at["o_sq"][:], bank(7), ACT.Square).then_inc(t_act, 1)
                if nxt:
                    rope_tile(stage, t0 + 1, j0 + 1, i, 2 * h + 3, "q_hi")
                act.wait_ge(t_dve, step(ATT_DVE, "scale", h))
                nc.scalar.activation(at["ao_hi"][:], at["o_n"][:], ACT.Copy).then_inc(t_act, 1)
                if nxt:
                    v_tile(stage, t0 + 2, j0 + 2, i)
                    act.wait_ge(t_pe, step(ATT_PE, "v_next", h))
                    nc.scalar.activation(at["v_hi"][:], bank(6), ACT.Copy).then_inc(t_act, 1)

            rope_tile(ATT_Q, 0, 0, 0, 0, "k_hi")
            rope_tile(ATT_Q, 1, 1, 0, 1, "q_hi")
            v_tile(ATT_Q, 2, 2, 0)
            act.wait_ge(t_pe, 1)
            nc.scalar.activation(at["v_hi"][:], bank(6), ACT.Copy).then_inc(t_act, 1)
            att_head(ATT_0, 0, 0, False, True)
            with act.Fori(0, H - 2) as i:
                att_head(ATT_H, i, i + 1, True, True)
            att_head(ATT_7, 0, H - 1, True, False)
            for m in range(KD):
                b, before = ATT_WO.out(m, 0)
                act.wait_ge(out_used[b], before + 1)
                square(N_FFN1, m)
            split(ATT_WO.tile(0, 0).ahead())
            normed(N_FFN1, lambda m: col(vec, V_FFN + KD + m))
            feed_forward(2)
            normed(N_OUT2, lambda m: col(vec, V_FIN + m))

        @block.vector
        def _(dve):
            def split(tile):
                if isinstance(tile.before, int) and tile.before >= N_TILES:
                    return
                dve.wait_ge(hi_ready, tile.before + 1)
                nc.vector.tensor_tensor(w_lo[:, tile.slot], raw[:, tile.raw], w_hi[:, tile.slot].bitcast(F32), SUB)\
                  .then_inc(lo_ready, 1)

            def next_tile(stage, t, i):
                tile = stage.tile(t, i)
                split(tile.ahead())
                dve.wait_ge(tile_done, tile.before + 1)
                return stage.out(t, i)

            def mean_squares(r):
                dve.wait_ge(n_pe, 2 * r + 1)
                nc.vector.tensor_scalar(col4(S_MS), bank(2)[:, 0:NC], 1.0 / D, EPS, MULT, ADD).then_inc(n_dve, 1)

            def token_factor(r):
                if r != N_MIX:
                    mean_squares(r)
                dve.wait_ge(n_pe, 2 * r + 2)

            def lo_part(r, m):
                dve.wait_ge(n_hi, split_base(r) + m + 1)
                nc.vector.tensor_tensor(h_lo[:, m], tmp[:, 2 + m % 2], h_hi[:, m].bitcast(F32), SUB).then_inc(h_ready, 1)

            def normed(r):
                token_factor(r)
                for m in range(KD):
                    if m >= 2:
                        dve.wait_ge(n_ht, scaled_base(r) + m - 1)
                    nc.vector.tensor_tensor(tmp[:, m % 2], x[:, m], bank(3), MULT).then_inc(n_t, 1)
                    if r in SPLIT_NORMS and m:
                        lo_part(r, m - 1)
                if r in SPLIT_NORMS:
                    lo_part(r, KD - 1)

            nc.vector.memset(raw[:], 0.0).then_inc(pro_dve, 1)
            nc.vector.memset(small[:], 0.0).then_inc(pro_dve, 1)
            for m in range(0, KD, 2):
                dve.wait_ge(pro_pe, m + 1)
                nc.vector.tensor_copy(x[:, m], bank(m)).then_inc(x_even, 1)
            dve.wait_ge(pro_pe, 9)
            for n, rows_in in enumerate(PACK_ROWS):
                copied = nc.vector.tensor_copy(vec[:, P * n:P * n + rows_in], bank(0)[:, P * n:P * n + rows_in])
            copied.then_inc(pro_dve, 1)
            dve.wait_ge(pro_dve, 3)
            dve.wait_ge(pro_pool, 1)
            nc.vector.tensor_scalar(small[:, S_GNW:S_GNW + 1], vec[:, V_GNW:V_GNW + 1], 0.5, None, MULT)
            nc.vector.tensor_scalar(small[:, S_SUB:S_SUB + 1], vec[:, V_SUB:V_SUB + 1], 1.0 - LAM_INIT, None, MULT)
            nc.vector.memset(small[:, S_PI2:S_PI2 + 1], float(np.pi / 2))
            dve.wait_ge(pro_act, 1)
            nc.vector.scalar_tensor_tensor(cact[:, 1], cact[:, 0], 1.0, vec[:, V_C:V_C + KD], ADD, MULT).then_inc(pro_dve, 1)
            dve.wait_ge(pro_dve, 4)
            nc.vector.tensor_scalar(cact[:, 1], cact[:, 1], 0.5, None, MULT).then_inc(pro_dve, 1)
            dve.wait_ge(pro_dve, 5)
            for turn, n in enumerate((0, 2, 3)):
                dve.wait_ge(ada_in[n], 16)
                total = ada0_sum[:, T * n:T * n + T]
                for k in range(KD):
                    src = ada0[:, k, T * n:T * n + T]
                    if k == 0:
                        nc.vector.tensor_scalar(total, src, cact[:, 1, k:k + 1], None, MULT).then_inc(ada0_own, 1)
                    else:
                        dve.wait_ge(ada0_own, KD * turn + k)
                        nc.vector.scalar_tensor_tensor(total, src, cact[:, 1, k:k + 1], total, MULT, ADD).then_inc(ada0_own, 1)
                if turn == 1:
                    mean_squares(N_MIX)
            split(Tile(0))
            split(Tile(1))
            dve.wait_ge(pro_pe, 10)
            nc.vector.tensor_tensor(mod[:, 0:16], bank(1)[:, 0:16], vec[:, V_BADA:V_BADA + 16], ADD).then_inc(pro_dve, 1)
            dve.wait_ge(pro_dve, 6)
            nc.vector.scalar_tensor_tensor(wsc[:, 0], mod[:, SC1:SC1 + KD], 1.0, vec[:, V_N1:V_N1 + KD], ADD, MULT)\
              .then_inc(mod_ready, 1)
            normed(N_MIX)
            split(Tile(2))
            split(Tile(3))

            dve.wait_ge(ab_in, 32)
            b, before = next_tile(AB, 0, 0)
            nc.vector.tensor_scalar(ab_f[0:2 * H], bank(b)[0:2 * H], small[0:2 * H, S_DT:S_DT + 1], None, ADD)\
              .then_inc(out_used[b], 1)
            v, e, s2, s3, s4, s5, s6 = [buf[:] for buf in ab]
            links = [0]

            def link(ins):
                ins.then_inc(ab_dve, 1)
                links[0] += 1
                dve.wait_ge(ab_dve, links[0])

            dve.wait_ge(ab_pe, 1)
            link(nc.vector.tensor_copy(v, bank(2)[:, 0:2 * H * NC].rearrange("p (n c) -> p n c", n=NC)))
            dve.wait_ge(ab_act, 2)
            link(nc.vector.tensor_scalar(s2, e, 2.0, None, ADD))
            link(nc.vector.reciprocal(s3, s2))
            link(nc.vector.tensor_tensor(s3, s3, e, MULT))
            link(nc.vector.tensor_tensor(s4, s3, s3, MULT))
            link(nc.vector.tensor_scalar(s5, s4, 1.0 / 15, None, MULT))
            for c in (13, 11, 9, 7, 5, 3):
                link(nc.vector.scalar_tensor_tensor(s5, s5, 1.0 / c, s4, ADD, MULT))
            link(nc.vector.scalar_tensor_tensor(s5, s5, 1.0, s3, ADD, MULT))
            link(nc.vector.tensor_scalar(s2, v, 0.0, None, ALU.max))
            link(nc.vector.scalar_tensor_tensor(s5, s5, 2.0, s2, MULT, ADD))
            dve.wait_ge(ab_act, 3)
            link(nc.vector.tensor_scalar(alog[:], alog[:], -1.0, None, MULT))
            link(nc.vector.tensor_tensor(s6.rearrange("p n (two h) -> p n two h", two=2), s5.rearrange("p n (two h) -> p n two h", two=2),
                                        alog[:].unsqueeze(1).unsqueeze(1).to_broadcast([P, NC, 2, H]), MULT))
            link(nc.vector.tensor_scalar(s2, e, 1.0, None, ADD))
            link(nc.vector.reciprocal(s4, s2))
            link(nc.vector.tensor_scalar(s3, v, 0.0, None, ALU.is_ge))
            link(nc.vector.tensor_scalar(s2, e, -1.0, 1.0, MULT, ADD))
            link(nc.vector.tensor_tensor(s3, s3, s2, MULT))
            link(nc.vector.tensor_tensor(s3, s3, e, ADD))
            link(nc.vector.tensor_tensor(b_tok[:], s3, s4, MULT))
            link(nc.vector.tensor_scalar(bh_tok[:], b_tok[:], 0.5, None, MULT))
            dve.wait_ge(ab_pe, 2)
            link(nc.vector.tensor_copy(g_tok[:], bank(3)[:, 0:2 * H * NC].rearrange("p (n c) -> p n c", n=NC)))
            assert links[0] == AB_LINKS
            dve.sem_inc(g_dve, 1)

            def conv_taps(stage, t, i, n, hh):
                b, before = stage.out(t, i)
                buf = conv_bufs[n]
                dve.wait_ge(cv_act, 7 * hh + 2 * n + 1)
                for d in (1, 2, 3):
                    if d > 1:
                        dve.wait_ge(cv_dve, 10 * hh + 3 * n + d - 1)
                    nc.vector.scalar_tensor_tensor(buf[:, d:T], bank(b)[:, 0:T - d],
                                                   col(vec, hh + (V_CONV + 24 * (3 - d) + 8 * n)), buf[:, d:T], MULT, ADD)\
                      .then_inc(*((cv_dve, 1) if d < 3 else (out_used[b], 1)))

            def conv_silu(n, hh):
                dve.wait_ge(cv_act, 7 * hh + 2 * n + 2)
                nc.vector.scalar_tensor_tensor(conv_bufs[n][:], gd["th"][:], 1.0, conv_bufs[n][:], ADD, MULT).then_inc(cv_dve, 1)

            def z_silu(stage, t, i, hh):
                b, before = stage.out(t, i)
                dve.wait_ge(cv_act, 7 * hh + 7)
                dve.wait_ge(out_used[b], before + 1)
                nc.vector.scalar_tensor_tensor(gd["z_g"][:], gd["th"][:], 1.0, gd["z_g"][:], ADD, MULT).then_inc(cv_dve, 1)

            conv_bufs = [gd[n] for n in ("q_s", "k_s", "v_s")]
            for n in range(3):
                split(QKVZ.tile(n, 0).ahead())
                conv_taps(QKVZ, n, 0, n, 0)
                conv_silu(n, 0)
            split(QKVZ.tile(3, 0).ahead())
            z_silu(QKVZ, 3, 0, 0)

            def head(stage, i, h):
                more = stage is HEAD
                scx, scb = (4, 5) if more else (1, 2)

                def ahead(t):
                    split(stage.tile(t, i).ahead())

                def short_conv():
                    b0, before0 = stage.out(0, i)
                    b, before = stage.out(scx, i)
                    dve.wait_ge(cv_dve, 10 * h + (19 if more else 10))
                    dve.wait_ge(out_used[b0], before0 + 1)
                    dve.wait_ge(tile_done, stage.tile(scx, i).before + 1)
                    nc.vector.tensor_tensor(gd["cx"][:], gd["cc"][:], bank(b), MULT).then_inc(out_used[b], 1)
                    dve.wait_ge(out_used[b], before + 1)
                    nc.vector.tensor_scalar(gd["cc"][:], gd["cx"][:], col(vec, h + (V_SCONV + 16)), None, MULT)\
                      .then_inc(sc_dve, 1)
                    for d in (1, 2):
                        dve.wait_ge(sc_dve, 3 * h + d)
                        nc.vector.scalar_tensor_tensor(gd["cc"][:, d:T], gd["cx"][:, 0:T - d],
                                                       col(vec, h + (V_SCONV + 8 * (2 - d))), gd["cc"][:, d:T],
                                                       MULT, ADD).then_inc(sc_dve, 1)

                def short_gate():
                    b, before = stage.out(scb, i)
                    dve.wait_ge(tile_done, stage.tile(scb, i).before + 1)
                    dve.wait_ge(sc_dve, 3 * h + 3)
                    nc.vector.tensor_tensor(dyn(sc_out, h), gd["cc"][:], bank(b), MULT).then_inc(out_used[b], 1)

                def after_pe(name):
                    dve.wait_ge(g_pe, step(PE_STEPS, name, h))

                def after_act(name):
                    dve.wait_ge(g_act, step(ACT_STEPS, name, h))

                def own(name):
                    dve.wait_ge(g_dve, step(DVE_STEPS, name, h))

                g_col = head_cols(g_tok, h)
                nc.vector.tensor_copy(col4(S_G), g_col).then_inc(g_dve, 1)
                after_act("k_squares")
                nc.vector.tensor_scalar(col4(S_KSS), col4(S_KSQ), 4 * EPS, None, ADD).then_inc(g_dve, 1)
                after_pe("g_rows")
                for n in range(NC):
                    arg = nc.vector.scalar_tensor_tensor(part(gd["dec"], n), part(bank(4), n), col(g_tok[:, n], h),
                                                         cst[:, C_LOW:C_LOW + P], SUB, ALU.min)
                arg.then_inc(g_dve, 1)
                nc.vector.tensor_tensor(col4(S_LEFT), chunks(bank(4))[:, :, P - 1], g_col, SUB).then_inc(g_dve, 1)
                dve.wait_ge(g_pool, step(POOL_STEPS, "k_norm", h))
                nc.vector.scalar_tensor_tensor(col4(S_KB), col4(S_KN), -1.0, head_cols(b_tok, h + H), MULT, MULT)\
                  .then_inc(g_dve, 1)
                after_act("exp_decay")
                after_pe("kb_rows")
                nc.vector.tensor_tensor(gd["low_d"][:], gd["dec"][:], bank(7), MULT).then_inc(g_dve, 1)
                own("kb_decay")
                for n in range(NC):
                    low = nc.vector.scalar_tensor_tensor(part(gd["low"], n), part(bank(5), n), small[:, S_KN + n:S_KN + n + 1],
                                                         part(gd["low_d"], n), MULT, MULT)
                low.then_inc(g_dve, 1)
                own("lower")
                nc.vector.tensor_tensor(chunks(gd["u_t"][:]), chunks(gd["low"][:]), every(cst[:, C_L1:C_L1 + P]), MULT)\
                  .then_inc(g_dve, 1)
                own("u_pairs")
                nc.vector.tensor_tensor(chunks(gd["u_t"][:]), chunks(gd["u_t"][:]), every(ident), ADD).then_inc(g_dve, 1)
                after_act("exp_g_rows")
                nc.vector.tensor_tensor(gd["q_g"][:], gd["q_s"][:], gd["y_t"][:], MULT).then_inc(g_dve, 1)
                for n in range(NC):
                    qk = nc.vector.scalar_tensor_tensor(part(gd["qk_t"], n), part(bank(6), n), small[:, S_KN + n:S_KN + n + 1],
                                                        part(gd["dec"], n), MULT, MULT)
                qk.then_inc(g_dve, 1)
                ahead(0)
                for n in range(LEVELS):
                    after_pe(f"y{n}")
                    if n == 0:
                        own("q_g")
                    nc.vector.tensor_tensor(chunks(gd["y_t"][:]), chunks(bank(4)), every(ident), ADD).then_inc(g_dve, 1)
                    if n == 0:
                        after_act("exp_g")
                        nc.vector.tensor_tensor(col4(S_KBEG), col4(S_KB), col4(S_EG), MULT).then_inc(g_dve, 1)
                        nc.vector.tensor_tensor(chunks(gd["v_b"][:]), chunks(bank(3)), spread(head_cols(bh_tok, h + H)), MULT)\
                          .then_inc(g_dve, 1)
                        own("kbeg_scale")
                        nc.vector.tensor_tensor(chunks(gd["k_beg"][:]), chunks(bank(2)), spread(col4(S_KBEG)), MULT)\
                          .then_inc(g_dve, 1)
                    if more and n == 1:
                        conv_taps(stage, 1, i, 0, h + 1)
                    if more and n == 2:
                        conv_silu(0, h + 1)
                    if more and n == 3:
                        ahead(2)
                    if more and n == 4:
                        conv_taps(stage, 3, i, 2, h + 1)
                    if not more and n == 2:
                        ahead(1)
                    if n == LEVELS - 1:
                        break
                    after_pe(f"x{n}")
                    nc.vector.tensor_copy(gd["x_t"][:], bank(5)).then_inc(g_dve, 1)
                    if n == 0:
                        after_act("exp_left")
                        nc.vector.tensor_tensor(col4(S_KDEC), col4(S_KN), col4(S_ELEFT), MULT).then_inc(g_dve, 1)
                        own("kdec_scale")
                        nc.vector.tensor_tensor(chunks(gd["k_dec"][:]), chunks(bank(2)), spread(col4(S_KDEC)), MULT)\
                          .then_inc(g_dve, 1)
                    if more and n == 1:
                        ahead(1)
                    if more and n == 2:
                        conv_taps(stage, 2, i, 1, h + 1)
                    if more and n == 3:
                        conv_silu(1, h + 1)
                    if more and n == 4:
                        ahead(3)
                    if not more and n == 1:
                        short_conv()
                if more:
                    conv_silu(2, h + 1)
                    short_conv()
                    ahead(4)
                else:
                    short_gate()
                for n in range(NC):
                    after_pe(f"v_new{n}")
                    nc.vector.tensor_copy(part(gd["y_t"], n), part(bank(2), n)).then_inc(g_dve, 1)
                    if n < NC - 1:
                        after_pe(f"o{n}")
                        if n == 0:
                            nc.vector.tensor_copy(state[:], part(bank(4), 0)).then_inc(g_dve, 1)
                        else:
                            nc.vector.scalar_tensor_tensor(state[:], state[:], small[:, S_ELAST + n:S_ELAST + n + 1],
                                                           part(bank(4), 0), MULT, ADD).then_inc(g_dve, 1)
                    if more and n == 1:
                        short_gate()
                        ahead(5)
                    if not more and n == 1:
                        ahead(2)
                after_act("o_squares")
                nc.vector.tensor_tensor(gd["dec"][:], gd["dec"][:], gd["q_sq"][:], ADD).then_inc(g_dve, 1)
                after_pe("o_sums")
                nc.vector.tensor_scalar(col4(S_OMS), bank(5)[:, 0:NC], P * EPS * 4 * EPS, None, ADD).then_inc(g_dve, 1)
                nc.vector.tensor_tensor(mod[:, bass.ds(4 * h + 16, 4)], bank(5)[:, 8:12],
                                        vec[:, bass.ds(4 * h + (V_BADA + 16), 4)], ADD).then_inc(g_dve, 1)
                nc.vector.tensor_tensor(mod[:, bass.ds(2 * h + 48, 2)], bank(5)[:, 12:14],
                                        vec[:, bass.ds(2 * h + V_BADAF, 2)], ADD).then_inc(g_dve, 1)
                dve.wait_ge(cv_dve, 10 * h + 10)
                nc.vector.tensor_tensor(gd["low"][:], bank(3), gd["z_g"][:], MULT).then_inc(g_dve, 1)
                if more:
                    ahead(6)
                after_pe("o_norm_rows")
                own("o_gate")
                nc.vector.tensor_tensor(gd["low_d"][:], gd["low"][:], bank(6), MULT).then_inc(g_dve, 1)
                after_act("o_hi")
                nc.vector.tensor_tensor(dyn(og_lo, h), gd["low_d"][:], dyn(og_hi, h).bitcast(F32), SUB).then_inc(g_dve, 1)
                if more:
                    ahead(7)
                    z_silu(stage, 7, i, h + 1)
                else:
                    ahead(3)

            with dve.Fori(0, H - 1) as h:
                head(HEAD, h, h)
            head(LAST, 0, H - 1)

            dve.wait_ge(g_dve, heads(DVE_STEPS, H))
            nc.vector.scalar_tensor_tensor(wsc[:, 1], mod[:, SC2:SC2 + KD], 1.0, vec[:, V_N2:V_N2 + KD], ADD, MULT)
            nc.vector.scalar_tensor_tensor(wsc[:, 2], mod[:, SCF:SCF + KD], 1.0, vec[:, V_NF:V_NF + KD], ADD, MULT)
            nc.vector.tensor_scalar(mod[:, G1:G1 + KD], mod[:, G1:G1 + KD], 0.5, None, MULT).then_inc(mod_ready, 1)
            dve.wait_ge(sc_split, 1)
            nc.vector.tensor_tensor(sc_lo[:], sc_out[:], sc_hi[:].bitcast(F32), SUB).then_inc(sc_split, 1)
            with dve.Fori(0, 2) as i:
                for t in range(4):
                    split(GATE.tile(t, i).ahead())
                for m in range(4):
                    bg, before_g = GATE.out(m, i)
                    b, before = next_tile(GATE, 4 + 2 * m, i)
                    dve.wait_ge(out_used[bg], before_g + 1)
                    nc.vector.scalar_tensor_tensor(yb[:], gb_t[:, m], 1.0, bank(b), ADD, MULT).then_inc(out_used[b], 1)
                    b2, before2 = next_tile(GATE, 5 + 2 * m, i)
                    ga = dyn(ga_t, 4 * i + m)
                    nc.vector.scalar_tensor_tensor(ga, ga, 1.0, bank(b2), ADD, MULT).then_inc(out_used[b2], 1)
                    dve.wait_ge(out_used[b], before + 1)
                    dve.wait_ge(out_used[b2], before2 + 1)
                    nc.vector.tensor_tensor(ga, ga, yb[:], ADD).then_inc(mixed, 1)
                    dve.wait_ge(mixed, 4 * i + m + 1)
            for m in range(KD):
                dve.wait_ge(mix_hi, m + 1)
                nc.vector.tensor_tensor(h_lo[:, m], ga_t[:, m], h_hi[:, m].bitcast(F32), SUB).then_inc(mix_lo, 1)
            dve.wait_ge(mod_ready, 2)
            with dve.Fori(0, 2) as i:
                for t in range(4):
                    b, before = next_tile(WO, t, i)
                    xm = dyn(x, 4 * i + t)
                    nc.vector.scalar_tensor_tensor(xm, bank(b), col(mod, 4 * i + (G1 + t)), xm, MULT, ADD)\
                      .then_inc(out_used[b], 1)

            def feed_forward(f):
                base = 0 if f == 0 else 2 * UPS + 4 * UPS * (f - 1)
                own = 2 * UPS * (f - 1)
                with dve.Fori(0, UPS) as i:
                    for j in range(2):
                        g, u, gu = tmp[:, 2 + j], 2 * j + 1, tmp[:, 4 + j]
                        b, before = next_tile(UP[f], 2 * j, i)
                        if f == 0:
                            dve.wait_ge(f_act, 2 * i + j + 1)
                            nc.vector.scalar_tensor_tensor(g, tmp[:, j], 1.0, bank(b), ADD, MULT).then_inc(out_used[b], 1)
                        else:
                            dve.wait_ge(f_act, 4 * i + (base + 2 * j + 1))
                            nc.vector.scalar_tensor_tensor(g[:, 1:T], bank(b)[:, 0:T - 1], col(vec, 2 * i + (V_FCW[f - 1] + j)),
                                                           g[:, 1:T], MULT, ADD).then_inc(f_dve, 1)
                            dve.wait_ge(f_dve, 2 * i + (own + j + 1))
                            nc.vector.scalar_tensor_tensor(g[:, 0:T - 1], bank(b)[:, 1:T],
                                                           col(vec, 2 * i + (V_FCW[f - 1] + 2 * KF + j)),
                                                           g[:, 0:T - 1], MULT, ADD).then_inc(out_used[b], 1)
                        bu, before_u = next_tile(UP[f], u, i)
                        if f == 0:
                            dve.wait_ge(out_used[b], before + 1)
                            nc.vector.scalar_tensor_tensor(gu, g, 0.5, bank(bu), MULT, MULT).then_inc(out_used[bu], 1)
                        else:
                            dve.wait_ge(f_act, 4 * i + (base + 2 * j + 2))
                            nc.vector.tensor_tensor(gu, tmp[:, j], bank(bu), MULT).then_inc(out_used[bu], 1)
                        dve.wait_ge(f_hi, 2 * i + (KF * f + j + 1))
                        nc.vector.tensor_tensor(dyn(act_lo, 2 * i + j), gu, dyn(act_hi, 2 * i + j).bitcast(F32), SUB)\
                          .then_inc(f_lo, 1)

                def down(i):
                    for m in range(4):
                        for c in range(3):
                            split(DOWN[f].tile(3 * m + c, i).ahead())
                        dve.wait_ge(tile_done, DOWN[f].tile(3 * m + 2, i).before + 1)
                        b, before = DOWN[f].out(m, i)
                        xm = dyn(x, 4 * i + m)
                        if f == 0:
                            nc.vector.scalar_tensor_tensor(xm, bank(b), col(mod, 4 * i + (G2 + m)), xm, MULT, ADD)\
                              .then_inc(out_used[b], 1)
                        else:
                            nc.vector.tensor_tensor(xm, xm, bank(b), ADD).then_inc(out_used[b], 1)

                if f == 2:
                    down(0)
                    down(1)
                else:
                    with dve.Fori(0, 2) as i:
                        down(i)

            normed(N_FFN)
            feed_forward(0)
            normed(N_OUT1)

            nc.vector.memset(win[0][:], 0.0).then_inc(pl_dve, 1)
            token_factor(N_POOL)
            dve.wait_ge(cnt_in, 16)
            count = 1

            def pool_lo(m):
                dve.wait_ge(pl_hi, m + 1)
                nc.vector.tensor_tensor(p_lo[:, m], tmp[:, 2 + m % 2], p_hi[:, m].bitcast(F32), SUB).then_inc(pl_lo, 1)

            for m in range(KD):
                group = m // 2
                centre = win[0][:, 8:8 + T]
                dve.wait_ge(pl_dve, count)
                dve.wait_ge(n_ht, scaled_base(N_OUT1) + m + 1)
                nc.vector.tensor_tensor(centre, x[:, m], bank(3), MULT).then_inc(pl_dve, 1)
                count += 1
                src = win[0]
                for n in range(group + 1):
                    back, ahead, edge = (1, 0, 1) if n == 0 else (1 << (n - 1), 1 << (n - 1), 1 << n)
                    dst = win[1 + n % 2]
                    lo, hi = edge, T + 16 - edge
                    dve.wait_ge(pl_dve, count)
                    nc.vector.tensor_tensor(dst[:, lo:hi], src[:, lo - back:hi - back], src[:, lo + ahead:hi + ahead], ADD)\
                      .then_inc(pl_dve, 1)
                    count += 1
                    src = dst
                if m >= 2:
                    dve.wait_ge(pl_act, m - 1)
                dve.wait_ge(pl_dve, count)
                nc.vector.tensor_tensor(pool_d[:, m % 2], src[:, 8:8 + T], inv_cnt[:, group], MULT).then_inc(pl_dve, 1)
                dve.wait_ge(pl_dve, count + 1)
                nc.vector.tensor_tensor(pool_d[:, m % 2], pool_d[:, m % 2], centre, SUB).then_inc(pl_dve, 1)
                count += 2
                assert count == POOL_STEP[m]
                if m:
                    pool_lo(m - 1)
            pool_lo(KD - 1)
            for t in range(2):
                for j in range(4):
                    m = 4 * t + j
                    b, before = POOLW.out(m, 0)
                    if j < 3:
                        dve.wait_ge(pl_out, 3 * t + j + 1)
                    else:
                        dve.wait_ge(tile_done, POOLW.tile(t, 0).before + 1)
                    nc.vector.scalar_tensor_tensor(x[:, m], bank(b), vec[:, V_PSC + m:V_PSC + m + 1], x[:, m], MULT, ADD)\
                      .then_inc(out_used[b], 1)
                split(POOLW.tile(t, 0).ahead())
            normed(N_FFN0)
            feed_forward(1)

            dve.wait_ge(pos_in, 16)
            nc.vector.tensor_copy(pos_f[0:1], pos_i[0:1]).then_inc(rp_dve, 1)
            normed(N_ATT)
            ang, rnd = at["ang"][:], at["rnd"][:]
            dve.wait_ge(rp_pe, 1)
            nc.vector.tensor_scalar(ang, bank(4), cst[:, C_FREQ:C_FREQ + 1], None, MULT).then_inc(rp_dve, 1)
            dve.wait_ge(rp_dve, 2)
            nc.vector.tensor_scalar(rnd, ang, float(1 / (2 * np.pi)), MAGIC, MULT, ADD).then_inc(rp_dve, 1)
            dve.wait_ge(rp_dve, 3)
            nc.vector.tensor_scalar(rnd, rnd, -MAGIC, None, ADD).then_inc(rp_dve, 1)
            for n in range(3):
                dve.wait_ge(rp_dve, 4 + n)
                nc.vector.scalar_tensor_tensor(ang, rnd, -TWO_PI[n], ang, MULT, ADD).then_inc(rp_dve, 1)
            dve.wait_ge(rp_dve, 7)
            nc.vector.tensor_scalar(ang, ang, 3.1415925, -3.1415925, ALU.min, ALU.max).then_inc(rp_dve, 1)
            dve.wait_ge(rp_act, 1)
            nc.vector.tensor_scalar(at["sin"][:], at["sin"][:], cst[:, C_SIGN:C_SIGN + 1], None, MULT).then_inc(rp_dve, 1)
            dve.wait_ge(lam_in_s, 64)
            pairs = lam_in[0:1].rearrange("o (c e) d -> o c e d", e=2)
            nc.vector.tensor_tensor(pairs[:, :, 0], pairs[:, :, 0], pairs[:, :, 1], MULT).then_inc(rp_dve, 1)
            dve.wait_ge(rp_dve, 10)
            nc.vector.tensor_reduce(small[0:1, S_MAX:S_MAX + 2], pairs[:, :, 0], AX_X, ADD).then_inc(rp_dve, 1)
            dve.wait_ge(rp_act, 4)
            nc.vector.scalar_tensor_tensor(small[0:1, S_SUM:S_SUM + 1], small[0:1, S_NEG:S_NEG + 1], LAM_INIT,
                                           small[0:1, S_NEG + 1:S_NEG + 2], ADD, SUB).then_inc(rp_dve, 1)

            def rope_tile(stage, t, j, i, n, name):
                split(stage.tile(t, i).ahead())
                b, before = stage.out(j, i)
                dve.wait_ge(rp_act, 2 * n + 5)
                nc.vector.tensor_tensor(at["rot"][:], bank(b), at["cos"][:], MULT).then_inc(out_used[b], 1)
                nc.vector.tensor_tensor(at["swap"][:], at["swap"][:], at["sin"][:], MULT).then_inc(rp_dve, 1)
                dve.wait_ge(out_used[b], before + 1)
                dve.wait_ge(rp_dve, roped(n) + 1)
                nc.vector.tensor_tensor(at["rot"][:], at["rot"][:], at["swap"][:], ADD).then_inc(rp_dve, 1)
                dve.wait_ge(rp_act, 2 * n + 6)
                nc.vector.tensor_tensor(at[name + "_lo"][:], at["rot"][:], at[name + "_hi"][:].bitcast(F32), SUB)\
                  .then_inc(rp_dve, 1)

            rope_tile(ATT_Q, 0, 0, 0, 0, "k")
            rope_tile(ATT_Q, 1, 1, 0, 1, "q")
            split(ATT_Q.tile(2, 0).ahead())
            dve.wait_ge(rp_pe, 2)
            nc.vector.tensor_copy(small[:, S_LAM:S_LAM + 1], bank(7)[:, 0:1])

            def v_lo():
                nc.vector.tensor_tensor(at["v_lo"][:], bank(6), at["v_hi"][:].bitcast(F32), SUB).then_inc(t_dve, 1)

            dve.wait_ge(t_act, 1)
            v_lo()

            def att_head(stage, i, h, wo, nxt):
                t0, j0 = (1, KD) if wo else (0, 0)

                def own(name):
                    dve.wait_ge(t_dve, step(ATT_DVE, name, h))

                def maxima(q):
                    s = 2 * (q % 2)
                    dve.wait_ge(t_pe, step(ATT_PE, f"scores{q}", h))
                    nc.vector.tensor_reduce(small[:, S_MAX + s:S_MAX + s + 2], ps[:, 2 + s:4 + s, :], AX_X, ALU.max)\
                      .then_inc(t_dve, 1)
                    own(f"max{q}")
                    nc.vector.tensor_scalar(small[:, S_NEG + s:S_NEG + s + 2], small[:, S_MAX + s:S_MAX + s + 2], -0.125, None,
                                            MULT).then_inc(t_dve, 1)

                def turn_lo(q):
                    dve.wait_ge(t_act, step(ATT_ACT, f"turn{q}", h))
                    nc.vector.tensor_tensor(at_lo[:, :, P * q:P * q + P], chunks(bank(6 + q % 2)),
                                            at_hi[:, :, P * q:P * q + P].bitcast(F32), SUB).then_inc(t_dve, 1)

                maxima(0)
                for q in range(NC):
                    if q + 1 < NC:
                        maxima(q + 1)
                    s, pr = 2 * (q % 2), prob[:, q % 2]
                    dve.wait_ge(t_act, step(ATT_ACT, f"exp{q}", h))
                    nc.vector.reciprocal(small[:, S_REC + s:S_REC + s + 2], small[:, S_SUM + s:S_SUM + s + 2]).then_inc(t_dve, 1)
                    own(f"recip{q}")
                    nc.vector.tensor_tensor(small[:, S_L + s:S_L + s + 1], small[:, S_REC + s + 1:S_REC + s + 2],
                                            small[:, S_LAM:S_LAM + 1], MULT).then_inc(t_dve, 1)
                    own(f"lam{q}")
                    nc.vector.tensor_scalar(pr[:, 1], pr[:, 1], small[:, S_L + s:S_L + s + 1], None, MULT).then_inc(t_dve, 1)
                    own(f"second{q}")
                    if q >= 2:
                        dve.wait_ge(t_pe, step(ATT_PE, f"turn{q - 2}", h))
                    nc.vector.scalar_tensor_tensor(a_sb[:, q % 2], pr[:, 0], small[:, S_REC + s:S_REC + s + 1], pr[:, 1], MULT, SUB)\
                      .then_inc(t_dve, 1)
                    if q >= 2:
                        turn_lo(q - 2)
                turn_lo(2)
                turn_lo(3)
                if wo:
                    split(stage.tile(0, i).ahead())
                if nxt:
                    rope_tile(stage, t0, j0, i, 2 * h + 2, "k")
                dve.wait_ge(t_pe, step(ATT_PE, "sums", h))
                nc.vector.tensor_scalar(col4(S_OMS), bank(7)[:, 0:NC], SUBLN_EPS, None, ADD).then_inc(t_dve, 1)
                dve.wait_ge(t_pe, step(ATT_PE, "rows", h))
                nc.vector.tensor_tensor(at["o_n"][:], at["o_s"][:], bank(6), MULT).then_inc(t_dve, 1)
                if nxt:
                    rope_tile(stage, t0 + 1, j0 + 1, i, 2 * h + 3, "q")
                dve.wait_ge(t_act, step(ATT_ACT, "hi", h))
                nc.vector.tensor_tensor(at["ao_lo"][:], at["o_n"][:], at["ao_hi"][:].bitcast(F32), SUB).then_inc(t_dve, 1)
                if nxt:
                    split(stage.tile(t0 + 2, i).ahead())
                    dve.wait_ge(t_act, step(ATT_ACT, "v_next", h))
                    v_lo()

            att_head(ATT_0, 0, 0, False, True)
            with dve.Fori(0, H - 2) as i:
                att_head(ATT_H, i, i + 1, True, True)
            att_head(ATT_7, 0, H - 1, True, False)
            dve.wait_ge(wo_add, KD * (H - 1) + 4)
            for m in range(KD):
                b, before = ATT_WO.out(m, 0)
                if m < KD - 1:
                    dve.wait_ge(wo_out, (KD - 1) * (H - 1) + m + 1)
                else:
                    dve.wait_ge(tile_done, ATT_WO.tile(0, 0).before + 1)
                nc.vector.tensor_tensor(x[:, m], x[:, m], bank(b), ADD).then_inc(out_used[b], 1)
            split(ATT_WO.tile(0, 0).ahead())
            normed(N_FFN1)
            feed_forward(2)
            normed(N_OUT2)

        @block.tensor
        def _(pe):
            def open_out(out):
                b, before = out
                if not (isinstance(before, int) and before == 0):
                    pe.wait_ge(out_used[b], before)
                return b

            def term(dst, tile, k, hi, lo, first, last):
                nc.tensor.matmul(dst, w_hi[:, tile.slot, k], hi, start=first, stop=False)
                nc.tensor.matmul(dst, w_hi[:, tile.slot, k], lo, start=False, stop=False)
                return nc.tensor.matmul(dst, w_lo[:, tile.slot, k], hi, start=False, stop=last)

            def quarter(stage, t, j, i, q):
                tile = stage.tile(t, i)
                if q == 0:
                    pe.wait_ge(lo_ready, tile.before + 1)
                    open_out(stage.out(j, i))
                for k in (2 * q, 2 * q + 1):
                    last = term(bank(stage.banks[j]), tile, k, h_hi[:, k], h_lo[:, k], k == 0, k == KD - 1)
                if q == 3:
                    last.then_inc(tile_done, 1)

            def product(stage, t, i, hi, lo):
                tile = stage.tile(t, i)
                pe.wait_ge(lo_ready, tile.before + 1)
                b = open_out(stage.out(t, i))
                for k in range(KD):
                    last = term(bank(b), tile, k, hi[:, k], lo[:, k], k == 0, k == KD - 1)
                last.then_inc(tile_done, 1)

            def turn(dst, src, n_rows=P):
                return nc.tensor.transpose(dst, src, ident[0:n_rows, 0:n_rows])

            def product_pair(outs, hi, lo, ready):
                pairs = []
                for stage, t in outs:
                    tile = stage.tile(t, 0)
                    pe.wait_ge(lo_ready, tile.before + 1)
                    pairs.append((tile, open_out(stage.out(t, 0))))
                for k in range(KD):
                    pe.wait_ge(ready[0], ready[1] + k + 1)
                    for tile, b in pairs:
                        last = term(bank(b), tile, k, hi[:, k], lo[:, k], k == 0, k == KD - 1)
                        if k == KD - 1:
                            last.then_inc(tile_done, 1)

            def sum_squares(r, m):
                pe.wait_ge(fsq_act, KD * PSUM_SUMS.index(r) + m + 1)
                if m == 0:
                    nc.tensor.matmul(bank(2)[:, 0:NC], ident, cst[:, C_ZERO:C_ZERO + NC], start=True, stop=False)
                for n in range(NC):
                    s = nc.tensor.matmul(bank(2)[:, n:n + 1], part(tmp[:, 2 + m % 4], n), one_col, start=False,
                                         stop=m == KD - 1 and n == NC - 1)
                s.then_inc(fsq_pe if m < KD - 1 else n_pe, 1)

            def rows_of(b, c):
                for n in range(NC):
                    t = turn(part(bank(b), n), small[:, c + n:c + n + 1].to_broadcast([P, P]))
                return t

            def first_sums():
                pe.wait_ge(sq_done, KD)
                for n in range(NC):
                    s = nc.tensor.matmul(bank(2)[:, n:n + 1], part(sq_sum, n), one_col, start=True, stop=True)
                s.then_inc(n_pe, 1)

            def norm(r):
                if r in POOL_SUMS and r != N_MIX:
                    pe.wait_ge(sq_done, KD * (POOL_SUMS.index(r) + 1))
                    for n in range(NC):
                        s = nc.tensor.matmul(bank(2)[:, n:n + 1], part(sq_sum, n), one_col, start=True, stop=True)
                    s.then_inc(n_pe, 1)
                pe.wait_ge(n_pool, r + 1)
                rows_of(3, S_RSTD).then_inc(n_pe, 1)

            pe.wait_ge(x_in, 16)
            pe.wait_ge(cst_in, 32)
            for m in range(KD):
                for n in range(NC):
                    t = turn(part(bank(m), n), x_tok[:, n, P * m:P * m + P])
                t.then_inc(pro_pe, 1)
            pe.wait_ge(pack_in, 16 * 17)
            pe.wait_ge(x_even, 1)
            for n, rows_in in enumerate(PACK_ROWS):
                t = turn(bank(0)[:, P * n:P * n + rows_in], pack[0:rows_in, n, :], rows_in)
            t.then_inc(pro_pe, 1)
            pe.wait_ge(x_odd, 1)
            pe.wait_ge(pro_dve, 5)
            pe.wait_ge(ada_in[1], 16)
            for j in range(4, 8):
                for k in range(KD):
                    nc.tensor.matmul(bank(1)[:, j:j + 1], ada0[:, k, P * j:P * j + P], cact[:, 1, k:k + 1],
                                     start=k == 0, stop=k == KD - 1)
            for turn_n, q in enumerate((0, 2, 3)):
                pe.wait_ge(ada0_own, KD * (turn_n + 1))
                for j in range(4 * q, 4 * q + 4):
                    s = nc.tensor.matmul(bank(1)[:, j:j + 1], ada0_sum[:, P * j:P * j + P], one_col, start=True, stop=True)
                if turn_n == 0:
                    first_sums()
            s.then_inc(pro_pe, 1)
            norm(N_MIX)
            pe.wait_ge(mod_ready, 1)
            product_pair(((AB, 0), (QKVZ, 0)), h_hi, h_lo, (h_ready, split_base(N_MIX)))
            pe.wait_ge(out_used[0], 1)
            for n in range(NC):
                t = turn(bank(2)[:, 2 * H * n:2 * H * n + 2 * H], part(ab_f[0:2 * H], n), 2 * H)
            t.then_inc(ab_pe, 1)
            product(QKVZ, 1, 0, h_hi, h_lo)
            pe.wait_ge(ab_dve, 17)
            nc.tensor.matmul(bank(3)[:, 0:2 * H * NC], cst[:, C_UP:C_UP + P], ab[6][:].rearrange("p n c -> p (n c)"),
                             start=True, stop=True).then_inc(ab_pe, 1)
            pe.sem_inc(g_pe, 1)
            for t in range(2, 4):
                product(QKVZ, t, 0, h_hi, h_lo)

            def head(stage, i, h, fills):
                q_s, k_s, v_s, x_t, y_t, u_t = [gd[n] for n in ("q_s", "k_s", "v_s", "x_t", "y_t", "u_t")]
                filled = [0]

                def fill(name):
                    for _ in range(fills.get(name, 0)):
                        t, q = divmod(filled[0], 4)
                        quarter(stage, t, t, i, q)
                        filled[0] += 1

                def after_dve(name):
                    pe.wait_ge(g_dve, step(DVE_STEPS, name, h))

                def after_act(name):
                    pe.wait_ge(g_act, step(ACT_STEPS, name, h))

                def by_chunk(b, lhs, rhs, turned=False):
                    for n in range(NC):
                        if turned:
                            ins = turn(part(bank(b), n), part(lhs, n))
                        else:
                            ins = nc.tensor.matmul(part(bank(b), n), part(lhs, n), part(rhs, n), start=True, stop=True)
                    return ins

                fill("kv_tokens")
                pe.wait_ge(cv_dve, 10 * h + 9)
                pe.wait_ge(g_dve, heads(DVE_STEPS, h))
                by_chunk(2, k_s, None, True)
                by_chunk(3, v_s, None, True).then_inc(g_pe, 1)
                fill("g_rows")
                after_dve("g_col")
                rows_of(4, S_G).then_inc(g_pe, 1)
                fill("kk_qk")
                by_chunk(5, k_s, k_s)
                by_chunk(6, k_s, q_s).then_inc(g_pe, 1)
                fill("kb_rows")
                after_dve("kb")
                rows_of(7, S_KB).then_inc(g_pe, 1)
                fill("x_pairs")
                after_dve("u0")
                after_act("exp_last")
                by_chunk(4, u_t, None, True).then_inc(g_pe, 1)
                for n in range(LEVELS):
                    fill(f"y{n}")
                    pe.wait_ge(g_pool, step(POOL_STEPS, f"mask{n}", h))
                    if n:
                        after_dve(f"x{n - 1}")
                    else:
                        after_act("x_pairs")
                    by_chunk(4, low_part[n % 2], x_t).then_inc(g_pe, 1)
                    fill(f"x{n}")
                    after_dve(f"y{n}")
                    if n:
                        after_act(f"u{n - 1}")
                    if n < LEVELS - 1:
                        by_chunk(5, u_t, y_t).then_inc(g_pe, 1)
                    fill(f"u{n}")
                    by_chunk(6, y_t, u_t).then_inc(g_pe, 1)
                fill("w")
                after_act(f"u{LEVELS - 1}")
                by_chunk(7, gd["k_beg"], u_t).then_inc(g_pe, 1)
                for n in range(NC):
                    fill(f"v_new{n}")
                    v_new = nc.tensor.matmul(part(bank(2), n), part(u_t, n), part(gd["v_b"], n), start=True, stop=n == 0)
                    if n:
                        after_act("w")
                        after_dve(f"state{n - 1}")
                        v_new = nc.tensor.matmul(part(bank(2), n), part(x_t, n), state[:], start=False, stop=True)
                    v_new.then_inc(g_pe, 1)
                    fill(f"o{n}")
                    after_dve(f"v_new{n}")
                    if n:
                        nc.tensor.matmul(part(bank(3), n), state[:], part(gd["q_g"], n), start=True, stop=False)
                    o = nc.tensor.matmul(part(bank(3), n), part(y_t, n), part(gd["qk_t"], n), start=n == 0, stop=True)
                    if n < NC - 1:
                        o = nc.tensor.matmul(part(bank(4), 0), part(gd["k_dec"], n), part(y_t, n), start=True, stop=True)
                    o.then_inc(g_pe, 1)
                fill("o_sums")
                after_dve("o_sum")
                for n in range(NC):
                    nc.tensor.matmul(bank(5)[:, n:n + 1], part(gd["dec"], n), cst[:, C_MEAN:C_MEAN + 1], start=True, stop=True)
                pe.wait_ge(g_pool, step(POOL_STEPS, "ada", h))
                for j in range(6):
                    s = nc.tensor.matmul(bank(5)[:, 8 + j:9 + j], ada_s[:, j], one_col, start=True, stop=True)
                s.then_inc(g_pe, 1)
                fill("o_norm_rows")
                pe.wait_ge(g_pool, step(POOL_STEPS, "o_norm", h))
                rows_of(6, S_ON).then_inc(g_pe, 1)

            with pe.Fori(0, H - 1) as h:
                head(HEAD, h, h, HEAD_FILL)
            head(LAST, 0, H - 1, LAST_FILL)

            with pe.Fori(0, 2) as i:
                for t in range(4):
                    product(GATE, t, i, h_hi, h_lo)
                for m in range(4):
                    if m == 0:
                        pe.wait_ge(sc_split, 2)
                    product(GATE, 4 + 2 * m, i, sc_hi, sc_lo)
                    if m == 0:
                        pe.wait_ge(g_dve, heads(DVE_STEPS, H))
                    product(GATE, 5 + 2 * m, i, og_hi, og_lo)
            product_pair(((WO, 0), (WO, 1)), h_hi, h_lo, (mix_lo, 0))
            for n in range(2, KD):
                product(WO, n % 4, n // 4, h_hi, h_lo)

            def feed_forward(f, r):
                product_pair(((UP[f], 0), (UP[f], 1)), h_hi, h_lo, (h_ready, split_base(r)))
                for t in (2, 3):
                    product(UP[f], t, 0, h_hi, h_lo)
                rest = UP[f].after_first()
                with pe.Fori(0, UPS - 1) as i:
                    for t in range(4):
                        product(rest, t, i, h_hi, h_lo)
                with pe.Fori(0, 2) as i:
                    for m in range(4):
                        b = open_out(DOWN[f].out(m, i))
                        for c in range(3):
                            tile = DOWN[f].tile(3 * m + c, i)
                            pe.wait_ge(lo_ready, tile.before + 1)
                            pe.wait_ge(f_lo, KF * f + min(KD * (c + 1), KF))
                            for k in range(min(KD, KF - KD * c)):
                                n = KD * c + k
                                last = term(bank(b), tile, k, act_hi[:, n], act_lo[:, n], n == 0, n == KF - 1)
                            last.then_inc(tile_done, 1)

            norm(N_FFN)
            feed_forward(0, N_FFN)
            norm(N_OUT1)

            for m in range(KD):
                sum_squares(N_POOL, m)
            norm(N_POOL)
            for t in range(2):
                tile = POOLW.tile(t, 0)
                pe.wait_ge(lo_ready, tile.before + 1)
                for j in range(4):
                    group, half = divmod(4 * t + j, 2)
                    b = open_out(POOLW.out(4 * t + j, 0))
                    pe.wait_ge(pl_lo, 2 * group + 2)
                    for k in range(2):
                        n = 2 * group + k
                        last = term(bank(b), tile, 4 * (group % 2) + 2 * k + half, p_hi[:, n], p_lo[:, n], k == 0, k == 1)
                    last.then_inc(tile_done if j == 3 else pl_out, 1)
                    if 4 * t + j >= 3:
                        sum_squares(N_FFN0, 4 * t + j - 3)
            for m in range(KD - 3, KD):
                sum_squares(N_FFN0, m)
            norm(N_FFN0)
            feed_forward(1, N_FFN0)

            pe.wait_ge(rp_dve, 1)
            nc.tensor.matmul(bank(4), ones[0:1, :], pos_f[0:1, :], start=True, stop=True).then_inc(rp_pe, 1)
            norm(N_ATT)
            product_pair(((ATT_Q, 0), (ATT_Q, 1)), h_hi, h_lo, (h_ready, split_base(N_ATT)))
            product(ATT_Q, 2, 0, h_hi, h_lo)
            pe.wait_ge(rp_dve, ROPE_SETUP)
            nc.tensor.matmul(bank(7)[:, 0:1], ones[0:1, :], small[0:1, S_SUM:S_SUM + 1], start=True, stop=True).then_inc(rp_pe, 1)

            def v_tokens(out):
                pe.wait_ge(out_used[out[0]], out[1] + 1)
                for n in range(NC):
                    t = turn(part(bank(6), n), part(at["v_f"], n))
                t.then_inc(t_pe, 1)

            v_tokens(ATT_Q.out(2, 0))

            def projection(stage, i, h, ms):
                tile = stage.tile(0, i)
                if ms[0] == 0:
                    pe.wait_ge(lo_ready, tile.before + 1)
                    pe.wait_ge(t_dve, step(ATT_DVE, "lo", h))
                for m in ms:
                    b = open_out(stage.out(m, i))
                    last = term(bank(b), tile, m, at["ao_hi"][:], at["ao_lo"][:], True, True)
                    last.then_inc(wo_out if m < KD - 1 else tile_done, 1)

            def split_product(dst, w, a, rows, cols):
                w_parts, a_parts = [at[w + p][rows, cols] for p in ("_hi", "_lo")], [at[a + p][rows, :] for p in ("_hi", "_lo")]
                nc.tensor.matmul(dst, w_parts[0], a_parts[0], start=True, stop=False)
                nc.tensor.matmul(dst, w_parts[0], a_parts[1], start=False, stop=False)
                return nc.tensor.matmul(dst, w_parts[1], a_parts[0], start=False, stop=True)

            def att_head(stage, i, h, wo, nxt):
                t0, j0 = (1, KD) if wo else (0, 0)

                def fill(t, q):
                    if nxt:
                        quarter(stage, t0 + t, j0 + t, i, q)

                pe.wait_ge(rp_dve, roped(2 * h + 2))
                for q in range(NC):
                    if q >= 2:
                        pe.wait_ge(t_act, step(ATT_ACT, f"exp{q - 2}", h))
                    for c in range(2):
                        s = split_product(bank(2 + 2 * (q % 2) + c), "q", "k", slice(64 * c, 64 * c + 64), slice(P * q, P * q + P))
                    s.then_inc(t_pe, 1)
                    if wo:
                        projection(stage, i, h - 1, (2 * q, 2 * q + 1))
                for q in range(NC):
                    pe.wait_ge(t_dve, step(ATT_DVE, f"a{q}", h))
                    pe.wait_ge(t_dve, step(ATT_DVE, f"turn_lo{q - 2}", h) if q >= 2 else heads(ATT_DVE, h))
                    for n in range(NC):
                        t = turn(part(bank(6 + q % 2), n), part(a_sb[:, q % 2], n))
                    t.then_inc(t_pe, 1)
                    fill(0, q)
                fill(1, 0)
                pe.wait_ge(t_dve, step(ATT_DVE, f"turn_lo{NC - 1}", h))
                for n in range(NC):
                    nc.tensor.matmul(bank(7), part(at["v_hi"], n), at_hi[:, n], start=n == 0, stop=False)
                    nc.tensor.matmul(bank(7), part(at["v_hi"], n), at_lo[:, n], start=False, stop=False)
                    o = nc.tensor.matmul(bank(7), part(at["v_lo"], n), at_hi[:, n], start=False, stop=n == NC - 1)
                o.then_inc(t_pe, 1)
                fill(1, 1)
                fill(1, 2)
                pe.wait_ge(t_act, step(ATT_ACT, "squares", h))
                for n in range(NC):
                    s = nc.tensor.matmul(bank(7)[:, n:n + 1], part(at["o_sq"], n), cst[:, C_MEAN:C_MEAN + 1], start=True, stop=True)
                s.then_inc(t_pe, 1)
                fill(1, 3)
                pe.wait_ge(t_pool, h + 1)
                rows_of(6, S_ON).then_inc(t_pe, 1)
                for q in range(4):
                    fill(2, q)
                if nxt:
                    pe.wait_ge(t_dve, step(ATT_DVE, "scale", h))
                    v_tokens(stage.out(j0 + 2, i))

            att_head(ATT_0, 0, 0, False, True)
            with pe.Fori(0, H - 2) as i:
                att_head(ATT_H, i, i + 1, True, True)
            att_head(ATT_7, 0, H - 1, True, False)
            for m in range(KD + 3):
                if m < KD:
                    projection(ATT_WO, 0, H - 1, (m,))
                if m >= 3:
                    sum_squares(N_FFN1, m - 3)
            norm(N_FFN1)
            feed_forward(2, N_FFN1)

            norm(N_OUT2)
            for m in range(KD):
                pe.wait_ge(n_ht, scaled_base(N_OUT2) + m + 1)
                if m >= 2:
                    pe.wait_ge(fin_act, m - 1)
                for n in range(NC):
                    t = turn(part(bank(4 + m % 2), n), part(tmp[:, 2 + m % 2], n))
                t.then_inc(fin_pe, 1)


def kernel(**inputs):
    import numpy as _np
    import concourse.bacc as _bacc
    from concourse import mybir as _mybir
    from concourse.bass_utils import run_bass_kernel_spmd as _run

    nc = _bacc.Bacc("TRN2", target_bir_lowering=False, num_devices=1)
    arrays = {name: _np.ascontiguousarray(v) for name, v in inputs.items() if _np.size(v)}
    tile, masks, counts = constants()
    arrays.update(const_tile=tile, const_masks=masks, const_counts=counts)
    aps = {name: nc.dram_tensor(name, v.shape, _mybir.dt.from_np(v.dtype), kind="ExternalInput").ap()
           for name, v in arrays.items()}
    out = nc.dram_tensor("out", (1, T, D), F32, kind="ExternalOutput").ap()
    block_kernel(nc, aps, out)
    r = _run(nc, [arrays], core_ids=[0])
    return r.results[0]["out"]
```

```python
from contextlib import ExitStack

import numpy as np

import concourse.bass as bass
from concourse import mybir

F32, F32R, I32 = mybir.dt.float32, mybir.dt.float32r, mybir.dt.int32
ALU = mybir.AluOpType
ACT = mybir.ActivationFunctionType
AX_X = mybir.AxisListType.X
MULT, ADD, SUB = ALU.mult, ALU.add, ALU.subtract

P = 128
T = 512
D = 1024
KD = D // P
NC = T // P
H = 8
FF = 2816
KF = FF // P
UPS = KF // 2
RING = 4
WINDOWS = (2, 4, 8, 16)
EDGE = WINDOWS[-1] // 2
LEVELS = 6
EPS = 1e-6
SUBLN_EPS = 1e-5
LAM_INIT = 0.8 - 0.6 * float(np.exp(-0.3))

Q0, K0, V0, Z0 = 0, D, 2 * D, 3 * D
AB0 = 4 * D
SCB0 = AB0 + 2 * H
SCC0, SCX0 = SCB0 + D, SCB0 + 2 * D
GA0, GB0 = SCB0 + 3 * D, SCB0 + 4 * D

SH1, SC1, G1, SH2, SC2, G2, SHF, SCF = range(0, 64, 8)

V_BADA, V_BADAF, V_N1, V_N2, V_NF, V_C, V_MIX, V_PSC, V_FIN = 0, 48, 64, 72, 80, 88, 96, 112, 120
V_CONV, V_SCONV, V_GNW, V_SUB = 128, 224, 248, 249
V_FCW = (256, 384)
V_FCB, V_FFN = 322, 366
PACK_ROWS = (128, 122, 126, 66)

C_ID, C_ONE, C_LOW, C_L1, C_UP, C_COL = 0, P, 2 * P, 3 * P, 4 * P, 5 * P
C_FREQ, C_SIGN, C_MEAN, C_ZERO = C_COL, C_COL + 1, C_COL + 2, C_COL + 4
TWO_PI = (6.28125, 0.0019350051879882812, 3.0199157663e-07)
FORBIDDEN = -1e4
MAGIC = 12582912.0

S_HALF, S_GNW, S_PI2, S_SUB, S_LAM = 0, 1, 2, 3, 4
S_DT = 5
S_MS, S_RSTD, S_KSQ, S_KSS, S_KN = 8, 12, 16, 20, 24
S_EG, S_ELAST, S_ELEFT, S_LEFT, S_OMS, S_ON = 28, 32, 36, 40, 44, 48
S_KB, S_KBEG, S_KDEC, S_G = 52, 56, 60, 64
S_MAX, S_NEG, S_SUM, S_REC, S_L = 16, 20, 24, 28, 32


def constants():
    s, c = np.arange(P)[:, None], np.arange(P)[None, :]
    tile = np.zeros((P, C_COL + 8), np.float32)
    tile[:, C_ID:C_ID + P] = s == c
    tile[:, C_ONE:C_ONE + P] = 1.0
    tile[:, C_UP:C_UP + P] = c >= s
    tile[:, C_LOW:C_LOW + P] = np.where(c >= s, 0.0, FORBIDDEN)
    tile[:, C_L1:C_L1 + P] = (s % 2 == 0) & (c == s + 1)
    inv = (np.float32(10000.0) ** (-np.arange(0, 64, 2, dtype=np.float32) / np.float32(64))).astype(np.float32)
    tile[:, C_FREQ] = np.tile(inv, 4)
    tile[:, C_SIGN] = np.where(np.arange(P) % 64 < 32, -1.0, 1.0)
    tile[:, C_MEAN] = 1.0 / P
    masks = np.zeros((P, LEVELS, P), np.float32)
    for n in range(LEVELS):
        b = 2 << n
        masks[:, n, :] = (s // (2 * b) == c // (2 * b)) & (s % (2 * b) < b) & (c % (2 * b) >= b)
    t = np.arange(T)
    edges = [w / (np.minimum(t + w // 2, T) - np.maximum(t - w // 2, 0)) for w in WINDOWS]
    edges = [np.concatenate([e[:EDGE], e[T - EDGE:]]) for e in edges]
    return tile, masks, np.array(edges, np.float32)


class Tile:

    def __init__(self, n0, step=0, i=0):
        self.n0, self.step, self.i = n0, step, i
        self.slot, self.raw = n0 % RING, n0 % 2
        self.before = n0 + step * i
        self.loads = n0 // 2 + (step // 2) * i

    def ahead(self):
        return Tile(self.n0 + RING, self.step, self.i)


class Stage:

    def __init__(self, tile0, tiles, base, banks, times):
        self.tile0, self.tiles, self.base, self.banks, self.times = tile0, tiles, base, banks, times

    def tile(self, t, i):
        return Tile(self.tile0 + t, self.tiles, i) if self.times > 1 else Tile(self.tile0 + t)

    def out(self, j, i):
        b = self.banks[j]
        loop = self.banks.count(b) * i if self.times > 1 else 0
        return b, self.base[b] + self.banks[:j].count(b) + loop

    def after_first(self):
        base = [n + self.banks.count(b) for b, n in enumerate(self.base)]
        return Stage(self.tile0 + self.tiles, self.tiles, base, self.banks, self.times - 1)


class Stream:
    def __init__(self):
        self.tiles, self.outs = 0, [0] * 8

    def stage(self, tiles, banks, times=1):
        s = Stage(self.tiles, tiles, tuple(self.outs), tuple(banks), times)
        self.tiles += tiles * times
        for b in range(8):
            self.outs[b] += s.banks.count(b) * times
        return s


PE_STEPS = ["kv_tokens", "g_rows", "kk_qk", "kb_rows", "x_pairs"]
DVE_STEPS = ["g_col", "kss", "decay_arg", "g_left", "kb", "kb_decay", "lower", "u_pairs", "u0", "q_g", "qk"]
ACT_STEPS = ["k_squares", "exp_decay", "exp_g", "exp_g_rows", "exp_last", "exp_left", "q_squares", "x_pairs"]
POOL_STEPS = ["k_norm"] + [f"mask{_n}" for _n in range(LEVELS)] + ["ada", "o_norm"]
for _n in range(LEVELS):
    _x = [f"x{_n}"] if _n < LEVELS - 1 else []
    PE_STEPS += [f"y{_n}"] + _x + [f"u{_n}"]
    ACT_STEPS += [f"u{_n}"]
    DVE_STEPS += [f"y{_n}"] + (["kbeg_scale", "v_beta", "k_beg"] if _n == 0 else []) + _x
    DVE_STEPS += ["kdec_scale", "k_dec"] if _n == 0 else []
PE_STEPS += ["w"]
ACT_STEPS += ["w", "o_squares", "o_hi"]
for _n in range(NC):
    PE_STEPS += [f"v_new{_n}", f"o{_n}"]
    DVE_STEPS += [f"v_new{_n}"] + ([f"state{_n}"] if _n < NC - 1 else [])
PE_STEPS += ["o_sums", "o_norm_rows"]
DVE_STEPS += ["o_sum", "o_mean", "ada", "ada_f", "o_gate", "o_scale", "o_lo"]

HEAD_FILL = {name: 1 for name in PE_STEPS if name != "w" and name not in [f"u{_n}" for _n in range(LEVELS - 1)]}
HEAD_FILL.update(kb_rows=2, x_pairs=3, o_sums=2, o_norm_rows=2)
LAST_FILL = {name: 1 for name in ["kv_tokens", "g_rows", "kk_qk", "kb_rows"] + [f"y{_n}" for _n in range(LEVELS)]}
LAST_FILL.update(x_pairs=2, o_sums=2, o_norm_rows=2)
assert sum(HEAD_FILL.values()) == 32 and sum(LAST_FILL.values()) == 16

ATT_PE = ["scores0", "v_turn", "scores1", "scores2", "scores3"] + [f"turn{_q}" for _q in range(NC)] + ["pv", "sums", "rows"]
ATT_ACT = ["exp0", "v_hi", "exp1", "exp2", "exp3"] + [f"turn{_q}" for _q in range(NC)] + ["o", "squares", "hi"]
ATT_DVE = ["max0", "neg0"]
for _n in range(NC):
    ATT_DVE += [f"max{_n + 1}", f"neg{_n + 1}"] if _n + 1 < NC else []
    ATT_DVE += [f"recip{_n}", f"lam{_n}", f"second{_n}", f"a{_n}"]
    ATT_DVE += ["v_lo"] if _n == 0 else [f"turn_lo{_n - 2}"] if _n >= 2 else []
ATT_DVE += ["turn_lo2", "turn_lo3", "mean", "scale", "lo"]



def step(steps, name, h):
    return len(steps) * h + (2 + steps.index(name))


def heads(steps, h):
    return len(steps) * h + 1


def block_kernel(nc, a, out):
    stream = Stream()
    AB = stream.stage(1, [0])
    QKVZ = stream.stage(4, [1, 0, 1, 0])
    HEAD = stream.stage(8, [0, 1] * 4, H - 1)
    LAST = stream.stage(4, [0, 1] * 2)
    GATE_B = stream.stage(4, [0, 1] * 2, 2)
    GATE = stream.stage(8, [0, 1] * 4, 2)
    WO = stream.stage(4, [0, 1, 5, 6], 2)
    UP = [stream.stage(4, [0, 1, 5, 6], UPS)]
    DOWN = [stream.stage(12, [0, 1] * 2, 2)]
    POOLW = stream.stage(2, [0, 1] * 4)
    UP.append(stream.stage(4, [0, 1, 5, 6], UPS))
    DOWN.append(stream.stage(12, [0, 1] * 2, 2))
    ATT_Q = stream.stage(3, [0, 1, 0])
    ATT_0 = stream.stage(3, [0, 1, 0])
    ATT_H = stream.stage(4, [0, 1] * 4 + [0, 1, 0], H - 2)
    ATT_7 = stream.stage(1, [0, 1] * 4)
    ATT_WO = stream.stage(1, [0, 1] * 4)
    UP.append(stream.stage(4, [0, 1, 5, 6], UPS))
    DOWN.append(stream.stage(12, [0, 1] * 2, 2))
    N_TILES = stream.tiles

    N_MIX, N_FFN, N_OUT1, N_POOL, N_FFN0, N_ATT, N_FFN1, N_OUT2 = range(8)
    SPLIT_NORMS = (N_MIX, N_FFN, N_FFN0, N_ATT, N_FFN1)
    POOL_SUMS = (N_MIX, N_FFN, N_OUT1, N_ATT, N_OUT2)
    DVE_SUMS = (N_POOL, N_FFN0, N_FFN1)
    SCALED_NORMS = (N_MIX, N_FFN, N_OUT1, N_FFN0, N_ATT, N_FFN1, N_OUT2)

    def split_base(r):
        return KD * SPLIT_NORMS.index(r)

    def scaled_base(r):
        return KD * SCALED_NORMS.index(r)

    AB_LINKS = 26

    POOL_NORMED = 2
    POOL_STEP = [POOL_NORMED + sum(n + 4 for n in range(g + 1)) for g in range(len(WINDOWS) - 1)]
    POOL_STEP.append(POOL_STEP[-1] + 2)

    ctx = ExitStack()
    with ctx:
        place = [(nc.sbuf_base + 63) // 64 * 64]

        def sb(name, shape, dt=F32, at=None):
            size = int(np.prod(shape[1:])) * 4
            off = place[0] if at is None else at
            if at is None:
                place[0] += size
            assert off + size <= nc.sbuf_usable_end, (name, off + size, nc.sbuf_usable_end)
            return nc.alloc_sbuf_tensor_at(name, list(shape), dt, offset=off)

        raw = sb("raw", [P, 2, KD, P])
        w_hi = sb("w_hi", [P, RING, KD, P], F32R)
        w_lo = sb("w_lo", [P, RING, KD, P], F32R)
        x = sb("x", [P, KD, T])
        h_hi = sb("h_hi", [P, KD, T], F32R)
        h_lo = sb("h_lo", [P, KD, T], F32R)
        cst = sb("cst", [P, C_COL + 8])
        masks = sb("masks", [P, LEVELS, P])
        vec = sb("vec", [P, 4 * P])
        mod = sb("mod", [P, 64])
        wsc = sb("wsc", [P, 3, KD])
        cact = sb("cact", [P, 2, KD])
        small = sb("small", [P, 72])
        edges = sb("edges", [P, len(WINDOWS), 2 * EDGE])
        alog = sb("alog", [P, H])
        state = sb("state", [P, P])
        g_tok = sb("g_tok", [P, NC, 16])
        b_tok = sb("b_tok", [P, NC, 16])
        bh_tok = sb("bh_tok", [P, NC, 16])
        work = place[0]
        sq_sum = sb("sq_sum", [P, T])
        sq_tmp = sb("sq_tmp", [P, T])
        tmp = sb("tmp", [P, 6, T])
        wide = place[0]
        end = nc.sbuf_usable_end // 64 * 64

        ident, ones = cst[:, C_ID:C_ID + P], cst[:, C_ONE:C_ONE + P]
        one_col = cst[:, C_ONE:C_ONE + 1]

        x_tok = sb("x_tok", [P, NC, D], at=wide)
        pack = sb("pack", [P, 4, P], at=wide + 16384)
        ada0 = sb("ada0", [P, KD, 2 * D], at=wide + 18432)
        ada0_sum = sb("ada0_sum", [P, 2 * D], at=wide + 18432 + 65536)
        ab_f = sb("ab_f", [P, T], at=wide)
        ab = [sb(f"ab{n}", [P, NC, 2 * H], at=wide + 2048 + 256 * n) for n in range(7)]
        og_hi = sb("og_hi", [P, H, T], F32R, at=end - 65536)
        og_lo = sb("og_lo", [P, H, T], F32R, at=end - 49152)
        sc_out = sb("sc_out", [P, KD, T], at=end - 32768)
        ga_t = sb("ga_t", [P, KD, T], at=end - 16384)
        names = ["q_s", "k_s", "v_s", "z_g", "th", "cc", "dec", "low_d", "low", "qk_t", "q_g", "u_t", "x_t",
                 "y_t", "k_beg", "k_dec", "v_b", "q_sq", "dia"]
        gd = {n: sb("gd_" + n, [P, T], at=work + 2048 * j) for j, n in enumerate(names)}
        gd["cx"] = gd["th"]
        low_part = (gd["low_d"], gd["dia"])
        ada_w = sb("ada_w", [P, 2, KD // 2, P], at=work + 2048 * len(names))
        ada_s = sb("ada_s", [P, 6, P], at=work + 2048 * len(names) + 4096)
        assert work + 2048 * len(names) + 4096 + 3072 <= end - 65536
        sc_hi = sb("sc_hi", [P, KD, T], F32R, at=work)
        sc_lo = sb("sc_lo", [P, KD, T], F32R, at=work + 16384)
        gb_t = sb("gb_t", [P, KD, T], at=end - 32768)
        yb = sb("yb", [P, T], at=work + 32768)
        act_hi = sb("act_hi", [P, KF, T], F32R, at=wide)
        act_lo = sb("act_lo", [P, KF, T], F32R, at=wide + 2048 * KF)
        pairs_at = [wide + 4224 * n for n in range(6)]
        win = [sb(f"win{n}", [P, 2, T + 2 * EDGE], at=pairs_at[n]) for n in range(3)]
        win_l = [sb(f"win_l{n}", [P, 2, T + 2 * EDGE], at=pairs_at[3 + n]) for n in range(3)]
        pool_d = sb("pool_d", [P, KD, T], at=wide + 25600)
        p_hi = sb("p_hi", [P, KD, T], F32R, at=wide + 41984)
        p_lo = sb("p_lo", [P, KD, T], F32R, at=wide + 58368)
        names = ["swap", "rot", "v_f", "o_s", "o_n", "o_sq"]
        at = {n: sb("at_" + n, [P, T], at=wide + 2048 * j) for j, n in enumerate(names)}
        at.update({n: sb("at_" + n, [P, T], at=wide + 4096 * KF + 2048 * j) for j, n in enumerate(("cos", "sin"))})
        pos_i = sb("pos_i", [P, T], I32, at=wide + 4096 * KF + 4096)
        pos_f = sb("pos_f", [P, T], at=wide + 4096 * KF + 4096)
        split_names = ["q_hi", "q_lo", "k_hi", "k_lo", "v_hi", "v_lo", "ao_hi", "ao_lo"]
        at.update({n: sb("at_" + n, [P, T], F32R, at=wide + 2048 * (11 + j)) for j, n in enumerate(split_names)})
        prob = sb("prob", [P, 2, 2, T], at=wide + 2048 * 19)
        a_sb = sb("a_sb", [P, 2, T], at=wide + 2048 * 23)
        at_hi = sb("a_t_hi", [P, NC, T], F32R, at=wide + 2048 * 25)
        at_lo = sb("a_t_lo", [P, NC, T], F32R, at=wide + 2048 * 29)
        wo_s = sb("wo_s", [P, 4, T], at=wide + 2048 * 33)
        lam_in = sb("lam_in", [P, 4, 64], at=wide + 2048 * 37)
        o_tok = sb("o_tok", [P, NC, D], at=wide)

        ps = ctx.enter_context(nc.psum_tensor("ps", [P, 8, T], F32))

        def bank(b):
            return ps[:, b, :]

        def chunks(v):
            return v.rearrange("p (n c) -> p n c", n=NC)

        def part(v, n):
            return v[:, P * n:P * n + P]

        def spread(col):
            return col.unsqueeze(2).to_broadcast([P, NC, P])

        def every(tile128):
            return tile128.unsqueeze(1).to_broadcast([P, NC, P])

        def col4(c):
            return small[:, c:c + NC]

        def dyn(buf, m):
            if isinstance(m, int):
                return buf[:, m]
            return buf[:, bass.ds(m, 1), :].rearrange("p o t -> p (o t)")

        def col(buf, c):
            return buf[:, c:c + 1] if isinstance(c, int) else buf[:, bass.ds(c, 1)]

        def head_cols(tok, c):
            if isinstance(c, int):
                return tok[:, :, c]
            return tok[:, :, bass.ds(c, 1)].rearrange("p n o -> p (n o)")

        def sem(name):
            return ctx.enter_context(nc.semaphore(name))

        w_landed = [sem("w_landed0"), sem("w_landed1")]
        hi_ready, lo_ready = sem("hi_ready"), sem("lo_ready")
        tile_done = sem("tile_done")
        out_used = {b: sem(f"out_used{b}") for b in (0, 1, 5, 6)}
        cst_in, pack_in, x_in, ab_in = sem("cst_in"), sem("pack_in"), sem("x_in"), sem("ab_in")
        ada_in = [sem(f"ada_in{n}") for n in range(4)]
        edges_in, pos_in, lam_in_s, out_done = sem("edges_in"), sem("pos_in"), sem("lam_in_s"), sem("out_done")
        pro_pe, pro_act, pro_dve, pro_pool = sem("pro_pe"), sem("pro_act"), sem("pro_dve"), sem("pro_pool")
        x_even, x_odd = sem("x_even"), sem("x_odd")
        ada0_own, ab_act, ab_dve, ab_pe = sem("ada0_own"), sem("ab_act"), sem("ab_dve"), sem("ab_pe")
        mod_ready = sem("mod_ready")
        sq_own, sq_done = sem("sq_own"), sem("sq_done")
        fsq_act, fsq_add = sem("fsq_act"), sem("fsq_add")
        n_pe, n_dve, n_pool = sem("n_pe"), sem("n_dve"), sem("n_pool")
        n_t, n_ht, n_hi, h_ready = sem("n_t"), sem("n_ht"), sem("n_hi"), sem("h_ready")
        g_pe, g_dve, g_act, g_pool = sem("g_pe"), sem("g_dve"), sem("g_act"), sem("g_pool")
        cv_act, cv_dve, sc_dve = sem("cv_act"), sem("cv_dve"), sem("sc_dve")
        ada_land = [sem("ada_land0"), sem("ada_land1")]
        ada_own = sem("ada_own")
        sc_split, mixed, mix_hi, mix_lo = sem("sc_split"), sem("mixed"), sem("mix_hi"), sem("mix_lo")
        f_act, f_dve, f_hi, f_lo = sem("f_act"), sem("f_dve"), sem("f_hi"), sem("f_lo")
        pl_dve, pl_pool, pl_hi, pl_lo = sem("pl_dve"), sem("pl_pool"), sem("pl_hi"), sem("pl_lo")
        t_pe, t_dve, t_act, t_pool = sem("t_pe"), sem("t_dve"), sem("t_act"), sem("t_pool")
        rp_pe, rp_act, rp_dve, wo_add = sem("rp_pe"), sem("rp_act"), sem("rp_dve"), sem("wo_add")
        fin_pe, fin_act = sem("fin_pe"), sem("fin_act")
        wo_out, pl_out = sem("wo_out"), sem("pl_out")

        def rows(w):
            return w.rearrange("(k p) c -> p k c", p=P)

        w_in, w_ada, w_ada_f = rows(a["w_in"][0]), rows(a["w_ada"][0]), rows(a["w_ada_f"])
        w_gdn, w_sc, w_o = rows(a["w_gdn_proj"][0]), rows(a["w_sc_out"][0]), rows(a["w_o"][0])
        w_up = [rows(w) for w in (a["w_ffn_in"][0], a["ffn_w_up_2"][0], a["ffn_w_up_2"][1])]
        w_dn = [rows(w) for w in (a["w_ffn_out"][0], a["ffn_w_down_2"][0], a["ffn_w_down_2"][1])]
        pool_w = a["pool_w_2"][0].rearrange("g (k p) c -> p g k c", p=P)
        w_qkv, w_ao = rows(a["diff_w_qkv_2"][0]), a["diff_w_o_2"][0]
        out_t = out[0].rearrange("(n p) d -> p n d", p=P)

        ROPE_SETUP = 12

        def roped(n):
            return ROPE_SETUP + 3 * n

        def double(engine, bufs, n):
            src, dst = bufs[0] if n == 0 else bufs[1 + (n - 1) % 2], bufs[1 + n % 2]
            back, ahead, cut = (1, 0, 1) if n == 0 else (1 << (n - 1), 1 << (n - 1), 1 << n)
            lo, hi = cut, T + 2 * EDGE - cut
            return engine.tensor_tensor(dst[:, :, lo:hi], src[:, :, lo - back:hi - back], src[:, :, lo + ahead:hi + ahead], ADD)

        block = ctx.enter_context(nc.Block())

        @block.sync
        def _(sp):
            def load(tile, src, blocks=KD):
                if tile.n0 >= 2:
                    sp.wait_ge(lo_ready, tile.before - 1)
                sp.dma_start(raw[:, tile.raw, 0:blocks, 0:src.shape[-1]], src).then_inc(w_landed[tile.raw], 16)

            def cols(w, start, k0=0, k=KD):
                return w[:, k0:k0 + k, bass.ds(start, P)]

            sp.dma_start(x_tok[:], a["x"][0].rearrange("(n p) d -> p n d", p=P)).then_inc(x_in, 16)
            sp.dma_start(edges[:], a["const_edges"].rearrange("(o g) t -> o g t", o=1).to_broadcast([P, 4, 2 * EDGE]))\
              .then_inc(edges_in, 16)
            sp.wait_ge(pack_in, 16 * 17)
            for n in range(4):
                sp.dma_start(ada0[:, :, T * n:T * n + T], w_ada[:, :, T * n:T * n + T]).then_inc(ada_in[n], 16)
            sp.wait_ge(pro_dve, 1)
            load(AB.tile(0, 0), w_in[:, :, AB0:AB0 + 2 * H])
            for t, c in enumerate((Q0, K0, V0, Z0)):
                load(QKVZ.tile(t, 0), cols(w_in, c))

            with sp.Fori(0, H - 1) as i:
                for t, c in enumerate((SCC0, Q0 + P, K0 + P, V0 + P, SCX0, SCB0, GA0, Z0 + P)):
                    load(HEAD.tile(t, i), cols(w_in, i * P + c))
            for t, c in enumerate((SCC0, SCX0, SCB0, GA0)):
                load(LAST.tile(t, 0), cols(w_in, (H - 1) * P + c))
            with sp.Fori(0, 2) as i:
                for m in range(4):
                    load(GATE_B.tile(m, i), cols(w_in, i * (4 * P) + (GB0 + m * P)))
            with sp.Fori(0, 2) as i:
                for m in range(4):
                    load(GATE.tile(2 * m, i), cols(w_sc, (i + 1) * (4 * P) + (m - 4) * P))
                    load(GATE.tile(2 * m + 1, i), cols(w_gdn, (i + 1) * (4 * P) + (m - 4) * P))
            with sp.Fori(0, 2) as i:
                for m in range(4):
                    load(WO.tile(m, i), cols(w_o, i * (4 * P) + m * P))

            def feed_forward(f):
                with sp.Fori(0, UPS) as i:
                    for j in range(2):
                        load(UP[f].tile(2 * j, i), cols(w_up[f], i * (2 * P) + j * P))
                        load(UP[f].tile(2 * j + 1, i), cols(w_up[f], i * (2 * P) + (FF + j * P)))
                with sp.Fori(0, 2) as i:
                    for m in range(4):
                        for c in range(3):
                            k = min(KD, KF - KD * c)
                            load(DOWN[f].tile(3 * m + c, i), cols(w_dn[f], i * (4 * P) + m * P, KD * c, k), k)

            feed_forward(0)
            for t in range(2):
                tile = POOLW.tile(t, 0)
                sp.wait_ge(lo_ready, tile.before - 1)
                dst = raw[:, tile.raw].rearrange("p (g k e) c -> p (g k) (e c)", g=2, k=2)
                sp.dma_start(dst, pool_w[:, 2 * t:2 * t + 2].rearrange("p g k c -> p (g k) c"))\
                  .then_inc(w_landed[tile.raw], 16)
            sp.dma_start(pos_i[0:1, :], a["positions_2"].rearrange("(o t) -> o t", o=1)).then_inc(pos_in, 16)
            feed_forward(1)
            for t, which in enumerate((1, 0, 2)):
                load(ATT_Q.tile(t, 0), cols(w_qkv, which * D))
            sp.wait_ge(tile_done, ATT_Q.tile0)
            for n, name in enumerate(("diff_lam_q1_2", "diff_lam_k1_2", "diff_lam_q2_2", "diff_lam_k2_2")):
                sp.dma_start(lam_in[0:1, n, :], a[name]).then_inc(lam_in_s, 16)

            def wo_rows(stage, i, h):
                tile = stage.tile(0, i)
                sp.wait_ge(lo_ready, tile.before - 1)
                sp.dma_start(raw[:, tile.raw], w_ao[bass.ds(h * P, P), :].rearrange("p (m c) -> p m c", c=P))\
                  .then_inc(w_landed[tile.raw], 16)

            for t, which in enumerate((1, 0, 2)):
                load(ATT_0.tile(t, 0), cols(w_qkv, P + which * D))
            with sp.Fori(0, H - 2) as i:
                wo_rows(ATT_H, i, i)
                for t, which in enumerate((1, 0, 2)):
                    load(ATT_H.tile(1 + t, i), cols(w_qkv, i * P + (which * D + 2 * P)))
            wo_rows(ATT_7, 0, H - 2)
            wo_rows(ATT_WO, 0, H - 1)
            feed_forward(2)
            for m in range(KD):
                sp.wait_ge(fin_act, m + 1)
                sp.dma_start(out_t[:, :, m * P:m * P + P], o_tok[:, :, m * P:m * P + P]).then_inc(out_done, 16)
            sp.wait_ge(out_done, 16 * KD)

        @block.gpsimd
        def _(pool):
            minus_half = small[:, S_HALF:S_HALF + 1].to_broadcast([P, NC])
            done = {"own": 0, "sum": 0}

            def clear_sum():
                nc.gpsimd.memset(sq_sum[:], 0.0).then_inc(sq_own, 1)
                done["own"] += 1
                pool.wait_ge(sq_own, done["own"])

            def add_square(xm, own, summed):
                if not (isinstance(summed, int) and summed == 0):
                    pool.wait_ge(sq_done, summed)
                nc.gpsimd.tensor_tensor(sq_tmp[:], xm, xm, MULT).then_inc(sq_own, 1)
                pool.wait_ge(sq_own, own + 1)
                nc.gpsimd.tensor_tensor(sq_sum[:], sq_sum[:], sq_tmp[:], ADD).then_inc(sq_done, 1)

            def sum_in_loop(stage):
                clear_sum()
                with pool.Fori(0, 2) as i:
                    for m in range(4):
                        b, before = stage.out(m, i)
                        pool.wait_ge(out_used[b], before + 1)
                        add_square(dyn(x, 4 * i + m), 4 * i + (done["own"] + m), 4 * i + (done["sum"] + m))
                done["own"] += KD
                done["sum"] += KD

            def sum_flat(ready):
                clear_sum()
                for m in range(KD):
                    ready(m)
                    add_square(x[:, m], done["own"], done["sum"])
                    done["own"] += 1
                    done["sum"] += 1

            def factor(r):
                pool.wait_ge(n_dve, r + 1)
                nc.gpsimd.tensor_tensor(col4(S_RSTD), col4(S_MS), minus_half, ALU.pow).then_inc(n_pool, 1)

            pool.wait_ge(pro_dve, 2)
            nc.gpsimd.memset(small[:, S_HALF:S_HALF + 1], -0.5).then_inc(pro_pool, 1)
            pool.wait_ge(pro_pool, 1)
            sum_flat(lambda m: pool.wait_ge(x_odd if m % 2 else x_even, m // 2 + 1))
            factor(N_MIX)

            def head(h):
                own = [42 * h + 1]

                def ada_load(j, half):
                    ks = slice(4 * half, 4 * half + 4)
                    src = w_ada[:, ks, bass.ds(h * (4 * P) + (2 * D + j * P), P)] if j < 4 else \
                        w_ada_f[:, ks, bass.ds(h * (2 * P) + (j - 4) * P, P)]
                    nc.gpsimd.dma_start(ada_w[:, half], src).then_inc(ada_land[half], 16)

                def add(dst, a, b, op=ADD):
                    nc.gpsimd.tensor_tensor(dst, a, b, op).then_inc(ada_own, 1)
                    own[0] += 1
                    pool.wait_ge(ada_own, own[0])

                pool.wait_ge(ada_own, own[0])
                ada_load(0, 0)
                ada_load(0, 1)
                pool.wait_ge(g_dve, step(DVE_STEPS, "kss", h))
                nc.gpsimd.tensor_tensor(col4(S_KN), col4(S_KSS), minus_half, ALU.pow).then_inc(g_pool, 1)
                def modulation(j, half):
                    w = ada_w[:, half]
                    pool.wait_ge(ada_land[half], 96 * h + 16 * (j + 1))
                    add(w, w, cact[:, 1, 4 * half:4 * half + 4].unsqueeze(2).to_broadcast([P, 4, P]), MULT)
                    add(w[:, 0:2], w[:, 0:2], w[:, 2:4])
                    add(w[:, 0] if half else ada_s[:, j], w[:, 0], w[:, 1])
                    if half:
                        add(ada_s[:, j], ada_s[:, j], w[:, 0])
                    if j < 5:
                        ada_load(j + 1, half)

                pool.wait_ge(g_pe, heads(PE_STEPS, h))
                pool.wait_ge(g_dve, step(DVE_STEPS, "lower", h))
                for n in range(LEVELS):
                    if n >= 2:
                        pool.wait_ge(g_pe, step(PE_STEPS, f"y{n - 2}", h))
                    nc.gpsimd.tensor_tensor(chunks(low_part[n % 2][:]), chunks(gd["low"][:]), every(masks[:, n]), MULT)\
                      .then_inc(g_pool, 1)
                    if n >= 1:
                        modulation((n - 1) // 2, (n - 1) % 2)
                for n in range(LEVELS - 1, 12):
                    modulation(n // 2, n % 2)
                pool.sem_inc(g_pool, 1)
                pool.wait_ge(g_dve, step(DVE_STEPS, "o_mean", h))
                nc.gpsimd.tensor_tensor(col4(S_ON), col4(S_OMS), minus_half, ALU.pow).then_inc(g_pool, 1)

            pool.wait_ge(ab_dve, AB_LINKS)
            pool.sem_inc(g_pool, 1)
            pool.sem_inc(ada_own, 1)
            with pool.Fori(0, H - 1) as h:
                head(h)
            head(H - 1)
            pool.wait_ge(mixed, KD)
            pool.wait_ge(mix_lo, KD)
            sum_in_loop(WO)
            factor(N_FFN)
            sum_in_loop(DOWN[0])
            factor(N_OUT1)
            nc.gpsimd.memset(win_l[0][:], 0.0).then_inc(pl_pool, 1)
            factor(N_POOL)
            pool.wait_ge(pl_dve, POOL_NORMED)
            for n in range(len(WINDOWS)):
                pool.wait_ge(pl_pool, n + 1)
                double(nc.gpsimd, win_l, n).then_inc(pl_pool, 1)
            factor(N_FFN0)
            sum_in_loop(DOWN[1])
            factor(N_ATT)

            def att_head(h):
                pool.wait_ge(t_dve, step(ATT_DVE, "mean", h))
                nc.gpsimd.tensor_tensor(col4(S_ON), col4(S_OMS), minus_half, ALU.pow).then_inc(t_pool, 1)

            def add_projection(stage, i, h):
                for m in range(KD):
                    b, before = stage.out(m, i)
                    pool.wait_ge(out_used[b], before + 1)
                    nc.gpsimd.tensor_tensor(x[:, m], x[:, m], wo_s[:, m % 4], ADD).then_inc(wo_add, 1)

            pool.sem_inc(wo_add, 4)
            att_head(0)
            with pool.Fori(0, H - 2) as i:
                add_projection(ATT_H, i, i)
                att_head(i + 1)
            add_projection(ATT_7, 0, H - 2)
            att_head(H - 1)
            factor(N_FFN1)
            sum_in_loop(DOWN[2])
            factor(N_OUT2)

        @block.scalar
        def _(act):
            def split(tile):
                if isinstance(tile.before, int) and tile.before >= N_TILES:
                    return
                act.wait_ge(w_landed[tile.raw], 16 * tile.loads + 16)
                if tile.n0 >= RING:
                    act.wait_ge(tile_done, tile.before - 3)
                nc.scalar.activation(w_hi[:, tile.slot], raw[:, tile.raw], ACT.Copy).then_inc(hi_ready, 1)

            def next_tile(stage, t, i):
                tile = stage.tile(t, i)
                split(tile.ahead())
                act.wait_ge(tile_done, tile.before + 1)
                return stage.out(t, i)

            def normed(r, scale, shift):
                base = scaled_base(r)
                for m in range(KD):
                    act.wait_ge(n_t, base + m + 1)
                    dst = x[:, m] if r == N_OUT1 else tmp[:, 2 + m % 2]
                    if m >= 2 and r in SPLIT_NORMS:
                        act.wait_ge(h_ready, split_base(r) + m - 1)
                    nc.scalar.activation(dst, tmp[:, m % 2], ACT.Identity, bias=shift(m), scale=scale(m)).then_inc(n_ht, 1)
                    if r in SPLIT_NORMS:
                        act.wait_ge(n_ht, base + m + 1)
                        nc.scalar.activation(h_hi[:, m], dst, ACT.Copy).then_inc(n_hi, 1)
                    if r == N_OUT1 and m:
                        act.wait_ge(n_ht, base + m)
                        square(N_POOL, m - 1)
                if r == N_OUT1:
                    act.wait_ge(n_ht, base + KD)
                    square(N_POOL, KD - 1)

            def normed_hi(r):
                for m in range(KD):
                    act.wait_ge(n_ht, scaled_base(r) + m + 1)
                    nc.scalar.activation(h_hi[:, m], tmp[:, 2 + m % 4], ACT.Copy).then_inc(n_hi, 1)

            def square(r, m):
                if m >= 4:
                    act.wait_ge(fsq_add, (KD - 1) * DVE_SUMS.index(r) + max(1, m - 4))
                nc.scalar.activation(tmp[:, 2 + m % 4], x[:, m], ACT.Square).then_inc(fsq_act, 1)

            def output(m):
                act.wait_ge(fin_pe, m + 1)
                nc.scalar.activation(o_tok[:, :, P * m:P * m + P], chunks(bank(4 + m % 2)), ACT.Copy).then_inc(fin_act, 1)

            act.dma_start(cst[:], a["const_tile"]).then_inc(cst_in, 16)
            act.dma_start(masks[:], a["const_masks"]).then_inc(cst_in, 16)

            def by_tile(v):
                return v.rearrange("(r p) -> r p", p=P)

            def by_row_tile(v):
                return v.rearrange("j (r p) -> (j r) p", p=P)

            for first, src in ((V_BADA, by_tile(a["b_ada"][0])), (V_BADAF, by_tile(a["b_ada_f"])),
                               (V_N1, by_tile(a["norm1_w"][0])), (V_N2, by_tile(a["norm2_w"][0])),
                               (V_NF, by_tile(a["normf_w"])), (V_C, by_tile(a["c"][0])),
                               (V_MIX, by_row_tile(a["mix_norm_2"])), (V_PSC, by_tile(a["pool_scale_2"][0])),
                               (V_FIN, by_tile(a["final_norm_2"])), (V_CONV, by_row_tile(a["gdn_conv_w"][0])),
                               (V_SCONV, by_row_tile(a["sc_conv_w"][0])), (V_GNW, a["gdn_norm_w"]),
                               (V_SUB, a["diff_subln_2"]), (V_FCW[0], by_row_tile(a["ffn_conv_w_2"][0])),
                               (V_FCB, by_row_tile(a["ffn_conv_b_2"])), (V_FFN, by_row_tile(a["ffn_norm_2"])),
                               (V_FCW[1], by_row_tile(a["ffn_conv_w_2"][1]))):
                act.dma_start(pack[first % P:first % P + src.shape[0], first // P, :], src).then_inc(pack_in, 16)
            act.wait_ge(pro_dve, 2)
            act.dma_start(small[0:H, S_DT:S_DT + 1], a["gdn_dt_bias"][0].rearrange("(p o) -> p o", o=1)).then_inc(ab_in, 16)
            act.dma_start(alog[:], a["gdn_a_log"].to_broadcast([P, H])).then_inc(ab_in, 16)
            for m in range(1, KD, 2):
                act.wait_ge(pro_pe, m + 1)
                nc.scalar.activation(x[:, m], bank(m), ACT.Copy).then_inc(x_odd, 1)
            act.wait_ge(pro_dve, 3)
            nc.scalar.activation(cact[:, 0], vec[:, V_C:V_C + KD], ACT.Tanh, scale=0.5).then_inc(pro_act, 1)
            split(Tile(0))
            split(Tile(1))
            act.wait_ge(mod_ready, 1)
            normed(N_MIX, lambda m: col(wsc[:, 0], m), lambda m: col(mod, SH1 + m))
            split(Tile(2))
            split(Tile(3))

            split(AB.tile(0, 0).ahead())
            act.wait_ge(ab_dve, 1)
            nc.scalar.activation(ab[1][:], ab[0][:], ACT.Abs).then_inc(ab_act, 1)
            act.wait_ge(ab_act, 1)
            nc.scalar.activation(ab[1][:], ab[1][:], ACT.Exp, scale=-1.0).then_inc(ab_act, 1)
            act.wait_ge(ab_in, 32)
            nc.scalar.activation(alog[:], alog[:], ACT.Exp).then_inc(ab_act, 1)

            def conv_tap(stage, t, i, n, hh):
                b, before = stage.out(t, i)
                act.wait_ge(tile_done, stage.tile(t, i).before + 1)
                nc.scalar.activation(conv_bufs[n][:], bank(b), ACT.Copy, scale=col(vec, hh + (V_CONV + 72 + 8 * n)))\
                  .then_inc(cv_act, 1)

            def conv_tanh(stage, t, i, n, hh):
                b, before = stage.out(t, i)
                act.wait_ge(out_used[b], before + 1)
                if not (isinstance(hh, int) and hh == 0 and n == 0):
                    act.wait_ge(cv_dve, 10 * hh + 3 * n)
                nc.scalar.activation(gd["th"][:], conv_bufs[n][:], ACT.Tanh, scale=0.5).then_inc(cv_act, 1)

            def z_tile(stage, t, i, hh):
                b, before = stage.out(t, i)
                act.wait_ge(tile_done, stage.tile(t, i).before + 1)
                nc.scalar.activation(gd["z_g"][:], bank(b), ACT.Copy, scale=small[:, S_GNW:S_GNW + 1]).then_inc(cv_act, 1)
                act.wait_ge(cv_dve, 10 * hh + 9)
                nc.scalar.activation(gd["th"][:], bank(b), ACT.Tanh, scale=0.5).then_inc(out_used[b], 1)

            conv_bufs = [gd[n] for n in ("q_s", "k_s", "v_s")]
            act.wait_ge(ab_dve, AB_LINKS)
            act.sem_inc(g_act, 1)
            for n in range(3):
                split(QKVZ.tile(n, 0).ahead())
                conv_tap(QKVZ, n, 0, n, 0)
                conv_tanh(QKVZ, n, 0, n, 0)
            split(QKVZ.tile(3, 0).ahead())
            z_tile(QKVZ, 3, 0, 0)

            def head(stage, i, h):
                more = stage is HEAD

                def ahead(t):
                    split(stage.tile(t, i).ahead())

                def after_pe(name):
                    act.wait_ge(g_pe, step(PE_STEPS, name, h))

                def after_dve(name):
                    act.wait_ge(g_dve, step(DVE_STEPS, name, h))

                after_pe("kv_tokens")
                for n in range(NC):
                    k_sq = nc.scalar.activation(part(gd["y_t"], n), part(bank(2), n), ACT.Square,
                                                accum_out=small[:, S_KSQ + n:S_KSQ + n + 1])
                k_sq.then_inc(g_act, 1)
                after_dve("decay_arg")
                nc.scalar.activation(gd["dec"][:], gd["dec"][:], ACT.Exp).then_inc(g_act, 1)
                nc.scalar.activation(col4(S_EG), head_cols(g_tok, h), ACT.Exp).then_inc(g_act, 1)
                after_dve("g_left")
                nc.scalar.activation(gd["y_t"][:], bank(4), ACT.Exp).then_inc(g_act, 1)
                nc.scalar.activation(col4(S_ELAST), chunks(bank(4))[:, :, P - 1], ACT.Exp).then_inc(g_act, 1)
                nc.scalar.activation(col4(S_ELEFT), col4(S_LEFT), ACT.Exp).then_inc(g_act, 1)
                nc.scalar.activation(gd["q_sq"][:], gd["q_s"][:], ACT.Square, scale=P * 1e-3).then_inc(g_act, 1)
                ahead(0)
                b, before = stage.out(0, i)
                act.wait_ge(tile_done, stage.tile(0, i).before + 1)
                nc.scalar.activation(gd["cc"][:], bank(b), ACT.Copy).then_inc(out_used[b], 1)
                after_pe("x_pairs")
                nc.scalar.activation(gd["x_t"][:], bank(4), ACT.Copy).then_inc(g_act, 1)
                for n in range(LEVELS):
                    after_pe(f"u{n}")
                    nc.scalar.activation(gd["u_t"][:], bank(6), ACT.Copy).then_inc(g_act, 1)
                    if more and n == 0:
                        after_pe("kk_qk")
                        after_dve("q_g")
                        conv_tap(stage, 1, i, 0, h + 1)
                        ahead(1)
                    if more and n == 1:
                        conv_tanh(stage, 1, i, 0, h + 1)
                        conv_tap(stage, 2, i, 1, h + 1)
                        ahead(2)
                    if more and n == 2:
                        conv_tanh(stage, 2, i, 1, h + 1)
                    if more and n == 3:
                        conv_tap(stage, 3, i, 2, h + 1)
                        ahead(3)
                    if more and n == 4:
                        conv_tanh(stage, 3, i, 2, h + 1)
                        ahead(4)
                    if not more and n == 1:
                        ahead(1)
                after_pe("w")
                nc.scalar.activation(gd["x_t"][:], bank(7), ACT.Copy).then_inc(g_act, 1)
                ahead(5 if more else 2)
                after_pe(f"o{NC - 1}")
                nc.scalar.activation(gd["dec"][:], bank(3), ACT.Square).then_inc(g_act, 1)
                if more:
                    ahead(6)
                    b, before = stage.out(6, i)
                    act.wait_ge(tile_done, stage.tile(6, i).before + 1)
                    nc.scalar.activation(dyn(ga_t, h), bank(b), ACT.Tanh, scale=0.5).then_inc(out_used[b], 1)
                after_dve("o_scale")
                nc.scalar.activation(dyn(og_hi, h), gd["low_d"][:], ACT.Copy).then_inc(g_act, 1)
                if more:
                    ahead(7)
                    after_dve("o_gate")
                    act.wait_ge(sc_dve, 3 * h + 3)
                    z_tile(stage, 7, i, h + 1)
                else:
                    b, before = next_tile(stage, 3, i)
                    nc.scalar.activation(dyn(ga_t, h), bank(b), ACT.Tanh, scale=0.5).then_inc(out_used[b], 1)

            with act.Fori(0, H - 1) as h:
                head(HEAD, h, h)
            head(LAST, 0, H - 1)

            act.wait_ge(out_used[LAST.out(2, 0)[0]], LAST.out(2, 0)[1] + 1)
            act.wait_ge(g_dve, heads(DVE_STEPS, H))
            nc.scalar.activation(sc_hi[:], sc_out[:], ACT.Copy).then_inc(sc_split, 1)
            act.wait_ge(sc_split, 2)
            with act.Fori(0, 2) as i:
                for t in range(4):
                    b, before = next_tile(GATE_B, t, i)
                    nc.scalar.activation(dyn(gb_t, 4 * i + t), bank(b), ACT.Tanh, scale=0.5).then_inc(out_used[b], 1)
            with act.Fori(0, 2) as i:
                for m in range(4):
                    split(GATE.tile(2 * m, i).ahead())
                    split(GATE.tile(2 * m + 1, i).ahead())
                    act.wait_ge(mixed, 4 * i + (m + 1))
                    nc.scalar.activation(dyn(h_hi, 4 * i + m), dyn(ga_t, 4 * i + m), ACT.Copy).then_inc(mix_hi, 1)
            with act.Fori(0, 2) as i:
                for t in range(4):
                    split(WO.tile(t, i).ahead())

            def rope_tables():
                act.wait_ge(rp_dve, 8)
                nc.scalar.activation(at["sin"][:], tmp[:, 0], ACT.Sin).then_inc(rp_act, 1)
                nc.scalar.activation(tmp[:, 1], tmp[:, 0], ACT.Abs).then_inc(rp_act, 1)
                act.wait_ge(rp_act, 2)
                nc.scalar.activation(at["cos"][:], tmp[:, 1], ACT.Sin, bias=small[:, S_PI2:S_PI2 + 1], scale=-1.0)\
                  .then_inc(rp_act, 1)

            def feed_forward(f):
                base = 0 if f == 0 else 2 * UPS + 4 * UPS * (f - 1)
                with act.Fori(0, UPS) as i:
                    for j in range(2):
                        b, before = next_tile(UP[f], 2 * j, i)
                        if f == 0:
                            nc.scalar.activation(tmp[:, j], bank(b), ACT.Tanh, scale=0.5).then_inc(f_act, 1)
                        else:
                            nc.scalar.activation(tmp[:, 2 + j], bank(b), ACT.Identity,
                                                 bias=col(vec, 2 * i + (V_FCB + KF * (f - 1) + j)),
                                                 scale=col(vec, 2 * i + (V_FCW[f - 1] + KF + j))).then_inc(f_act, 1)
                            act.wait_ge(out_used[b], before + 1)
                            nc.scalar.activation(tmp[:, j], tmp[:, 2 + j], ACT.Gelu).then_inc(f_act, 1)
                        split(UP[f].tile(2 * j + 1, i).ahead())
                        b, before = UP[f].out(2 * j + 1, i)
                        act.wait_ge(out_used[b], before + 1)
                        nc.scalar.activation(dyn(act_hi, 2 * i + j), tmp[:, 4 + j], ACT.Copy).then_inc(f_hi, 1)
                if f == 1:
                    rope_tables()
                if f == 2:
                    for n in range(24):
                        split(DOWN[f].tile(n % 12, n // 12).ahead())
                else:
                    with act.Fori(0, 2) as i:
                        for t in range(12):
                            split(DOWN[f].tile(t, i).ahead())

            act.wait_ge(mod_ready, 2)
            normed(N_FFN, lambda m: col(wsc[:, 1], m), lambda m: col(mod, SH2 + m))
            feed_forward(0)
            normed(N_OUT1, lambda m: col(wsc[:, 2], m), lambda m: col(mod, SHF + m))

            for m in range(KD):
                act.wait_ge(pl_dve, POOL_STEP[m // 2])
                nc.scalar.activation(p_hi[:, m], pool_d[:, m], ACT.Copy, scale=col(vec, V_MIX + m)).then_inc(pl_hi, 1)
            for m in range(KD):
                b, before = POOLW.out(m, 0)
                act.wait_ge(out_used[b], before + 1)
                square(N_FFN0, m)
            for t in range(2):
                split(POOLW.tile(t, 0).ahead())
            normed_hi(N_FFN0)
            feed_forward(1)

            normed_hi(N_ATT)
            act.wait_ge(rp_dve, 11)
            nc.scalar.activation(small[0:1, S_NEG:S_NEG + 2], small[0:1, S_MAX:S_MAX + 2], ACT.Exp).then_inc(rp_act, 1)

            def rope_tile(stage, t, j, i, n, name):
                tile = stage.tile(t, i)
                split(tile.ahead())
                act.wait_ge(tile_done, tile.before + 1)
                b, before = stage.out(j, i)
                act.wait_ge(rp_dve, roped(n))
                for q in range(4):
                    swapped = nc.scalar.activation(at["swap"][32 * q:32 * q + 32], ps[32 * (q ^ 1):32 * (q ^ 1) + 32, b, :],
                                                   ACT.Copy)
                swapped.then_inc(rp_act, 1)
                act.wait_ge(rp_dve, roped(n) + 2)
                nc.scalar.activation(at[name][:], at["rot"][:], ACT.Copy).then_inc(rp_act, 1)

            def v_tile(stage, t, j, i):
                tile = stage.tile(t, i)
                split(tile.ahead())
                act.wait_ge(tile_done, tile.before + 1)
                b, before = stage.out(j, i)
                nc.scalar.activation(at["v_f"][:], bank(b), ACT.Copy).then_inc(out_used[b], 1)

            def projection(stage, i, h, m):
                b, before = stage.out(m, i)
                tile = stage.tile(0, i)
                if m < KD - 1:
                    act.wait_ge(wo_out, (KD - 1) * h + m + 1)
                else:
                    split(tile.ahead())
                    act.wait_ge(tile_done, tile.before + 1)
                act.wait_ge(wo_add, KD * h + m + 1)
                nc.scalar.activation(wo_s[:, m % 4], bank(b), ACT.Copy).then_inc(out_used[b], 1)

            def att_head(stage, i, h, wo, nxt):
                t0, j0 = (1, KD) if wo else (0, 0)
                for q in range(NC):
                    if wo:
                        projection(stage, i, h - 1, 2 * q)
                    act.wait_ge(t_dve, step(ATT_DVE, f"neg{q}", h))
                    if q >= 2:
                        act.wait_ge(t_dve, step(ATT_DVE, f"a{q - 2}", h))
                    for c in range(2):
                        s = 2 * (q % 2) + c
                        e = nc.scalar.activation(prob[:, q % 2, c], bank(2 + s), ACT.Exp, bias=small[:, S_NEG + s:S_NEG + s + 1],
                                                 scale=0.125, accum_out=small[:, S_SUM + s:S_SUM + s + 1])
                    e.then_inc(t_act, 1)
                    if wo:
                        projection(stage, i, h - 1, 2 * q + 1)
                    if q == 0:
                        act.wait_ge(t_pe, step(ATT_PE, "v_turn", h))
                        nc.scalar.activation(at["v_hi"][:], bank(6), ACT.Copy).then_inc(t_act, 1)
                for q in range(NC):
                    act.wait_ge(t_pe, step(ATT_PE, f"turn{q}", h))
                    nc.scalar.activation(at_hi[:, :, P * q:P * q + P], chunks(bank(6 + q % 2)), ACT.Copy).then_inc(t_act, 1)
                if nxt:
                    rope_tile(stage, t0, j0, i, 2 * h + 2, "k_hi")
                act.wait_ge(t_pe, step(ATT_PE, "pv", h))
                nc.scalar.activation(at["o_s"][:], bank(7), ACT.Copy, scale=small[:, S_SUB:S_SUB + 1]).then_inc(t_act, 1)
                nc.scalar.activation(at["o_sq"][:], bank(7), ACT.Square).then_inc(t_act, 1)
                if nxt:
                    rope_tile(stage, t0 + 1, j0 + 1, i, 2 * h + 3, "q_hi")
                act.wait_ge(t_dve, step(ATT_DVE, "scale", h))
                nc.scalar.activation(at["ao_hi"][:], at["o_n"][:], ACT.Copy).then_inc(t_act, 1)
                if nxt:
                    v_tile(stage, t0 + 2, j0 + 2, i)

            rope_tile(ATT_Q, 0, 0, 0, 0, "k_hi")
            rope_tile(ATT_Q, 1, 1, 0, 1, "q_hi")
            v_tile(ATT_Q, 2, 2, 0)
            act.sem_inc(t_act, 1)
            att_head(ATT_0, 0, 0, False, True)
            with act.Fori(0, H - 2) as i:
                att_head(ATT_H, i, i + 1, True, True)
            att_head(ATT_7, 0, H - 1, True, False)
            for m in range(KD):
                b, before = ATT_WO.out(m, 0)
                act.wait_ge(out_used[b], before + 1)
                square(N_FFN1, m)
            split(ATT_WO.tile(0, 0).ahead())
            normed_hi(N_FFN1)
            feed_forward(2)
            for m in range(KD):
                output(m)

        @block.vector
        def _(dve):
            def split(tile):
                if isinstance(tile.before, int) and tile.before >= N_TILES:
                    return
                dve.wait_ge(hi_ready, tile.before + 1)
                nc.vector.tensor_tensor(w_lo[:, tile.slot], raw[:, tile.raw], w_hi[:, tile.slot].bitcast(F32), SUB)\
                  .then_inc(lo_ready, 1)

            def next_tile(stage, t, i):
                tile = stage.tile(t, i)
                split(tile.ahead())
                dve.wait_ge(tile_done, tile.before + 1)
                return stage.out(t, i)

            def add_square(r, m):
                base = (KD - 1) * DVE_SUMS.index(r)
                dve.wait_ge(fsq_act, KD * DVE_SUMS.index(r) + m + 1)
                if m > 1:
                    dve.wait_ge(fsq_add, base + m - 1)
                nc.vector.tensor_tensor(sq_sum[:], tmp[:, 2] if m == 1 else sq_sum[:], tmp[:, 2 + m % 4], ADD).then_inc(fsq_add, 1)

            def mean_squares(r):
                dve.wait_ge(n_pe, 2 * r + 1)
                nc.vector.tensor_scalar(col4(S_MS), bank(2)[:, 0:NC], 1.0 / D, EPS, MULT, ADD).then_inc(n_dve, 1)

            def token_factor(r):
                if r != N_MIX:
                    mean_squares(r)
                dve.wait_ge(n_pe, 2 * r + 2)

            def lo_part(r, m):
                dve.wait_ge(n_hi, split_base(r) + m + 1)
                nc.vector.tensor_tensor(h_lo[:, m], tmp[:, 2 + m % 2], h_hi[:, m].bitcast(F32), SUB).then_inc(h_ready, 1)

            def normed(r):
                token_factor(r)
                for m in range(KD):
                    if m >= 2:
                        dve.wait_ge(n_ht, scaled_base(r) + m - 1)
                    nc.vector.tensor_tensor(tmp[:, m % 2], x[:, m], bank(3), MULT).then_inc(n_t, 1)
                    if r in SPLIT_NORMS and m:
                        lo_part(r, m - 1)
                    if r == N_OUT1 and m >= 3:
                        add_square(N_POOL, m - 2)
                if r == N_OUT1:
                    add_square(N_POOL, KD - 2)
                    add_square(N_POOL, KD - 1)
                if r in SPLIT_NORMS:
                    lo_part(r, KD - 1)

            def normed_gain(r, gain):
                token_factor(r)

                def lo(m):
                    dve.wait_ge(n_hi, split_base(r) + m + 1)
                    nc.vector.tensor_tensor(h_lo[:, m], tmp[:, 2 + m % 4], h_hi[:, m].bitcast(F32), SUB).then_inc(h_ready, 1)

                for m in range(KD):
                    if m >= 4:
                        if r == N_OUT2:
                            dve.wait_ge(fin_pe, m - 3)
                        else:
                            dve.wait_ge(h_ready, split_base(r) + m - 3)
                    nc.vector.scalar_tensor_tensor(tmp[:, 2 + m % 4], x[:, m], vec[:, gain + m:gain + m + 1], bank(3), MULT, MULT)\
                      .then_inc(n_ht, 1)
                    if r in SPLIT_NORMS and m:
                        lo(m - 1)
                if r in SPLIT_NORMS:
                    lo(KD - 1)

            nc.vector.memset(raw[:], 0.0).then_inc(pro_dve, 1)
            nc.vector.memset(small[:], 0.0).then_inc(pro_dve, 1)
            for m in range(0, KD, 2):
                dve.wait_ge(pro_pe, m + 1)
                nc.vector.tensor_copy(x[:, m], bank(m)).then_inc(x_even, 1)
            dve.wait_ge(pro_pe, 9)
            for n, rows_in in enumerate(PACK_ROWS):
                copied = nc.vector.tensor_copy(vec[:, P * n:P * n + rows_in], bank(0)[:, P * n:P * n + rows_in])
            copied.then_inc(pro_dve, 1)
            dve.wait_ge(pro_dve, 3)
            dve.wait_ge(pro_pool, 1)
            nc.vector.tensor_scalar(small[:, S_GNW:S_GNW + 1], vec[:, V_GNW:V_GNW + 1], 0.5, None, MULT)
            nc.vector.tensor_scalar(small[:, S_SUB:S_SUB + 1], vec[:, V_SUB:V_SUB + 1], 1.0 - LAM_INIT, None, MULT)
            nc.vector.memset(small[:, S_PI2:S_PI2 + 1], float(np.pi / 2))
            dve.wait_ge(pro_act, 1)
            nc.vector.scalar_tensor_tensor(cact[:, 1], cact[:, 0], 1.0, vec[:, V_C:V_C + KD], ADD, MULT).then_inc(pro_dve, 1)
            dve.wait_ge(pro_dve, 4)
            nc.vector.tensor_scalar(cact[:, 1], cact[:, 1], 0.5, None, MULT).then_inc(pro_dve, 1)
            dve.wait_ge(pro_dve, 5)
            for turn, n in enumerate((0, 2, 3)):
                dve.wait_ge(ada_in[n], 16)
                total = ada0_sum[:, T * n:T * n + T]
                for k in range(KD):
                    src = ada0[:, k, T * n:T * n + T]
                    if k == 0:
                        nc.vector.tensor_scalar(total, src, cact[:, 1, k:k + 1], None, MULT).then_inc(ada0_own, 1)
                    else:
                        dve.wait_ge(ada0_own, KD * turn + k)
                        nc.vector.scalar_tensor_tensor(total, src, cact[:, 1, k:k + 1], total, MULT, ADD).then_inc(ada0_own, 1)
                if turn == 1:
                    mean_squares(N_MIX)
            split(Tile(0))
            split(Tile(1))
            dve.wait_ge(pro_pe, 10)
            nc.vector.tensor_tensor(mod[:, 0:16], bank(1)[:, 0:16], vec[:, V_BADA:V_BADA + 16], ADD).then_inc(pro_dve, 1)
            dve.wait_ge(pro_dve, 6)
            nc.vector.scalar_tensor_tensor(wsc[:, 0], mod[:, SC1:SC1 + KD], 1.0, vec[:, V_N1:V_N1 + KD], ADD, MULT)\
              .then_inc(mod_ready, 1)
            normed(N_MIX)
            split(Tile(2))
            split(Tile(3))

            dve.wait_ge(ab_in, 32)
            b, before = next_tile(AB, 0, 0)
            nc.vector.tensor_scalar(ab_f[0:2 * H], bank(b)[0:2 * H], small[0:2 * H, S_DT:S_DT + 1], None, ADD)\
              .then_inc(out_used[b], 1)
            v, e, s2, s3, s4, s5, s6 = [buf[:] for buf in ab]
            links = [0]

            def link(ins):
                ins.then_inc(ab_dve, 1)
                links[0] += 1
                dve.wait_ge(ab_dve, links[0])

            dve.wait_ge(ab_pe, 1)
            link(nc.vector.tensor_copy(v, bank(2)[:, 0:2 * H * NC].rearrange("p (n c) -> p n c", n=NC)))
            dve.wait_ge(ab_act, 2)
            link(nc.vector.tensor_scalar(s2, e, 2.0, None, ADD))
            link(nc.vector.reciprocal(s3, s2))
            link(nc.vector.tensor_tensor(s3, s3, e, MULT))
            link(nc.vector.tensor_tensor(s4, s3, s3, MULT))
            link(nc.vector.tensor_scalar(s5, s4, 1.0 / 15, None, MULT))
            for c in (13, 11, 9, 7, 5, 3):
                link(nc.vector.scalar_tensor_tensor(s5, s5, 1.0 / c, s4, ADD, MULT))
            link(nc.vector.scalar_tensor_tensor(s5, s5, 1.0, s3, ADD, MULT))
            link(nc.vector.tensor_scalar(s2, v, 0.0, None, ALU.max))
            link(nc.vector.scalar_tensor_tensor(s5, s5, 2.0, s2, MULT, ADD))
            dve.wait_ge(ab_act, 3)
            link(nc.vector.tensor_scalar(alog[:], alog[:], -1.0, None, MULT))
            link(nc.vector.tensor_tensor(s6.rearrange("p n (two h) -> p n two h", two=2), s5.rearrange("p n (two h) -> p n two h", two=2),
                                        alog[:].unsqueeze(1).unsqueeze(1).to_broadcast([P, NC, 2, H]), MULT))
            link(nc.vector.tensor_scalar(s2, e, 1.0, None, ADD))
            link(nc.vector.reciprocal(s4, s2))
            link(nc.vector.tensor_scalar(s3, v, 0.0, None, ALU.is_ge))
            link(nc.vector.tensor_scalar(s2, e, -1.0, 1.0, MULT, ADD))
            link(nc.vector.tensor_tensor(s3, s3, s2, MULT))
            link(nc.vector.tensor_tensor(s3, s3, e, ADD))
            link(nc.vector.tensor_tensor(b_tok[:], s3, s4, MULT))
            link(nc.vector.tensor_scalar(bh_tok[:], b_tok[:], 0.5, None, MULT))
            dve.wait_ge(ab_pe, 2)
            link(nc.vector.tensor_copy(g_tok[:], bank(3)[:, 0:2 * H * NC].rearrange("p (n c) -> p n c", n=NC)))
            assert links[0] == AB_LINKS
            dve.sem_inc(g_dve, 1)

            def conv_taps(stage, t, i, n, hh):
                b, before = stage.out(t, i)
                buf = conv_bufs[n]
                dve.wait_ge(cv_act, 7 * hh + 2 * n + 1)
                for d in (1, 2, 3):
                    if d > 1:
                        dve.wait_ge(cv_dve, 10 * hh + 3 * n + d - 1)
                    nc.vector.scalar_tensor_tensor(buf[:, d:T], bank(b)[:, 0:T - d],
                                                   col(vec, hh + (V_CONV + 24 * (3 - d) + 8 * n)), buf[:, d:T], MULT, ADD)\
                      .then_inc(*((cv_dve, 1) if d < 3 else (out_used[b], 1)))

            def conv_silu(n, hh):
                dve.wait_ge(cv_act, 7 * hh + 2 * n + 2)
                nc.vector.scalar_tensor_tensor(conv_bufs[n][:], gd["th"][:], 1.0, conv_bufs[n][:], ADD, MULT).then_inc(cv_dve, 1)

            def z_silu(stage, t, i, hh):
                b, before = stage.out(t, i)
                dve.wait_ge(cv_act, 7 * hh + 7)
                dve.wait_ge(out_used[b], before + 1)
                nc.vector.scalar_tensor_tensor(gd["z_g"][:], gd["th"][:], 1.0, gd["z_g"][:], ADD, MULT).then_inc(cv_dve, 1)

            conv_bufs = [gd[n] for n in ("q_s", "k_s", "v_s")]
            for n in range(3):
                split(QKVZ.tile(n, 0).ahead())
                conv_taps(QKVZ, n, 0, n, 0)
                conv_silu(n, 0)
            split(QKVZ.tile(3, 0).ahead())
            z_silu(QKVZ, 3, 0, 0)

            def head(stage, i, h):
                more = stage is HEAD
                scx, scb = (4, 5) if more else (1, 2)

                def ahead(t):
                    split(stage.tile(t, i).ahead())

                def short_conv():
                    b0, before0 = stage.out(0, i)
                    b, before = stage.out(scx, i)
                    dve.wait_ge(cv_dve, 10 * h + (19 if more else 10))
                    dve.wait_ge(out_used[b0], before0 + 1)
                    dve.wait_ge(tile_done, stage.tile(scx, i).before + 1)
                    nc.vector.tensor_tensor(gd["cx"][:], gd["cc"][:], bank(b), MULT).then_inc(out_used[b], 1)
                    dve.wait_ge(out_used[b], before + 1)
                    nc.vector.tensor_scalar(gd["cc"][:], gd["cx"][:], col(vec, h + (V_SCONV + 16)), None, MULT)\
                      .then_inc(sc_dve, 1)
                    for d in (1, 2):
                        dve.wait_ge(sc_dve, 3 * h + d)
                        nc.vector.scalar_tensor_tensor(gd["cc"][:, d:T], gd["cx"][:, 0:T - d],
                                                       col(vec, h + (V_SCONV + 8 * (2 - d))), gd["cc"][:, d:T],
                                                       MULT, ADD).then_inc(sc_dve, 1)

                def short_gate():
                    b, before = stage.out(scb, i)
                    dve.wait_ge(tile_done, stage.tile(scb, i).before + 1)
                    dve.wait_ge(sc_dve, 3 * h + 3)
                    nc.vector.tensor_tensor(dyn(sc_out, h), gd["cc"][:], bank(b), MULT).then_inc(out_used[b], 1)

                def after_pe(name):
                    dve.wait_ge(g_pe, step(PE_STEPS, name, h))

                def after_act(name):
                    dve.wait_ge(g_act, step(ACT_STEPS, name, h))

                def own(name):
                    dve.wait_ge(g_dve, step(DVE_STEPS, name, h))

                g_col = head_cols(g_tok, h)
                nc.vector.tensor_copy(col4(S_G), g_col).then_inc(g_dve, 1)
                after_act("k_squares")
                nc.vector.tensor_scalar(col4(S_KSS), col4(S_KSQ), 4 * EPS, None, ADD).then_inc(g_dve, 1)
                after_pe("g_rows")
                for n in range(NC):
                    arg = nc.vector.scalar_tensor_tensor(part(gd["dec"], n), part(bank(4), n), col(g_tok[:, n], h),
                                                         cst[:, C_LOW:C_LOW + P], SUB, ALU.min)
                arg.then_inc(g_dve, 1)
                nc.vector.tensor_tensor(col4(S_LEFT), chunks(bank(4))[:, :, P - 1], g_col, SUB).then_inc(g_dve, 1)
                dve.wait_ge(g_pool, step(POOL_STEPS, "k_norm", h))
                nc.vector.scalar_tensor_tensor(col4(S_KB), col4(S_KN), -1.0, head_cols(b_tok, h + H), MULT, MULT)\
                  .then_inc(g_dve, 1)
                after_act("exp_decay")
                after_pe("kb_rows")
                nc.vector.tensor_tensor(gd["low_d"][:], gd["dec"][:], bank(7), MULT).then_inc(g_dve, 1)
                own("kb_decay")
                for n in range(NC):
                    low = nc.vector.scalar_tensor_tensor(part(gd["low"], n), part(bank(5), n), small[:, S_KN + n:S_KN + n + 1],
                                                         part(gd["low_d"], n), MULT, MULT)
                low.then_inc(g_dve, 1)
                own("lower")
                nc.vector.tensor_tensor(chunks(gd["u_t"][:]), chunks(gd["low"][:]), every(cst[:, C_L1:C_L1 + P]), MULT)\
                  .then_inc(g_dve, 1)
                own("u_pairs")
                nc.vector.tensor_tensor(chunks(gd["u_t"][:]), chunks(gd["u_t"][:]), every(ident), ADD).then_inc(g_dve, 1)
                after_act("exp_g_rows")
                nc.vector.tensor_tensor(gd["q_g"][:], gd["q_s"][:], gd["y_t"][:], MULT).then_inc(g_dve, 1)
                for n in range(NC):
                    qk = nc.vector.scalar_tensor_tensor(part(gd["qk_t"], n), part(bank(6), n), small[:, S_KN + n:S_KN + n + 1],
                                                        part(gd["dec"], n), MULT, MULT)
                qk.then_inc(g_dve, 1)
                ahead(0)
                for n in range(LEVELS):
                    after_pe(f"y{n}")
                    if n == 0:
                        own("q_g")
                    nc.vector.tensor_tensor(chunks(gd["y_t"][:]), chunks(bank(4)), every(ident), ADD).then_inc(g_dve, 1)
                    if n == 0:
                        after_act("exp_g")
                        nc.vector.tensor_tensor(col4(S_KBEG), col4(S_KB), col4(S_EG), MULT).then_inc(g_dve, 1)
                        nc.vector.tensor_tensor(chunks(gd["v_b"][:]), chunks(bank(3)), spread(head_cols(bh_tok, h + H)), MULT)\
                          .then_inc(g_dve, 1)
                        own("kbeg_scale")
                        nc.vector.tensor_tensor(chunks(gd["k_beg"][:]), chunks(bank(2)), spread(col4(S_KBEG)), MULT)\
                          .then_inc(g_dve, 1)
                    if more and n == 1:
                        conv_taps(stage, 1, i, 0, h + 1)
                    if more and n == 2:
                        conv_silu(0, h + 1)
                    if more and n == 3:
                        ahead(2)
                    if more and n == 4:
                        conv_taps(stage, 3, i, 2, h + 1)
                    if not more and n == 2:
                        ahead(1)
                    if n == LEVELS - 1:
                        break
                    after_pe(f"x{n}")
                    nc.vector.tensor_copy(gd["x_t"][:], bank(5)).then_inc(g_dve, 1)
                    if n == 0:
                        after_act("exp_left")
                        nc.vector.tensor_tensor(col4(S_KDEC), col4(S_KN), col4(S_ELEFT), MULT).then_inc(g_dve, 1)
                        own("kdec_scale")
                        nc.vector.tensor_tensor(chunks(gd["k_dec"][:]), chunks(bank(2)), spread(col4(S_KDEC)), MULT)\
                          .then_inc(g_dve, 1)
                    if more and n == 1:
                        ahead(1)
                    if more and n == 2:
                        conv_taps(stage, 2, i, 1, h + 1)
                    if more and n == 3:
                        conv_silu(1, h + 1)
                    if more and n == 4:
                        ahead(3)
                    if not more and n == 1:
                        short_conv()
                if more:
                    conv_silu(2, h + 1)
                    short_conv()
                    ahead(4)
                else:
                    short_gate()
                for n in range(NC):
                    after_pe(f"v_new{n}")
                    nc.vector.tensor_copy(part(gd["y_t"], n), part(bank(2), n)).then_inc(g_dve, 1)
                    if n < NC - 1:
                        after_pe(f"o{n}")
                        if n == 0:
                            nc.vector.tensor_copy(state[:], part(bank(4), 0)).then_inc(g_dve, 1)
                        else:
                            nc.vector.scalar_tensor_tensor(state[:], state[:], small[:, S_ELAST + n:S_ELAST + n + 1],
                                                           part(bank(4), 0), MULT, ADD).then_inc(g_dve, 1)
                    if more and n == 1:
                        short_gate()
                        ahead(5)
                    if not more and n == 1:
                        ahead(2)
                after_act("o_squares")
                nc.vector.tensor_tensor(gd["dec"][:], gd["dec"][:], gd["q_sq"][:], ADD).then_inc(g_dve, 1)
                after_pe("o_sums")
                nc.vector.tensor_scalar(col4(S_OMS), bank(5)[:, 0:NC], P * EPS * 4 * EPS, None, ADD).then_inc(g_dve, 1)
                nc.vector.tensor_tensor(mod[:, bass.ds(4 * h + 16, 4)], bank(5)[:, 8:12],
                                        vec[:, bass.ds(4 * h + (V_BADA + 16), 4)], ADD).then_inc(g_dve, 1)
                nc.vector.tensor_tensor(mod[:, bass.ds(2 * h + 48, 2)], bank(5)[:, 12:14],
                                        vec[:, bass.ds(2 * h + V_BADAF, 2)], ADD).then_inc(g_dve, 1)
                dve.wait_ge(cv_dve, 10 * h + 10)
                nc.vector.tensor_tensor(gd["low"][:], bank(3), gd["z_g"][:], MULT).then_inc(g_dve, 1)
                if more:
                    ahead(6)
                after_pe("o_norm_rows")
                own("o_gate")
                nc.vector.tensor_tensor(gd["low_d"][:], gd["low"][:], bank(6), MULT).then_inc(g_dve, 1)
                after_act("o_hi")
                nc.vector.tensor_tensor(dyn(og_lo, h), gd["low_d"][:], dyn(og_hi, h).bitcast(F32), SUB).then_inc(g_dve, 1)
                if more:
                    ahead(7)
                    z_silu(stage, 7, i, h + 1)
                else:
                    ahead(3)

            with dve.Fori(0, H - 1) as h:
                head(HEAD, h, h)
            head(LAST, 0, H - 1)

            dve.wait_ge(g_dve, heads(DVE_STEPS, H))
            nc.vector.scalar_tensor_tensor(wsc[:, 1], mod[:, SC2:SC2 + KD], 1.0, vec[:, V_N2:V_N2 + KD], ADD, MULT)
            nc.vector.scalar_tensor_tensor(wsc[:, 2], mod[:, SCF:SCF + KD], 1.0, vec[:, V_NF:V_NF + KD], ADD, MULT)
            nc.vector.tensor_scalar(mod[:, G1:G1 + KD], mod[:, G1:G1 + KD], 0.5, None, MULT).then_inc(mod_ready, 1)
            dve.wait_ge(sc_split, 1)
            nc.vector.tensor_tensor(sc_lo[:], sc_out[:], sc_hi[:].bitcast(F32), SUB).then_inc(sc_split, 1)
            with dve.Fori(0, 2) as i:
                for t in range(4):
                    split(GATE_B.tile(t, i).ahead())
            for t in (2, 3):
                b, before = GATE_B.out(t, 1)
                dve.wait_ge(out_used[b], before + 1)
            with dve.Fori(0, 2) as i:
                for m in range(4):
                    ga = dyn(ga_t, 4 * i + m)
                    b, before = next_tile(GATE, 2 * m, i)
                    nc.vector.scalar_tensor_tensor(yb[:], dyn(gb_t, 4 * i + m), 1.0, bank(b), ADD, MULT).then_inc(out_used[b], 1)
                    b2, before2 = next_tile(GATE, 2 * m + 1, i)
                    nc.vector.scalar_tensor_tensor(ga, ga, 1.0, bank(b2), ADD, MULT).then_inc(out_used[b2], 1)
                    dve.wait_ge(out_used[b], before + 1)
                    dve.wait_ge(out_used[b2], before2 + 1)
                    nc.vector.tensor_tensor(ga, ga, yb[:], ADD).then_inc(mixed, 1)
                    dve.wait_ge(mix_hi, 4 * i + (m + 1))
                    nc.vector.tensor_tensor(dyn(h_lo, 4 * i + m), ga, dyn(h_hi, 4 * i + m).bitcast(F32), SUB).then_inc(mix_lo, 1)
            dve.wait_ge(mod_ready, 2)
            with dve.Fori(0, 2) as i:
                for t in range(4):
                    b, before = WO.out(t, i)
                    tile = WO.tile(t, i)
                    xm = dyn(x, 4 * i + t)
                    dve.wait_ge(tile_done, tile.before + 1)
                    nc.vector.scalar_tensor_tensor(xm, bank(b), col(mod, 4 * i + (G1 + t)), xm, MULT, ADD)\
                      .then_inc(out_used[b], 1)
                    split(tile.ahead())

            def rope_tables():
                ang, rnd = tmp[:, 0], tmp[:, 1]
                dve.wait_ge(rp_pe, 1)
                nc.vector.tensor_scalar(ang, bank(4), cst[:, C_FREQ:C_FREQ + 1], None, MULT).then_inc(rp_dve, 1)
                dve.wait_ge(rp_dve, 2)
                nc.vector.tensor_scalar(rnd, ang, float(1 / (2 * np.pi)), MAGIC, MULT, ADD).then_inc(rp_dve, 1)
                dve.wait_ge(rp_dve, 3)
                nc.vector.tensor_scalar(rnd, rnd, -MAGIC, None, ADD).then_inc(rp_dve, 1)
                for n in range(3):
                    dve.wait_ge(rp_dve, 4 + n)
                    nc.vector.scalar_tensor_tensor(ang, rnd, -TWO_PI[n], ang, MULT, ADD).then_inc(rp_dve, 1)
                dve.wait_ge(rp_dve, 7)
                nc.vector.tensor_scalar(ang, ang, 3.1415925, -3.1415925, ALU.min, ALU.max).then_inc(rp_dve, 1)
                dve.wait_ge(rp_act, 1)
                nc.vector.tensor_scalar(at["sin"][:], at["sin"][:], cst[:, C_SIGN:C_SIGN + 1], None, MULT).then_inc(rp_dve, 1)

            def feed_forward(f):
                base = 0 if f == 0 else 2 * UPS + 4 * UPS * (f - 1)
                own = 2 * UPS * (f - 1)
                with dve.Fori(0, UPS) as i:
                    for j in range(2):
                        g, u, gu = tmp[:, 2 + j], 2 * j + 1, tmp[:, 4 + j]
                        b, before = next_tile(UP[f], 2 * j, i)
                        if f == 0:
                            dve.wait_ge(f_act, 2 * i + j + 1)
                            nc.vector.scalar_tensor_tensor(g, tmp[:, j], 1.0, bank(b), ADD, MULT).then_inc(out_used[b], 1)
                        else:
                            dve.wait_ge(f_act, 4 * i + (base + 2 * j + 1))
                            nc.vector.scalar_tensor_tensor(g[:, 1:T], bank(b)[:, 0:T - 1], col(vec, 2 * i + (V_FCW[f - 1] + j)),
                                                           g[:, 1:T], MULT, ADD).then_inc(f_dve, 1)
                            dve.wait_ge(f_dve, 2 * i + (own + j + 1))
                            nc.vector.scalar_tensor_tensor(g[:, 0:T - 1], bank(b)[:, 1:T],
                                                           col(vec, 2 * i + (V_FCW[f - 1] + 2 * KF + j)),
                                                           g[:, 0:T - 1], MULT, ADD).then_inc(out_used[b], 1)
                        bu, before_u = next_tile(UP[f], u, i)
                        if f == 0:
                            dve.wait_ge(out_used[b], before + 1)
                            nc.vector.scalar_tensor_tensor(gu, g, 0.5, bank(bu), MULT, MULT).then_inc(out_used[bu], 1)
                        else:
                            dve.wait_ge(f_act, 4 * i + (base + 2 * j + 2))
                            nc.vector.tensor_tensor(gu, tmp[:, j], bank(bu), MULT).then_inc(out_used[bu], 1)
                        dve.wait_ge(f_hi, 2 * i + (KF * f + j + 1))
                        nc.vector.tensor_tensor(dyn(act_lo, 2 * i + j), gu, dyn(act_hi, 2 * i + j).bitcast(F32), SUB)\
                          .then_inc(f_lo, 1)

                def down(i):
                    for m in range(4):
                        for c in range(2):
                            split(DOWN[f].tile(3 * m + c, i).ahead())
                        last = DOWN[f].tile(3 * m + 2, i)
                        dve.wait_ge(tile_done, last.before + 1)
                        b, before = DOWN[f].out(m, i)
                        xm = dyn(x, 4 * i + m)
                        if f == 0:
                            nc.vector.scalar_tensor_tensor(xm, bank(b), col(mod, 4 * i + (G2 + m)), xm, MULT, ADD)\
                              .then_inc(out_used[b], 1)
                        else:
                            nc.vector.tensor_tensor(xm, xm, bank(b), ADD).then_inc(out_used[b], 1)
                        split(last.ahead())

                if f == 1:
                    rope_tables()
                if f == 2:
                    down(0)
                    down(1)
                else:
                    with dve.Fori(0, 2) as i:
                        down(i)

            normed(N_FFN)
            feed_forward(0)
            normed(N_OUT1)

            dve.wait_ge(pos_in, 16)
            nc.vector.tensor_copy(pos_f[32:33], pos_i[0:1]).then_inc(rp_dve, 1)

            nc.vector.memset(win[0][:], 0.0).then_inc(pl_dve, 1)
            token_factor(N_POOL)
            dve.wait_ge(edges_in, 16)
            count = 1
            last_group = len(WINDOWS) - 1
            inside = slice(EDGE, EDGE + T)

            def normed_pair(bufs, group):
                nc.vector.tensor_tensor(bufs[0][:, :, inside], x[:, 2 * group:2 * group + 2],
                                        bank(3).rearrange("p (o t) -> p o t", o=1).to_broadcast([P, 2, T]), MULT)\
                  .then_inc(pl_dve, 1)

            def less_centre(bufs, group, count):
                total, width = bufs[1 + group % 2], WINDOWS[group]
                ends = total[:, :, inside].rearrange("p m (e c) -> p m e c", c=EDGE)[:, :, ::T // EDGE - 1]
                factors = edges[:, group].rearrange("p (m e c) -> p m e c", m=1, e=2).to_broadcast([P, 2, 2, EDGE])
                nc.vector.tensor_tensor(ends, ends, factors, MULT).then_inc(pl_dve, 1)
                dve.wait_ge(pl_dve, count + 1)
                nc.vector.scalar_tensor_tensor(pool_d[:, 2 * group:2 * group + 2], total[:, :, inside], 1.0 / width,
                                               bufs[0][:, :, inside], MULT, SUB).then_inc(pl_dve, 1)
                assert count + 2 == POOL_STEP[group]

            def pool_lo(group):
                for m in (2 * group, 2 * group + 1):
                    dve.wait_ge(pl_hi, m + 1)
                    nc.vector.scalar_tensor_tensor(p_lo[:, m], pool_d[:, m], vec[:, V_MIX + m:V_MIX + m + 1],
                                                   p_hi[:, m].bitcast(F32), MULT, SUB).then_inc(pl_lo, 1)

            def mixed_in(group):
                for m in (2 * group, 2 * group + 1):
                    b, before = POOLW.out(m, 0)
                    t, j = divmod(m, 4)
                    if j < 3:
                        dve.wait_ge(pl_out, 3 * t + j + 1)
                    else:
                        dve.wait_ge(tile_done, POOLW.tile(t, 0).before + 1)
                    nc.vector.scalar_tensor_tensor(x[:, m], bank(b), vec[:, V_PSC + m:V_PSC + m + 1], x[:, m], MULT, ADD)\
                      .then_inc(out_used[b], 1)
                    if m >= 3:
                        add_square(N_FFN0, m - 2)

            dve.wait_ge(n_ht, scaled_base(N_OUT1) + KD)
            dve.wait_ge(pl_pool, 1)
            normed_pair(win_l, last_group)
            count += 1
            assert count == POOL_NORMED
            for group in range(last_group):
                dve.wait_ge(pl_dve, count)
                normed_pair(win, group)
                count += 1
                for n in range(group + 1):
                    dve.wait_ge(pl_dve, count)
                    double(nc.vector, win, n).then_inc(pl_dve, 1)
                    count += 1
                dve.wait_ge(pl_dve, count)
                less_centre(win, group, count)
                count += 2
                if group:
                    pool_lo(group - 1)
            mixed_in(0)
            dve.wait_ge(pl_pool, 1 + len(WINDOWS))
            less_centre(win_l, last_group, count)
            pool_lo(last_group - 1)
            mixed_in(1)
            pool_lo(last_group)
            mixed_in(2)
            mixed_in(3)
            add_square(N_FFN0, KD - 2)
            add_square(N_FFN0, KD - 1)
            for t in range(2):
                split(POOLW.tile(t, 0).ahead())
            normed_gain(N_FFN0, V_FFN)
            feed_forward(1)

            normed_gain(N_ATT, V_MIX + KD)
            dve.wait_ge(lam_in_s, 64)
            pairs = lam_in[0:1].rearrange("o (c e) d -> o c e d", e=2)
            nc.vector.tensor_tensor(pairs[:, :, 0], pairs[:, :, 0], pairs[:, :, 1], MULT).then_inc(rp_dve, 1)
            dve.wait_ge(rp_dve, 10)
            nc.vector.tensor_reduce(small[0:1, S_MAX:S_MAX + 2], pairs[:, :, 0], AX_X, ADD).then_inc(rp_dve, 1)
            dve.wait_ge(rp_act, 4)
            nc.vector.scalar_tensor_tensor(small[0:1, S_SUM:S_SUM + 1], small[0:1, S_NEG:S_NEG + 1], LAM_INIT,
                                           small[0:1, S_NEG + 1:S_NEG + 2], ADD, SUB).then_inc(rp_dve, 1)

            def rope_tile(stage, t, j, i, n, name):
                split(stage.tile(t, i).ahead())
                b, before = stage.out(j, i)
                dve.wait_ge(rp_act, 2 * n + 5)
                nc.vector.tensor_tensor(at["rot"][:], bank(b), at["cos"][:], MULT).then_inc(out_used[b], 1)
                nc.vector.tensor_tensor(at["swap"][:], at["swap"][:], at["sin"][:], MULT).then_inc(rp_dve, 1)
                dve.wait_ge(out_used[b], before + 1)
                dve.wait_ge(rp_dve, roped(n) + 1)
                nc.vector.tensor_tensor(at["rot"][:], at["rot"][:], at["swap"][:], ADD).then_inc(rp_dve, 1)
                dve.wait_ge(rp_act, 2 * n + 6)
                nc.vector.tensor_tensor(at[name + "_lo"][:], at["rot"][:], at[name + "_hi"][:].bitcast(F32), SUB)\
                  .then_inc(rp_dve, 1)

            rope_tile(ATT_Q, 0, 0, 0, 0, "k")
            rope_tile(ATT_Q, 1, 1, 0, 1, "q")
            split(ATT_Q.tile(2, 0).ahead())
            dve.wait_ge(rp_pe, 2)
            nc.vector.tensor_copy(small[:, S_LAM:S_LAM + 1], bank(7)[:, 0:1]).then_inc(t_dve, 1)

            def att_head(stage, i, h, wo, nxt):
                t0, j0 = (1, KD) if wo else (0, 0)

                def own(name):
                    dve.wait_ge(t_dve, step(ATT_DVE, name, h))

                def maxima(q):
                    s = 2 * (q % 2)
                    dve.wait_ge(t_pe, step(ATT_PE, f"scores{q}", h))
                    nc.vector.tensor_reduce(small[:, S_MAX + s:S_MAX + s + 2], ps[:, 2 + s:4 + s, :], AX_X, ALU.max)\
                      .then_inc(t_dve, 1)
                    own(f"max{q}")
                    nc.vector.tensor_scalar(small[:, S_NEG + s:S_NEG + s + 2], small[:, S_MAX + s:S_MAX + s + 2], -0.125, None,
                                            MULT).then_inc(t_dve, 1)

                def turn_lo(q):
                    dve.wait_ge(t_act, step(ATT_ACT, f"turn{q}", h))
                    nc.vector.tensor_tensor(at_lo[:, :, P * q:P * q + P], chunks(bank(6 + q % 2)),
                                            at_hi[:, :, P * q:P * q + P].bitcast(F32), SUB).then_inc(t_dve, 1)

                maxima(0)
                for q in range(NC):
                    if q + 1 < NC:
                        maxima(q + 1)
                    s, pr = 2 * (q % 2), prob[:, q % 2]
                    dve.wait_ge(t_act, step(ATT_ACT, f"exp{q}", h))
                    nc.vector.reciprocal(small[:, S_REC + s:S_REC + s + 2], small[:, S_SUM + s:S_SUM + s + 2]).then_inc(t_dve, 1)
                    own(f"recip{q}")
                    nc.vector.tensor_tensor(small[:, S_L + s:S_L + s + 1], small[:, S_REC + s + 1:S_REC + s + 2],
                                            small[:, S_LAM:S_LAM + 1], MULT).then_inc(t_dve, 1)
                    own(f"lam{q}")
                    nc.vector.tensor_scalar(pr[:, 1], pr[:, 1], small[:, S_L + s:S_L + s + 1], None, MULT).then_inc(t_dve, 1)
                    own(f"second{q}")
                    if q >= 2:
                        dve.wait_ge(t_pe, step(ATT_PE, f"turn{q - 2}", h))
                    nc.vector.scalar_tensor_tensor(a_sb[:, q % 2], pr[:, 0], small[:, S_REC + s:S_REC + s + 1], pr[:, 1], MULT, SUB)\
                      .then_inc(t_dve, 1)
                    if q == 0:
                        dve.wait_ge(t_act, step(ATT_ACT, "v_hi", h))
                        nc.vector.tensor_tensor(at["v_lo"][:], bank(6), at["v_hi"][:].bitcast(F32), SUB).then_inc(t_dve, 1)
                    if q >= 2:
                        turn_lo(q - 2)
                turn_lo(2)
                turn_lo(3)
                if wo:
                    split(stage.tile(0, i).ahead())
                if nxt:
                    rope_tile(stage, t0, j0, i, 2 * h + 2, "k")
                dve.wait_ge(t_pe, step(ATT_PE, "sums", h))
                nc.vector.tensor_scalar(col4(S_OMS), bank(7)[:, 0:NC], SUBLN_EPS, None, ADD).then_inc(t_dve, 1)
                dve.wait_ge(t_pe, step(ATT_PE, "rows", h))
                nc.vector.tensor_tensor(at["o_n"][:], at["o_s"][:], bank(6), MULT).then_inc(t_dve, 1)
                if nxt:
                    rope_tile(stage, t0 + 1, j0 + 1, i, 2 * h + 3, "q")
                dve.wait_ge(t_act, step(ATT_ACT, "hi", h))
                nc.vector.tensor_tensor(at["ao_lo"][:], at["o_n"][:], at["ao_hi"][:].bitcast(F32), SUB).then_inc(t_dve, 1)
                if nxt:
                    split(stage.tile(t0 + 2, i).ahead())

            att_head(ATT_0, 0, 0, False, True)
            with dve.Fori(0, H - 2) as i:
                att_head(ATT_H, i, i + 1, True, True)
            att_head(ATT_7, 0, H - 1, True, False)
            dve.wait_ge(wo_add, KD * (H - 1) + 4)
            for m in range(KD):
                b, before = ATT_WO.out(m, 0)
                if m < KD - 1:
                    dve.wait_ge(wo_out, (KD - 1) * (H - 1) + m + 1)
                else:
                    dve.wait_ge(tile_done, ATT_WO.tile(0, 0).before + 1)
                nc.vector.tensor_tensor(x[:, m], x[:, m], bank(b), ADD).then_inc(out_used[b], 1)
                if m >= 3:
                    add_square(N_FFN1, m - 2)
            add_square(N_FFN1, KD - 2)
            add_square(N_FFN1, KD - 1)
            split(ATT_WO.tile(0, 0).ahead())
            normed_gain(N_FFN1, V_FFN + KD)
            feed_forward(2)
            normed_gain(N_OUT2, V_FIN)

        @block.tensor
        def _(pe):
            def open_out(out):
                b, before = out
                if not (isinstance(before, int) and before == 0):
                    pe.wait_ge(out_used[b], before)
                return b

            def term(dst, tile, k, hi, lo, first, last):
                nc.tensor.matmul(dst, w_hi[:, tile.slot, k], hi, start=first, stop=False)
                nc.tensor.matmul(dst, w_hi[:, tile.slot, k], lo, start=False, stop=False)
                return nc.tensor.matmul(dst, w_lo[:, tile.slot, k], hi, start=False, stop=last)

            def quarter(stage, t, j, i, q):
                tile = stage.tile(t, i)
                if q == 0:
                    pe.wait_ge(lo_ready, tile.before + 1)
                    open_out(stage.out(j, i))
                for k in (2 * q, 2 * q + 1):
                    last = term(bank(stage.banks[j]), tile, k, h_hi[:, k], h_lo[:, k], k == 0, k == KD - 1)
                if q == 3:
                    last.then_inc(tile_done, 1)

            def product(stage, t, i, hi, lo):
                tile = stage.tile(t, i)
                pe.wait_ge(lo_ready, tile.before + 1)
                b = open_out(stage.out(t, i))
                for k in range(KD):
                    last = term(bank(b), tile, k, hi[:, k], lo[:, k], k == 0, k == KD - 1)
                last.then_inc(tile_done, 1)

            def turn(dst, src, n_rows=P):
                return nc.tensor.transpose(dst, src, ident[0:n_rows, 0:n_rows])

            def product_group(outs, hi, lo, ready, together=KD):
                pairs = []
                for stage, t in outs:
                    tile = stage.tile(t, 0)
                    pe.wait_ge(lo_ready, tile.before + 1)
                    pairs.append((tile, open_out(stage.out(t, 0))))
                for k in range(together):
                    pe.wait_ge(ready[0], ready[1] + k + 1)
                    for tile, b in pairs:
                        last = term(bank(b), tile, k, hi[:, k], lo[:, k], k == 0, k == KD - 1)
                        if k == KD - 1:
                            last.then_inc(tile_done, 1)
                for n, (tile, b) in enumerate(pairs):
                    for k in range(together, KD):
                        if n == 0:
                            pe.wait_ge(ready[0], ready[1] + k + 1)
                        last = term(bank(b), tile, k, hi[:, k], lo[:, k], False, k == KD - 1)
                    if together < KD:
                        last.then_inc(tile_done, 1)

            def rows_of(b, c):
                for n in range(NC):
                    t = turn(part(bank(b), n), small[:, c + n:c + n + 1].to_broadcast([P, P]))
                return t

            def sums(r):
                if r in POOL_SUMS:
                    pe.wait_ge(sq_done, KD * (POOL_SUMS.index(r) + 1))
                else:
                    pe.wait_ge(fsq_add, (KD - 1) * (DVE_SUMS.index(r) + 1))
                for n in range(NC):
                    s = nc.tensor.matmul(bank(2)[:, n:n + 1], part(sq_sum, n), one_col, start=True, stop=True)
                s.then_inc(n_pe, 1)

            def norm(r):
                if r != N_MIX:
                    sums(r)
                pe.wait_ge(n_pool, r + 1)
                rows_of(3, S_RSTD).then_inc(n_pe, 1)

            pe.wait_ge(x_in, 16)
            pe.wait_ge(cst_in, 32)
            for m in range(KD):
                for n in range(NC):
                    t = turn(part(bank(m), n), x_tok[:, n, P * m:P * m + P])
                t.then_inc(pro_pe, 1)
            pe.wait_ge(pack_in, 16 * 17)
            pe.wait_ge(x_even, 1)
            for n, rows_in in enumerate(PACK_ROWS):
                t = turn(bank(0)[:, P * n:P * n + rows_in], pack[0:rows_in, n, :], rows_in)
            t.then_inc(pro_pe, 1)
            pe.wait_ge(x_odd, 1)
            pe.wait_ge(pro_dve, 5)
            pe.wait_ge(ada_in[1], 16)
            for j in range(4, 8):
                for k in range(KD):
                    nc.tensor.matmul(bank(1)[:, j:j + 1], ada0[:, k, P * j:P * j + P], cact[:, 1, k:k + 1],
                                     start=k == 0, stop=k == KD - 1)
            for turn_n, q in enumerate((0, 2, 3)):
                pe.wait_ge(ada0_own, KD * (turn_n + 1))
                for j in range(4 * q, 4 * q + 4):
                    s = nc.tensor.matmul(bank(1)[:, j:j + 1], ada0_sum[:, P * j:P * j + P], one_col, start=True, stop=True)
                if turn_n == 0:
                    sums(N_MIX)
            s.then_inc(pro_pe, 1)
            norm(N_MIX)
            pe.wait_ge(mod_ready, 1)
            product_group(((AB, 0), (QKVZ, 0)), h_hi, h_lo, (h_ready, split_base(N_MIX)))
            pe.wait_ge(out_used[0], 1)
            for n in range(NC):
                t = turn(bank(2)[:, 2 * H * n:2 * H * n + 2 * H], part(ab_f[0:2 * H], n), 2 * H)
            t.then_inc(ab_pe, 1)
            product(QKVZ, 1, 0, h_hi, h_lo)
            pe.wait_ge(ab_dve, 17)
            nc.tensor.matmul(bank(3)[:, 0:2 * H * NC], cst[:, C_UP:C_UP + P], ab[6][:].rearrange("p n c -> p (n c)"),
                             start=True, stop=True).then_inc(ab_pe, 1)
            pe.sem_inc(g_pe, 1)
            for t in range(2, 4):
                product(QKVZ, t, 0, h_hi, h_lo)

            def head(stage, i, h, fills):
                q_s, k_s, v_s, x_t, y_t, u_t = [gd[n] for n in ("q_s", "k_s", "v_s", "x_t", "y_t", "u_t")]
                filled = [0]

                def fill(name):
                    for _ in range(fills.get(name, 0)):
                        t, q = divmod(filled[0], 4)
                        quarter(stage, t, t, i, q)
                        filled[0] += 1

                def after_dve(name):
                    pe.wait_ge(g_dve, step(DVE_STEPS, name, h))

                def after_act(name):
                    pe.wait_ge(g_act, step(ACT_STEPS, name, h))

                def by_chunk(b, lhs, rhs, turned=False):
                    for n in range(NC):
                        if turned:
                            ins = turn(part(bank(b), n), part(lhs, n))
                        else:
                            ins = nc.tensor.matmul(part(bank(b), n), part(lhs, n), part(rhs, n), start=True, stop=True)
                    return ins

                fill("kv_tokens")
                pe.wait_ge(cv_dve, 10 * h + 9)
                pe.wait_ge(g_dve, heads(DVE_STEPS, h))
                by_chunk(2, k_s, None, True)
                by_chunk(3, v_s, None, True).then_inc(g_pe, 1)
                fill("g_rows")
                after_dve("g_col")
                rows_of(4, S_G).then_inc(g_pe, 1)
                fill("kk_qk")
                by_chunk(5, k_s, k_s)
                by_chunk(6, k_s, q_s).then_inc(g_pe, 1)
                fill("kb_rows")
                after_dve("kb")
                rows_of(7, S_KB).then_inc(g_pe, 1)
                fill("x_pairs")
                after_dve("u0")
                after_act("exp_last")
                by_chunk(4, u_t, None, True).then_inc(g_pe, 1)
                for n in range(LEVELS):
                    fill(f"y{n}")
                    pe.wait_ge(g_pool, step(POOL_STEPS, f"mask{n}", h))
                    if n:
                        after_dve(f"x{n - 1}")
                    else:
                        after_act("x_pairs")
                    by_chunk(4, low_part[n % 2], x_t).then_inc(g_pe, 1)
                    fill(f"x{n}")
                    after_dve(f"y{n}")
                    if n:
                        after_act(f"u{n - 1}")
                    if n < LEVELS - 1:
                        by_chunk(5, u_t, y_t).then_inc(g_pe, 1)
                    fill(f"u{n}")
                    by_chunk(6, y_t, u_t).then_inc(g_pe, 1)
                fill("w")
                after_act(f"u{LEVELS - 1}")
                by_chunk(7, gd["k_beg"], u_t).then_inc(g_pe, 1)
                for n in range(NC):
                    fill(f"v_new{n}")
                    v_new = nc.tensor.matmul(part(bank(2), n), part(u_t, n), part(gd["v_b"], n), start=True, stop=n == 0)
                    if n:
                        after_act("w")
                        after_dve(f"state{n - 1}")
                        v_new = nc.tensor.matmul(part(bank(2), n), part(x_t, n), state[:], start=False, stop=True)
                    v_new.then_inc(g_pe, 1)
                    fill(f"o{n}")
                    after_dve(f"v_new{n}")
                    if n:
                        nc.tensor.matmul(part(bank(3), n), state[:], part(gd["q_g"], n), start=True, stop=False)
                    o = nc.tensor.matmul(part(bank(3), n), part(y_t, n), part(gd["qk_t"], n), start=n == 0, stop=True)
                    if n < NC - 1:
                        o = nc.tensor.matmul(part(bank(4), 0), part(gd["k_dec"], n), part(y_t, n), start=True, stop=True)
                    o.then_inc(g_pe, 1)
                fill("o_sums")
                after_dve("o_sum")
                for n in range(NC):
                    nc.tensor.matmul(bank(5)[:, n:n + 1], part(gd["dec"], n), cst[:, C_MEAN:C_MEAN + 1], start=True, stop=True)
                pe.wait_ge(g_pool, step(POOL_STEPS, "ada", h))
                for j in range(6):
                    s = nc.tensor.matmul(bank(5)[:, 8 + j:9 + j], ada_s[:, j], one_col, start=True, stop=True)
                s.then_inc(g_pe, 1)
                fill("o_norm_rows")
                pe.wait_ge(g_pool, step(POOL_STEPS, "o_norm", h))
                rows_of(6, S_ON).then_inc(g_pe, 1)

            with pe.Fori(0, H - 1) as h:
                head(HEAD, h, h, HEAD_FILL)
            head(LAST, 0, H - 1, LAST_FILL)

            with pe.Fori(0, 2) as i:
                for t in range(4):
                    product(GATE_B, t, i, h_hi, h_lo)
            pe.wait_ge(sc_split, 2)
            pe.wait_ge(g_dve, heads(DVE_STEPS, H))
            with pe.Fori(0, 2) as i:
                for m in range(4):
                    product(GATE, 2 * m, i, sc_hi, sc_lo)
                    product(GATE, 2 * m + 1, i, og_hi, og_lo)
            product_group([(WO, t) for t in range(3)], h_hi, h_lo, (mix_lo, 0), 5)
            for n in range(3, KD):
                product(WO, n % 4, n // 4, h_hi, h_lo)

            def feed_forward(f, r):
                product_group([(UP[f], t) for t in range(3)], h_hi, h_lo, (h_ready, split_base(r)), 5)
                product(UP[f], 3, 0, h_hi, h_lo)
                rest = UP[f].after_first()
                with pe.Fori(0, UPS - 1) as i:
                    for t in range(4):
                        product(rest, t, i, h_hi, h_lo)
                with pe.Fori(0, 2) as i:
                    for m in range(4):
                        b = open_out(DOWN[f].out(m, i))
                        for c in range(3):
                            tile = DOWN[f].tile(3 * m + c, i)
                            pe.wait_ge(lo_ready, tile.before + 1)
                            pe.wait_ge(f_lo, KF * f + min(KD * (c + 1), KF))
                            for k in range(min(KD, KF - KD * c)):
                                n = KD * c + k
                                last = term(bank(b), tile, k, act_hi[:, n], act_lo[:, n], n == 0, n == KF - 1)
                            last.then_inc(tile_done, 1)

            norm(N_FFN)
            feed_forward(0, N_FFN)
            norm(N_OUT1)

            pe.wait_ge(rp_dve, 1)
            nc.tensor.matmul(bank(4), ones[32:33, :], pos_f[32:33, :], start=True, stop=True).then_inc(rp_pe, 1)

            norm(N_POOL)
            for t in range(2):
                tile = POOLW.tile(t, 0)
                pe.wait_ge(lo_ready, tile.before + 1)
                for j in range(4):
                    group, half = divmod(4 * t + j, 2)
                    b = open_out(POOLW.out(4 * t + j, 0))
                    pe.wait_ge(pl_lo, 2 * group + 2)
                    for k in range(2):
                        n = 2 * group + k
                        last = term(bank(b), tile, 4 * (group % 2) + 2 * k + half, p_hi[:, n], p_lo[:, n], k == 0, k == 1)
                    last.then_inc(tile_done if j == 3 else pl_out, 1)
            norm(N_FFN0)
            feed_forward(1, N_FFN0)

            norm(N_ATT)
            product_group(((ATT_Q, 0), (ATT_Q, 1)), h_hi, h_lo, (h_ready, split_base(N_ATT)))
            product(ATT_Q, 2, 0, h_hi, h_lo)
            pe.wait_ge(rp_dve, ROPE_SETUP)
            nc.tensor.matmul(bank(7)[:, 0:1], ones[0:1, :], small[0:1, S_SUM:S_SUM + 1], start=True, stop=True).then_inc(rp_pe, 1)

            pe.sem_inc(t_pe, 1)

            def projection(stage, i, h, ms):
                tile = stage.tile(0, i)
                if ms[0] == 0:
                    pe.wait_ge(lo_ready, tile.before + 1)
                    pe.wait_ge(t_dve, step(ATT_DVE, "lo", h))
                for m in ms:
                    b = open_out(stage.out(m, i))
                    last = term(bank(b), tile, m, at["ao_hi"][:], at["ao_lo"][:], True, True)
                    last.then_inc(wo_out if m < KD - 1 else tile_done, 1)

            def split_product(dst, w, a, rows, cols):
                w_parts, a_parts = [at[w + p][rows, cols] for p in ("_hi", "_lo")], [at[a + p][rows, :] for p in ("_hi", "_lo")]
                nc.tensor.matmul(dst, w_parts[0], a_parts[0], start=True, stop=False)
                nc.tensor.matmul(dst, w_parts[0], a_parts[1], start=False, stop=False)
                return nc.tensor.matmul(dst, w_parts[1], a_parts[0], start=False, stop=True)

            def att_head(stage, i, h, wo, nxt):
                t0, j0 = (1, KD) if wo else (0, 0)

                def fill(t, q):
                    if nxt:
                        quarter(stage, t0 + t, j0 + t, i, q)

                pe.wait_ge(rp_dve, roped(2 * h + 2))
                for q in range(NC):
                    if q >= 2:
                        pe.wait_ge(t_act, step(ATT_ACT, f"exp{q - 2}", h))
                    for c in range(2):
                        s = split_product(bank(2 + 2 * (q % 2) + c), "q", "k", slice(64 * c, 64 * c + 64), slice(P * q, P * q + P))
                    s.then_inc(t_pe, 1)
                    if wo:
                        projection(stage, i, h - 1, (2 * q, 2 * q + 1))
                    if q == 0:
                        open_out(stage.out(0, i))
                        for n in range(NC):
                            t = turn(part(bank(6), n), part(at["v_f"], n))
                        t.then_inc(t_pe, 1)
                for q in range(NC):
                    pe.wait_ge(t_dve, step(ATT_DVE, f"a{q}", h))
                    pe.wait_ge(t_dve, step(ATT_DVE, f"turn_lo{q - 2}" if q >= 2 else "v_lo", h))
                    for n in range(NC):
                        t = turn(part(bank(6 + q % 2), n), part(a_sb[:, q % 2], n))
                    t.then_inc(t_pe, 1)
                    fill(0, q)
                fill(1, 0)
                pe.wait_ge(t_dve, step(ATT_DVE, f"turn_lo{NC - 1}", h))
                for n in range(NC):
                    nc.tensor.matmul(bank(7), part(at["v_hi"], n), at_hi[:, n], start=n == 0, stop=False)
                    nc.tensor.matmul(bank(7), part(at["v_hi"], n), at_lo[:, n], start=False, stop=False)
                    o = nc.tensor.matmul(bank(7), part(at["v_lo"], n), at_hi[:, n], start=False, stop=n == NC - 1)
                o.then_inc(t_pe, 1)
                fill(1, 1)
                fill(1, 2)
                pe.wait_ge(t_act, step(ATT_ACT, "squares", h))
                for n in range(NC):
                    s = nc.tensor.matmul(bank(7)[:, n:n + 1], part(at["o_sq"], n), cst[:, C_MEAN:C_MEAN + 1], start=True, stop=True)
                s.then_inc(t_pe, 1)
                fill(1, 3)
                pe.wait_ge(t_pool, h + 1)
                rows_of(6, S_ON).then_inc(t_pe, 1)
                for q in range(4):
                    fill(2, q)

            att_head(ATT_0, 0, 0, False, True)
            with pe.Fori(0, H - 2) as i:
                att_head(ATT_H, i, i + 1, True, True)
            att_head(ATT_7, 0, H - 1, True, False)
            for q in range(4):
                projection(ATT_WO, 0, H - 1, (2 * q, 2 * q + 1))
            norm(N_FFN1)
            feed_forward(2, N_FFN1)

            norm(N_OUT2)
            for m in range(KD):
                pe.wait_ge(n_ht, scaled_base(N_OUT2) + m + 1)
                if m >= 2:
                    pe.wait_ge(fin_act, m - 1)
                for n in range(NC):
                    t = turn(part(bank(4 + m % 2), n), part(tmp[:, 2 + m % 4], n))
                t.then_inc(fin_pe, 1)


def kernel(**inputs):
    import numpy as _np
    import concourse.bacc as _bacc
    from concourse import mybir as _mybir
    from concourse.bass_utils import run_bass_kernel_spmd as _run

    nc = _bacc.Bacc("TRN2", target_bir_lowering=False, num_devices=1)
    arrays = {name: _np.ascontiguousarray(v) for name, v in inputs.items() if _np.size(v)}
    tile, masks, edges = constants()
    arrays.update(const_tile=tile, const_masks=masks, const_edges=edges)
    aps = {name: nc.dram_tensor(name, v.shape, _mybir.dt.from_np(v.dtype), kind="ExternalInput").ap()
           for name, v in arrays.items()}
    out = nc.dram_tensor("out", (1, T, D), F32, kind="ExternalOutput").ap()
    block_kernel(nc, aps, out)
    r = _run(nc, [arrays], core_ids=[0])
    return r.results[0]["out"]
```
